# Optimizing a Trainium2 kernel written in Bass

```python
import math
import jax
import jax.numpy as jnp
from jax import lax
import numpy as np

D_MODEL = 1024
BATCH = 1
SEQ = 1024
DEPTH = 1

CHUNK = 64
Q_BLOCK = 128
EPS = 1e-6

A_HEADS = 8
A_HEAD_DIM = 64
A_Q_LORA = 256
A_KV_LORA = 256
IDX_HEADS = 8
IDX_DIM = 64
IDX_TOPK_MAX = 256
ATTN_SCALE = A_HEAD_DIM ** -0.5
IDX_SCALE = (IDX_HEADS * IDX_DIM) ** -0.5

B_HEADS = 4
B_HEAD_DIM = 128
B_QK = B_HEADS * B_HEAD_DIM
CONV_WIDTH = 4

REL_BUCKETS = 32
REL_MAX_DIST = 128

MEM_LEN = 256
X_HEADS = 4
X_HEAD_DIM = 128

P_HEADS = 8
N_KEYS = 128
N_EXPERTS = N_KEYS * N_KEYS
P_TOPK = 16
P_QDIM = 256
P_TOKEN_BLOCK = 128

COL_WIDTHS = (A_Q_LORA, A_KV_LORA, IDX_DIM, IDX_HEADS, B_QK, B_QK, B_QK, B_QK, B_HEADS, B_HEADS)
IN_COLS = sum(COL_WIDTHS)
MIX_WIDTH = A_HEADS * A_HEAD_DIM + B_HEADS * B_HEAD_DIM

kernel_name = 'hybrid_dsa_gdn_peer_block'

def rmsnorm(x, g):
    xf = x.astype(jnp.float32)
    y = xf * lax.rsqrt(jnp.mean(xf * xf, axis=-1, keepdims=True) + EPS)
    return (y * g.astype(jnp.float32)).astype(x.dtype)

def l2norm(x):
    return x * lax.rsqrt(jnp.sum(x * x, axis=-1, keepdims=True) + EPS)

def split_columns(p, widths):
    out, start = [], 0
    for w in widths:
        out.append(p[..., start:start + w])
        start += w
    return out

def t5_bucket(rel):
    half = REL_BUCKETS // 2
    max_exact = half // 2
    n = jnp.abs(rel)
    nf = jnp.maximum(n, max_exact).astype(jnp.float32)
    large = max_exact + (jnp.log(nf / max_exact) / math.log(REL_MAX_DIST / max_exact)
                         * (half - max_exact)).astype(jnp.int32)
    large = jnp.minimum(large, half - 1)
    return jnp.where(rel > 0, half, 0) + jnp.where(n < max_exact, n, large)

def dsa_attention(cq, ckv, kidx, widx, g_cq, g_ckv, g_kidx, w_uq, w_iq, w_uk, w_uv, rel_bias):
    bsz, seq, _ = cq.shape
    topk = min(IDX_TOPK_MAX, seq // 4)
    n_blocks = seq // Q_BLOCK
    cq = rmsnorm(cq, g_cq)
    ckv = rmsnorm(ckv, g_ckv)
    kidx = rmsnorm(kidx, g_kidx).astype(jnp.float32)
    key_pos = jnp.arange(seq, dtype=jnp.int32)

    def blockify(a):
        return jnp.moveaxis(a.reshape(bsz, n_blocks, Q_BLOCK, a.shape[-1]), 1, 0)

    def one_block(args):
        cq_b, w_b, start = args
        qpos = start + jnp.arange(Q_BLOCK, dtype=jnp.int32)
        limit = (qpos // CHUNK + 1) * CHUNK
        admissible = key_pos[None, :] < limit[:, None]
        qi = jnp.einsum('bqc,chd->bqhd', cq_b, w_iq).astype(jnp.float32)
        dots = jax.nn.relu(jnp.einsum('bqhd,bsd->bqhs', qi, kidx))
        score = jnp.einsum('bqh,bqhs->bqs', w_b.astype(jnp.float32) * IDX_SCALE, dots)
        score = jnp.where(admissible[None], score, -jnp.inf)
        _, sel = lax.top_k(score, topk)
        valid = sel < limit[None, :, None]
        c_sel = jax.vmap(lambda c, i: c[i])(ckv, sel)
        q = jnp.einsum('bqc,chd->bqhd', cq_b, w_uq)
        q_lat = jnp.einsum('bqhd,chd->bqhc', q, w_uk)
        logits = jnp.einsum('bqhc,bqkc->bhqk', q_lat, c_sel).astype(jnp.float32) * ATTN_SCALE
        bias = rel_bias[t5_bucket(sel - qpos[None, :, None])].astype(jnp.float32)
        logits = logits + jnp.transpose(bias, (0, 3, 1, 2))
        logits = jnp.where(valid[:, None], logits, -jnp.inf)
        p = jax.nn.softmax(logits, axis=-1).astype(c_sel.dtype)
        o_lat = jnp.einsum('bhqk,bqkc->bqhc', p, c_sel)
        o = jnp.einsum('bqhc,chd->bqhd', o_lat, w_uv)
        return o.reshape(bsz, Q_BLOCK, A_HEADS * A_HEAD_DIM)

    starts = jnp.arange(n_blocks, dtype=jnp.int32) * Q_BLOCK
    o = lax.map(one_block, (blockify(cq), blockify(widx), starts))
    return jnp.moveaxis(o, 0, 1).reshape(bsz, seq, A_HEADS * A_HEAD_DIM)

def causal_dwconv(x, w):
    ch = x.shape[-1]
    return lax.conv_general_dilated(x, w[:, None, :].astype(x.dtype), window_strides=(1,),
                                    padding=[(CONV_WIDTH - 1, 0)],
                                    dimension_numbers=('NWC', 'WIO', 'NWC'),
                                    feature_group_count=ch)

def gated_deltanet(q, k, v, z, a, b, conv_w, A_log, dt_bias, g_onorm):
    bsz, seq, _ = q.shape
    f32 = jnp.float32
    H, Dh = B_HEADS, B_HEAD_DIM
    nc = seq // CHUNK
    qkv = jax.nn.silu(causal_dwconv(jnp.concatenate([q, k, v], axis=-1), conv_w)).astype(f32)
    q, k, v = [t.reshape(bsz, seq, H, Dh) for t in jnp.split(qkv, 3, axis=-1)]
    q = l2norm(q) * (Dh ** -0.5)
    k = l2norm(k)
    beta = jax.nn.sigmoid(b.astype(f32))
    g = -jnp.exp(A_log.astype(f32)) * jax.nn.softplus(a.astype(f32) + dt_bias.astype(f32))

    def to_chunks(t):
        t = t.reshape(bsz, nc, CHUNK, *t.shape[2:])
        return jnp.moveaxis(t, 3, 1)

    q, k, v, beta = to_chunks(q), to_chunks(k), to_chunks(v), to_chunks(beta)
    g = jnp.cumsum(to_chunks(g), axis=-1)
    pos = jnp.arange(CHUNK)
    causal = pos[:, None] >= pos[None, :]
    strict = pos[:, None] > pos[None, :]
    decay = jnp.exp(jnp.where(causal, g[..., :, None] - g[..., None, :], -jnp.inf))
    m = jnp.where(strict, beta[..., :, None] * jnp.einsum('bhnid,bhnjd->bhnij', k, k) * decay, 0.0)
    rhs = jnp.concatenate([v * beta[..., None], k * (beta * jnp.exp(g))[..., None]], axis=-1)
    sol = lax.linalg.triangular_solve(m, rhs, left_side=True, lower=True, unit_diagonal=True)
    u, w = sol[..., :Dh], sol[..., Dh:]
    intra = jnp.einsum('bhnid,bhnjd->bhnij', q, k) * decay
    q_dec = q * jnp.exp(g)[..., None]
    k_tail = k * jnp.exp(g[..., -1:] - g)[..., None]
    chunk_decay = jnp.exp(g[..., -1])

    def step(state, inp):
        q_c, u_c, w_c, a_c, kt_c, d_c = inp
        v_new = u_c - jnp.einsum('bhcd,bhde->bhce', w_c, state)
        o_c = jnp.einsum('bhcd,bhde->bhce', q_c, state) + jnp.einsum('bhij,bhje->bhie', a_c, v_new)
        state = state * d_c[..., None, None] + jnp.einsum('bhcd,bhce->bhde', kt_c, v_new)
        return state, o_c

    xs = tuple(jnp.moveaxis(t, 2, 0) for t in (q_dec, u, w, intra, k_tail, chunk_decay))
    _, o = lax.scan(step, jnp.zeros((bsz, H, Dh, Dh), f32), xs)
    o = jnp.transpose(o, (1, 0, 3, 2, 4)).reshape(bsz, seq, H, Dh)
    o = o * lax.rsqrt(jnp.mean(o * o, axis=-1, keepdims=True) + EPS) * g_onorm.astype(f32)
    o = o * jax.nn.silu(z.astype(f32).reshape(bsz, seq, H, Dh))
    return o.reshape(bsz, seq, H * Dh).astype(z.dtype)

def memory_cross_attention(h, mem_n, wq, wk, wv, wo):
    q = jnp.einsum('bsd,dhe->bhse', h, wq)
    k = jnp.einsum('bmd,dhe->bhme', mem_n, wk)
    v = jnp.einsum('bmd,dhe->bhme', mem_n, wv)
    logits = jnp.einsum('bhse,bhme->bhsm', q, k).astype(jnp.float32) * (X_HEAD_DIM ** -0.5)
    p = jax.nn.softmax(logits, axis=-1).astype(v.dtype)
    o = jnp.einsum('bhsm,bhme->bshe', p, v)
    return jnp.einsum('bshe,hed->bsd', o, wo)

def peer_ffn(h, w_pq, sub_keys, u_emb, v_emb):
    bsz, seq, d = h.shape
    n_tok = bsz * seq
    hb = h.reshape(n_tok // P_TOKEN_BLOCK, P_TOKEN_BLOCK, d)

    def one_block(xb):
        n = xb.shape[0]
        qr = jnp.einsum('nd,dhe->nhe', xb, w_pq).reshape(n, P_HEADS, 2, P_QDIM // 2)
        s = jnp.einsum('nhpe,hpke->nhpk', qr, sub_keys).astype(jnp.float32)
        s1, i1 = lax.top_k(s[:, :, 0], P_TOPK)
        s2, i2 = lax.top_k(s[:, :, 1], P_TOPK)
        cand = (s1[..., :, None] + s2[..., None, :]).reshape(n, P_HEADS, P_TOPK * P_TOPK)
        cidx = (i1[..., :, None] * N_KEYS + i2[..., None, :]).reshape(n, P_HEADS, P_TOPK * P_TOPK)
        best, pos = lax.top_k(cand, P_TOPK)
        eidx = jnp.take_along_axis(cidx, pos, axis=-1)
        gate = jax.nn.softmax(best, axis=-1).astype(xb.dtype)
        act = jax.nn.gelu(jnp.einsum('nhkd,nd->nhk', u_emb[eidx], xb), approximate=False)
        return jnp.einsum('nhk,nhkd->nd', gate * act, v_emb[eidx])

    return lax.map(one_block, hb).reshape(bsz, seq, d)

def setup_inputs(seed: int = 0) -> dict:
    key = jax.random.key(seed)
    ks = jax.random.split(key, 32)
    f32 = jnp.float32
    L = DEPTH

    def nrm(k, shape, scale):
        return jax.random.normal(k, shape, f32) * scale

    def gain(k, shape):
        return 1.0 + 0.02 * jax.random.normal(k, shape, f32)

    dt = jnp.exp(jax.random.uniform(ks[14], (L, B_HEADS), f32, math.log(1e-3), math.log(1e-1)))
    return {
        'x': nrm(ks[0], (BATCH, SEQ, D_MODEL), 1.0),
        'mem': nrm(ks[1], (BATCH, MEM_LEN, D_MODEL), 1.0),
        'g_mix': gain(ks[2], (L, D_MODEL)),
        'w_in': nrm(ks[3], (L, D_MODEL, IN_COLS), D_MODEL ** -0.5),
        'g_cq': gain(ks[4], (L, A_Q_LORA)),
        'g_ckv': gain(ks[5], (L, A_KV_LORA)),
        'g_kidx': gain(ks[6], (L, IDX_DIM)),
        'w_uq': nrm(ks[7], (L, A_Q_LORA, A_HEADS, A_HEAD_DIM), A_Q_LORA ** -0.5),
        'w_iq': nrm(ks[8], (L, A_Q_LORA, IDX_HEADS, IDX_DIM), A_Q_LORA ** -0.5),
        'w_uk': nrm(ks[9], (L, A_KV_LORA, A_HEADS, A_HEAD_DIM), A_KV_LORA ** -0.5),
        'w_uv': nrm(ks[10], (L, A_KV_LORA, A_HEADS, A_HEAD_DIM), A_KV_LORA ** -0.5),
        'rel_bias': nrm(ks[11], (REL_BUCKETS, A_HEADS), 0.3),
        'conv_w': nrm(ks[12], (L, CONV_WIDTH, 3 * B_QK), CONV_WIDTH ** -0.5),
        'A_log': jnp.log(jax.random.uniform(ks[13], (L, B_HEADS), f32, 1.0, 16.0)),
        'dt_bias': dt + jnp.log(-jnp.expm1(-dt)),
        'g_onorm': gain(ks[15], (L, B_HEAD_DIM)),
        'w_out': nrm(ks[16], (L, MIX_WIDTH, D_MODEL), MIX_WIDTH ** -0.5),
        'g_cross': gain(ks[17], (L, D_MODEL)),
        'g_mem': gain(ks[18], (L, D_MODEL)),
        'wq_x': nrm(ks[19], (L, D_MODEL, X_HEADS, X_HEAD_DIM), D_MODEL ** -0.5),
        'wk_x': nrm(ks[20], (L, D_MODEL, X_HEADS, X_HEAD_DIM), D_MODEL ** -0.5),
        'wv_x': nrm(ks[21], (L, D_MODEL, X_HEADS, X_HEAD_DIM), D_MODEL ** -0.5),
        'wo_x': nrm(ks[22], (L, X_HEADS, X_HEAD_DIM, D_MODEL), (X_HEADS * X_HEAD_DIM) ** -0.5),
        'g_ffn': gain(ks[23], (L, D_MODEL)),
        'w_pq': nrm(ks[24], (L, D_MODEL, P_HEADS, P_QDIM), D_MODEL ** -0.5),
        'sub_keys': nrm(ks[25], (L, P_HEADS, 2, N_KEYS, P_QDIM // 2), (P_QDIM // 2) ** -0.5),
        'u_emb': nrm(ks[26], (L, N_EXPERTS, D_MODEL), D_MODEL ** -0.5),
        'v_emb': nrm(ks[27], (L, N_EXPERTS, D_MODEL), P_HEADS ** -0.5),
        'g_final': gain(ks[28], (D_MODEL,)),
    }

def reference(x, mem, g_mix, w_in, g_cq, g_ckv, g_kidx, w_uq, w_iq, w_uk, w_uv, rel_bias, conv_w, A_log, dt_bias, g_onorm, w_out, g_cross, g_mem, wq_x, wk_x, wv_x, wo_x, g_ffn, w_pq, sub_keys, u_emb, v_emb, g_final):
    for l in range(DEPTH):
        h = rmsnorm(x, g_mix[l])
        proj = jnp.einsum('bsd,dc->bsc', h, w_in[l])
        cq, ckv, kidx, widx, bq, bk, bv, bz, ba, bb = split_columns(proj, COL_WIDTHS)
        o_a = dsa_attention(cq, ckv, kidx, widx, g_cq[l], g_ckv[l], g_kidx[l],
                            w_uq[l], w_iq[l], w_uk[l], w_uv[l], rel_bias)
        o_b = gated_deltanet(bq, bk, bv, bz, ba, bb, conv_w[l], A_log[l], dt_bias[l], g_onorm[l])
        x = x + jnp.einsum('bsc,cd->bsd', jnp.concatenate([o_a, o_b], axis=-1), w_out[l])
        x = x + memory_cross_attention(rmsnorm(x, g_cross[l]), rmsnorm(mem, g_mem[l]),
                                       wq_x[l], wk_x[l], wv_x[l], wo_x[l])
        x = x + peer_ffn(rmsnorm(x, g_ffn[l]), w_pq[l], sub_keys[l], u_emb[l], v_emb[l])
    return rmsnorm(x, g_final)


_drawn_inputs = setup_inputs


def setup_inputs(seed=0):
    import zlib

    import numpy as np

    out = dict(_drawn_inputs(seed))
    spreads = {}
    factors = {'g_cq': 3.843,
     'g_ckv': 5.797,
     'g_kidx': 3.801,
     'g_onorm': 3.443,
     'g_cross': 7.108,
     'g_mem': 6.226,
     'g_final': 7.498,
     'g_ffn': 8.0,
     'u_emb': 2.686}
    for name, (base, spread) in spreads.items():
        noise = np.random.default_rng([zlib.crc32(name.encode()), seed]).standard_normal(out[name].shape)
        drawn = base * np.exp(spread * noise) if base else spread * noise
        out[name] = jnp.asarray(drawn.astype(out[name].dtype))
    for name, factor in factors.items():
        out[name] = (out[name] * factor).astype(out[name].dtype)
    return out
```

```python
from contextlib import ExitStack, contextmanager
import math

import numpy as np
import concourse.bass as bass
from concourse import mybir

P = 128
D_MODEL, SEQ = 1024, 1024
NT = SEQ // P
DK = D_MODEL // P
CHUNK = 64
EPS = 1e-6
A_HEADS, A_DIM, A_LORA = 8, 64, 256
IDX_HEADS, IDX_DIM, TOPK = 8, 64, 256
B_HEADS, B_DIM = 4, 128
B_QK = B_HEADS * B_DIM
CONV = 4
MEM, X_HEADS, X_DIM = 256, 4, 128
P_HEADS, N_KEYS, P_TOPK = 8, 128, 16
REL_BUCKETS, REL_MAX_DIST = 32, 128
NEAR = 2 * P
NREL = 3 * P
COL_IDX = 2 * A_LORA
COL_QKV = COL_IDX + IDX_DIM + IDX_HEADS
COL_Z = COL_QKV + 3 * B_QK
COL_AB = COL_Z + B_QK
IN_COLS = COL_AB + 2 * B_HEADS
N_IDX = COL_IDX
N_A = N_IDX + IDX_DIM + IDX_HEADS
N_B = N_A + B_HEADS
N_Z = N_B + B_HEADS
N_COLS = N_Z + B_QK
MASKED = -1e30
TAKEN = -3e38
INADMISSIBLE = -2e30

F32 = mybir.dt.float32
U32 = mybir.dt.uint32
ALU = mybir.AluOpType
ACT = mybir.ActivationFunctionType
AX = mybir.AxisListType


@contextmanager
def phase(nc, name, signals):
    sems = {n: nc.alloc_semaphore(f"{name}_{n}") for n in signals.split()}
    yield sems
    nc.clear_and_free_semaphores(list(sems.values()))
    nc.all_engine_barrier()


class Order:

    def __init__(self, eng, sem, base=0):
        self.eng, self.sem, self.base, self.n = eng, sem, base, 0

    def then(self, ins):
        self.n += 1
        ins.then_inc(self.sem, 1)
        self.eng.wait_ge(self.sem, self.base + self.n)


def bcast(ap, axis, n):
    shape = list(ap.shape)
    shape.insert(axis, n)
    return ap.unsqueeze(axis).to_broadcast(shape)


def load_all(nc, name, pairs):
    with phase(nc, name, "loaded") as s, nc.Block() as block:
        @block.sync
        def _(sp):
            for dst, src in pairs:
                sp.dma_start(dst, src).then_inc(s["loaded"], 16)
            sp.wait_ge(s["loaded"], 16 * len(pairs))


def norm_transposed(nc, name, src, dram, gain, ident, outT, tiles):
    with ExitStack() as ctx:
        sb = lambda n, sh: ctx.enter_context(nc.sbuf_tensor(f"{name}_{n}", sh, F32))
        ps = ctx.enter_context(nc.psum_tensor(f"{name}_ps", [P, 4, 512], F32))
        normed = sb("normed", [P, tiles, D_MODEL])
        junk = sb("junk", [P, 2, D_MODEL])
        ssq = sb("ssq", [P, tiles])
        root = sb("root", [P, tiles])
        rinv = sb("rinv", [P, tiles])
        epst = sb("eps", [P, 1])
        per = min(4, tiles)
        groups = tiles // per
        s = ctx.enter_context(phase(nc, name, "eps_ready squared rooted inverted scaled transposed evac_v evac_s " + " ".join(f"src{t}" for t in range(tiles))))
        block = ctx.enter_context(nc.Block())

        @block.sync
        def _(sp):
            if dram is not None:
                for t in range(tiles):
                    sp.dma_start(src[:, t, :], dram[t * P:(t + 1) * P, :]).then_inc(s[f"src{t}"], 16)

        @block.scalar
        def _(act):
            for t in range(tiles):
                if dram is not None:
                    act.wait_ge(s[f"src{t}"], 16)
                if t >= 2:
                    act.wait_ge(s["squared"], t - 1)
                act.activation(junk[:, t % 2, :], src[:, t, :], ACT.Square, accum_out=ssq[:, t:t + 1]).then_inc(s["squared"], 1)
            act.wait_ge(s["squared"], tiles)
            act.wait_ge(s["eps_ready"], 1)
            act.activation(root[:, :], ssq[:, :], ACT.Sqrt, bias=epst[:, :], scale=1.0 / D_MODEL).then_inc(s["rooted"], 1)
            for b in range(1, groups * DK, 2):
                k, g = b // groups, b % groups
                act.wait_ge(s["transposed"], b + 1)
                act.activation(outT[:, k, g * per * P:(g + 1) * per * P], ps[:, b % 4, 0:per * P], ACT.Copy, scale=gain[:, k:k + 1]).then_inc(s["evac_s"], 1)

        @block.vector
        def _(dve):
            dve.memset(epst[:, :], EPS).then_inc(s["eps_ready"], 1)
            dve.wait_ge(s["rooted"], 1)
            dve.reciprocal(rinv[:, :], root[:, :]).then_inc(s["inverted"], 1)
            dve.wait_ge(s["inverted"], 1)
            for t in range(tiles):
                dve.tensor_scalar(normed[:, t, :], src[:, t, :], rinv[:, t:t + 1], None, ALU.mult).then_inc(s["scaled"], 1)
            for b in range(0, groups * DK, 2):
                k, g = b // groups, b % groups
                dve.wait_ge(s["transposed"], b + 1)
                dve.tensor_scalar(outT[:, k, g * per * P:(g + 1) * per * P], ps[:, b % 4, 0:per * P], gain[:, k:k + 1], None, ALU.mult).then_inc(s["evac_v"], 1)

        @block.tensor
        def _(pe):
            for b in range(groups * DK):
                k, g = b // groups, b % groups
                pe.wait_ge(s["scaled"], (g + 1) * per)
                if b >= 4:
                    pe.wait_ge(s["evac_s"] if b % 2 else s["evac_v"], (b - 4) // 2 + 1)
                for j in range(per):
                    last = pe.transpose(ps[:, b % 4, j * P:(j + 1) * P], normed[:, g * per + j, k * P:(k + 1) * P], ident)
                last.then_inc(s["transposed"], 1)


def project(nc, a, hT, nat, proj, ident):
    w_in = a["w_in"].rearrange("(k p) c -> p k c", p=P)
    chunks = 3 * B_QK // P
    with ExitStack() as ctx:
        sb = lambda n, sh: ctx.enter_context(nc.sbuf_tensor(n, sh, F32))
        w1 = sb("w1", [P, DK, 512])
        w2 = sb("w2", [P, DK, 80])
        wc = sb("wc", [P, 2, DK, P])
        raw = sb("raw", [P, 2, CONV - 1 + SEQ])
        conv = sb("conv", [P, 2, SEQ])
        cw = sb("cw", [P, chunks, CONV])
        psn = ctx.enter_context(nc.psum_tensor("psn", [P, 4, 512], F32))
        pst = ctx.enter_context(nc.psum_tensor("pst", [P, 2, 1024], F32))
        s = ctx.enter_context(phase(nc, "project", "cw_loaded wc0 wc1 w1_loaded w2_loaded w3_loaded padded chunk_done raw_ready conv_step conv_done silu_done nat_done nat_evac tok_done tok_evac"))
        block = ctx.enter_context(nc.Block())
        groups = [(w1, "w1_loaded", 16, 0, 512), (w2, "w2_loaded", 32, N_IDX, 80), (w1, "w3_loaded", 16, N_Z, 512)]

        @block.sync
        def _(sp):
            sp.dma_start(cw[:, :, :], a["conv_w"]).then_inc(s["cw_loaded"], 16)
            for c in range(chunks):
                if c >= 2:
                    sp.wait_ge(s["chunk_done"], c - 1)
                sp.dma_start(wc[:, c % 2], w_in[:, :, COL_QKV + c * P:COL_QKV + (c + 1) * P]).then_inc(s[f"wc{c % 2}"], 16)
                if c == 1:
                    sp.dma_start(w1[:, :, :], w_in[:, :, 0:512]).then_inc(s["w1_loaded"], 16)
                    sp.dma_start(w2[:, :, 0:72], w_in[:, :, COL_IDX:COL_QKV]).then_inc(s["w2_loaded"], 16)
                    sp.dma_start(w2[:, :, 72:80], w_in[:, :, COL_AB:IN_COLS]).then_inc(s["w2_loaded"], 16)
            sp.wait_ge(s["tok_done"], NT)
            sp.dma_start(w1[:, :, :], w_in[:, :, COL_Z:COL_AB]).then_inc(s["w3_loaded"], 16)

        @block.tensor
        def _(pe):
            def to_token_major(c):
                pe.wait_ge(s["silu_done"], c + 1)
                if c >= 2:
                    pe.wait_ge(s["nat_evac"], c - 1)
                for t in range(NT):
                    last = pe.transpose(pst[:, c % 2, t * P:(t + 1) * P], conv[:, c % 2, t * P:(t + 1) * P], ident)
                last.then_inc(s["nat_done"], 1)

            for c in range(chunks):
                pe.wait_ge(s[f"wc{c % 2}"], 16 * (c // 2 + 1))
                if c >= 2:
                    pe.wait_ge(s["raw_ready"], c - 1)
                for half in range(2):
                    for k in range(DK):
                        last = pe.matmul(psn[:, 2 * (c % 2) + half, :], lhsT=wc[:, c % 2, k, :], rhs=hT[:, k, half * 512:(half + 1) * 512], start=(k == 0), stop=(k == DK - 1))
                last.then_inc(s["chunk_done"], 1)
                if c >= 1:
                    to_token_major(c - 1)
            to_token_major(chunks - 1)
            pe.wait_ge(s["raw_ready"], chunks)
            n = 0
            for w, loaded, count, col, width in groups:
                pe.wait_ge(s[loaded], count)
                for t in range(NT):
                    if n >= 4:
                        pe.wait_ge(s["tok_evac"], n - 3)
                    for k in range(DK):
                        last = pe.matmul(psn[:, n % 4, 0:width], lhsT=hT[:, k, t * P:(t + 1) * P], rhs=w[:, k, :], start=(k == 0), stop=(k == DK - 1))
                    last.then_inc(s["tok_done"], 1)
                    n += 1

        @block.scalar
        def _(act):
            for c in range(chunks):
                act.wait_ge(s["chunk_done"], c + 1)
                if c == 0:
                    act.wait_ge(s["padded"], 1)
                if c >= 2:
                    act.wait_ge(s["conv_done"], c - 1)
                act.activation(raw[:, c % 2, CONV - 1:], psn[:, 2 * (c % 2):2 * (c % 2) + 2, :].rearrange("p a n -> p (a n)"), ACT.Copy).then_inc(s["raw_ready"], 1)
                act.wait_ge(s["conv_done"], c + 1)
                act.activation(conv[:, c % 2, :], conv[:, c % 2, :], ACT.Silu).then_inc(s["silu_done"], 1)
            n = 0
            for w, loaded, count, col, width in groups:
                for t in range(NT):
                    act.wait_ge(s["tok_done"], n + 1)
                    act.activation(proj[:, t, col:col + width], psn[:, n % 4, 0:width], ACT.Copy).then_inc(s["tok_evac"], 1)
                    n += 1

        @block.vector
        def _(dve):
            order = Order(dve, s["conv_step"])
            dve.memset(raw[:, :, 0:CONV - 1], 0.0).then_inc(s["padded"], 1)
            dve.wait_ge(s["cw_loaded"], 16)

            def evacuate(c):
                dve.wait_ge(s["nat_done"], c + 1)
                dve.tensor_copy(nat[:, :, c * P:(c + 1) * P], pst[:, c % 2, :].rearrange("p (t n) -> p t n", t=NT)).then_inc(s["nat_evac"], 1)

            for c in range(chunks):
                dve.wait_ge(s["raw_ready"], c + 1)
                if c >= 2:
                    dve.wait_ge(s["nat_done"], c - 1)
                out = conv[:, c % 2, :]
                order.then(dve.tensor_scalar(out, raw[:, c % 2, 0:SEQ], cw[:, c, 0:1], None, ALU.mult))
                for i in range(1, CONV):
                    ins = dve.scalar_tensor_tensor(out, raw[:, c % 2, i:i + SEQ], cw[:, c, i:i + 1], out, ALU.mult, ALU.add)
                    if i < CONV - 1:
                        order.then(ins)
                ins.then_inc(s["conv_done"], 1)
                if c >= 1:
                    evacuate(c - 1)
            evacuate(chunks - 1)


def delta_net(nc, a, proj, nat, mix, scratch, consts):
    H, W = B_HEADS, B_HEADS * P
    ident, tri, dmask, strict, lev, levT = (consts[n] for n in ("ident", "tri", "dmask", "strict", "lev", "levT"))
    with ExitStack() as ctx:
        sb = lambda n, sh: ctx.enter_context(nc.sbuf_tensor(n, sh, F32))
        pt = [ctx.enter_context(nc.psum_tensor(f"dn{i}", [P, 512], F32)) for i in range(8)]
        pq, pk, pd, pg, pc, px, pe_, po = pt
        h4 = lambda x: x[:, :].rearrange("p (h n) -> p h n", h=H)
        dtb, alog, gon = sb("dtb", [P, H]), sb("alog", [P, H]), sb("gon", [P, P])
        abs_ = sb("ab_abs", [P, NT, H])
        soft = sb("ab_soft", [P, NT, H])
        gate = sb("ab_gate", [P, NT, H])
        beta = sb("beta", [P, NT, H])
        g4 = sb("g4", [P, 4, NT, H])
        eg = sb("eg", [P, NT, H])
        etail = sb("etail", [P, NT, H])
        dch = sb("dch", [P, 2, NT, H])
        beg = sb("beg", [P, NT, H])
        epst = sb("dn_eps", [P, 1])
        sq = sb("dn_sq", [P, 2 * H, P])
        ssq, root, rinv = sb("dn_ssq", [P, 2 * H]), sb("dn_root", [P, 2 * H]), sb("dn_rinv", [P, 2 * H])
        qk = sb("dn_qk", [P, 2 * H, P])
        qd, vb, kbg, ktail, diag = (sb(f"dn_{n}", [P, H, P]) for n in ("qd", "vb", "kbg", "ktail", "diag"))
        qT, kT, qdT = (sb(f"dn_{n}", [P, H, P]) for n in ("qT", "kT", "qdT"))
        dexp, decay, dstr, m, intra, mT, intraT = (sb(f"dn_{n}", [P, H, P]) for n in ("dexp", "decay", "dstr", "m", "intra", "mT", "intraT"))
        tiles = (scratch[:, i // 2, (i % 2) * W:(i % 2 + 1) * W].rearrange("p (h n) -> p h n", h=H) for i in range(2 * NT))
        x, xT, cT, y, u, wT, vnew, state, o, osq, zs = (next(tiles) for _ in range(11))
        oss, oroot, orinv = sb("dn_oss", [P, H]), sb("dn_oroot", [P, H]), sb("dn_orinv", [P, H])
        s = ctx.enter_context(phase(nc, "delta",
            "rows_loaded dt_added abs_done negexp_done plus_one_done log_done alog_done gate_ready sums_mm sums_ready gate_exps beta_ready "
            "vorder aorder ssq_ready root_ready nat_ready diag_ready transposed qT_ready row_mm kk_mm dexp_ready "
            "decay_ready m_ready mT_mm intraT_ready c_ready y_mm y_ready x_mm x_ready uw_mm wT_ready u_ready "
            "vp_mm vnew_ready o_mm su_mm state_ready oss_ready oroot_ready z_ready block_done"))
        block = ctx.enter_context(nc.Block())
        VSTEPS = 24

        @block.sync
        def _(sp):
            sp.dma_start(dtb[:, :], a["dt_bias"].partition_broadcast(P)).then_inc(s["rows_loaded"], 16)
            sp.dma_start(alog[:, :], a["A_log"].partition_broadcast(P)).then_inc(s["rows_loaded"], 16)
            sp.dma_start(gon[:, :], a["g_onorm"].partition_broadcast(P)).then_inc(s["rows_loaded"], 16)

        @block.scalar
        def _(act):
            act.wait_ge(s["rows_loaded"], 48)
            act.activation(alog[:, :], alog[:, :], ACT.Exp).then_inc(s["alog_done"], 1)
            act.activation(beta[:, :, :], proj[:, :, N_B:N_B + H], ACT.Sigmoid).then_inc(s["beta_ready"], 1)
            act.wait_ge(s["dt_added"], 1)
            act.activation(abs_[:, :, :], gate[:, :, :], ACT.Abs).then_inc(s["abs_done"], 1)
            act.wait_ge(s["abs_done"], 1)
            act.activation(soft[:, :, :], abs_[:, :, :], ACT.Exp, scale=-1.0).then_inc(s["negexp_done"], 1)
            act.wait_ge(s["plus_one_done"], 1)
            act.activation(soft[:, :, :], soft[:, :, :], ACT.Ln).then_inc(s["log_done"], 1)
            act.wait_ge(s["sums_ready"], 2)
            act.activation(eg[:, :, :], g4[:, 0], ACT.Exp)
            act.activation(etail[:, :, :], etail[:, :, :], ACT.Exp)
            act.activation(dch[:, :, :, :], g4[:, 2:4], ACT.Exp).then_inc(s["gate_exps"], 1)
            with act.Fori(0, NT) as t:
                act.wait_ge(s["ssq_ready"], t + 1)
                act.activation(root[:, :], ssq[:, :], ACT.Sqrt, bias=epst[:, :]).then_inc(s["root_ready"], 1)
                act.wait_ge(s["transposed"], t + 1)
                act.activation(qT[:, :, :], h4(pq), ACT.Copy)
                act.activation(kT[:, :, :], h4(pk), ACT.Copy)
                act.activation(qdT[:, :, :], h4(pd), ACT.Copy).then_inc(s["qT_ready"], 1)
                act.wait_ge(s["dexp_ready"], t + 1)
                act.activation(decay[:, :, :], dexp[:, :, :], ACT.Exp).then_inc(s["decay_ready"], 1)
                act.wait_ge(s["mT_mm"], t + 1)
                act.activation(intraT[:, :, :], h4(pk), ACT.Copy).then_inc(s["intraT_ready"], 1)
                for l in range(5):
                    act.wait_ge(s["y_mm"], t * 5 + l + 1)
                    act.activation(y[:, :, :], h4(pd), ACT.Copy).then_inc(s["y_ready"], 1)
                act.wait_ge(s["uw_mm"], t + 1)
                act.activation(wT[:, :, :], h4(px), ACT.Copy).then_inc(s["wT_ready"], 1)
                act.activation(zs[:, :, :], proj[:, bass.ds(t, 1), N_Z:].rearrange("p a (h n) -> p (a h) n", h=H), ACT.Silu).then_inc(s["z_ready"], 1)
                act.wait_ge(s["oss_ready"], t + 1)
                act.activation(oroot[:, :], oss[:, :], ACT.Sqrt, bias=epst[:, :], scale=1.0 / B_DIM).then_inc(s["oroot_ready"], 1)

        @block.tensor
        def _(pe):
            pe.wait_ge(s["gate_ready"], 1)
            for i in range(4):
                last = pe.matmul(pg[:, i * 32:(i + 1) * 32], lhsT=tri[:, i, :], rhs=gate[:, :, :].rearrange("p t h -> p (t h)"), start=True, stop=True)
            last.then_inc(s["sums_mm"], 1)
            with pe.Fori(0, NT) as t:
                pe.wait_ge(s["nat_ready"], t + 1)
                for h in range(H):
                    pe.transpose(h4(pq)[:, h], qk[:, h, :], ident)
                for h in range(H):
                    pe.transpose(h4(pk)[:, h], qk[:, H + h, :], ident)
                for h in range(H):
                    last = pe.transpose(h4(pd)[:, h], qd[:, h, :], ident)
                last.then_inc(s["transposed"], 1)
                pe.wait_ge(s["diag_ready"], t + 1)
                pe.matmul(pg[:, :], lhsT=consts["ones"], rhs=diag[:, :, :].rearrange("p h n -> p (h n)"), start=True, stop=True).then_inc(s["row_mm"], 1)
                pe.wait_ge(s["qT_ready"], t + 1)
                for h in range(H):
                    pe.matmul(h4(pc)[:, h], lhsT=kT[:, h, :], rhs=kT[:, h, :], start=True, stop=True)
                for h in range(H):
                    last = pe.matmul(h4(px)[:, h], lhsT=qT[:, h, :], rhs=kT[:, h, :], start=True, stop=True)
                last.then_inc(s["kk_mm"], 1)
                pe.wait_ge(s["m_ready"], t + 1)
                for h in range(H):
                    pe.transpose(h4(pq)[:, h], m[:, h, :], ident)
                for h in range(H):
                    last = pe.transpose(h4(pk)[:, h], intra[:, h, :], ident)
                last.then_inc(s["mT_mm"], 1)
                for l in range(5):
                    pe.wait_ge(s["c_ready"], t * 5 + l + 1)
                    for h in range(H):
                        last = pe.matmul(h4(pd)[:, h], lhsT=cT[:, h, :], rhs=x[:, h, :], start=True, stop=True)
                    last.then_inc(s["y_mm"], 1)
                    pe.wait_ge(s["y_ready"], t * 5 + l + 1)
                    for h in range(H):
                        pe.matmul(h4(pg)[:, h], lhsT=xT[:, h, :], rhs=y[:, h, :], start=True, stop=True)
                    for h in range(H):
                        last = pe.matmul(h4(pc)[:, h], lhsT=y[:, h, :], rhs=xT[:, h, :], start=True, stop=True)
                    last.then_inc(s["x_mm"], 1)
                pe.wait_ge(s["x_ready"], t * 5 + 5)
                for h in range(H):
                    pe.matmul(h4(pc)[:, h], lhsT=xT[:, h, :], rhs=vb[:, h, :], start=True, stop=True)
                for h in range(H):
                    last = pe.matmul(h4(px)[:, h], lhsT=kbg[:, h, :], rhs=xT[:, h, :], start=True, stop=True)
                last.then_inc(s["uw_mm"], 1)
                pe.wait_ge(s["wT_ready"], t + 1)
                for c in range(2):
                    r = slice(c * CHUNK, (c + 1) * CHUNK)
                    pe.wait_ge(s["state_ready"], 2 * t + c + 1)
                    for h in range(H):
                        last = pe.matmul(h4(pe_)[r, h], lhsT=wT[:, h, r], rhs=state[:, h, :], start=True, stop=True)
                    last.then_inc(s["vp_mm"], 1)
                    pe.wait_ge(s["vnew_ready"], 2 * t + c + 1)
                    for h in range(H):
                        last = pe.matmul(h4(pq)[:, h], lhsT=ktail[r, h, :], rhs=vnew[r, h, :], start=True, stop=True)
                    last.then_inc(s["su_mm"], 1)
                    for h in range(H):
                        pe.matmul(h4(po)[r, h], lhsT=qdT[:, h, r], rhs=state[:, h, :], start=True, stop=False)
                        last = pe.matmul(h4(po)[r, h], lhsT=intraT[r, h, r], rhs=vnew[r, h, :], start=False, stop=True)
                    last.then_inc(s["o_mm"], 1)

        @block.vector
        def _(dve):
            order = Order(dve, s["vorder"])
            ab = proj[:, :, N_A:N_A + H]
            row = lambda r: bcast(r[:, :], 1, NT)
            dve.memset(epst[:, :], EPS)
            order.then(dve.memset(state[:, :, :], 0.0))
            dve.wait_ge(s["rows_loaded"], 48)
            dve.tensor_tensor(gate[:, :, :], ab, row(dtb), ALU.add).then_inc(s["dt_added"], 1)
            dve.wait_ge(s["negexp_done"], 1)
            dve.tensor_scalar(soft[:, :, :], soft[:, :, :], 1.0, None, ALU.add).then_inc(s["plus_one_done"], 1)
            dve.wait_ge(s["log_done"], 1)
            order.then(dve.scalar_tensor_tensor(soft[:, :, :], gate[:, :, :], 0.0, soft[:, :, :], ALU.max, ALU.add))
            dve.wait_ge(s["alog_done"], 1)
            dve.scalar_tensor_tensor(gate[:, :, :], soft[:, :, :], -1.0, row(alog), ALU.mult, ALU.mult).then_inc(s["gate_ready"], 1)
            dve.wait_ge(s["sums_mm"], 1)
            dve.tensor_copy(g4[:, :, :, :].rearrange("p a t h -> p (a t h)"), pg[:, 0:128]).then_inc(s["sums_ready"], 1)
            dve.wait_ge(s["sums_ready"], 1)
            dve.tensor_tensor(etail[:, :, :], g4[:, 1], g4[:, 0], ALU.subtract).then_inc(s["sums_ready"], 1)
            dve.wait_ge(s["gate_exps"], 1)
            dve.wait_ge(s["beta_ready"], 1)
            order.then(dve.tensor_tensor(beg[:, :, :], beta[:, :, :], eg[:, :, :], ALU.mult))
            base = order.n
            dve.sem_inc(s["state_ready"], 1)
            with dve.Fori(0, NT) as t:
                order = Order(dve, s["vorder"], t * VSTEPS + base)
                one = lambda z: z[:, bass.ds(t, 1), :].rearrange("p a h -> p (a h)")
                wide = lambda z: bcast(one(z), 2, P)
                qkt = nat[:, bass.ds(t, 1), 0:2 * W].rearrange("p a (h n) -> p (a h) n", n=P)
                vt = nat[:, bass.ds(t, 1), 2 * W:3 * W].rearrange("p a (h n) -> p (a h) n", n=P)
                order.then(dve.tensor_tensor(sq[:, :, :], qkt, qkt, ALU.mult))
                dve.tensor_reduce(ssq[:, :], sq[:, :, :], AX.X, ALU.add).then_inc(s["ssq_ready"], 1)
                order.then(dve.tensor_tensor(diag[:, :, :], bcast(ident, 1, H), bcast(g4[:, 0, bass.ds(t, 1), :].rearrange("p a h -> p (a h)"), 2, P), ALU.mult))
                dve.sem_inc(s["diag_ready"], 1)
                order.then(dve.tensor_tensor(vb[:, :, :], vt, wide(beta), ALU.mult))
                dve.wait_ge(s["root_ready"], t + 1)
                order.then(dve.reciprocal(rinv[:, :], root[:, :]))
                order.then(dve.tensor_scalar(rinv[:, 0:H], rinv[:, 0:H], B_DIM ** -0.5, None, ALU.mult))
                order.then(dve.tensor_tensor(qk[:, :, :], qkt, bcast(rinv[:, :], 2, P), ALU.mult))
                dve.tensor_tensor(qd[:, :, :], qk[:, 0:H, :], wide(eg), ALU.mult).then_inc(s["nat_ready"], 1)
                dve.tensor_tensor(kbg[:, :, :], qk[:, H:, :], wide(beg), ALU.mult)
                order.then(dve.tensor_tensor(ktail[:, :, :], qk[:, H:, :], wide(etail), ALU.mult))
                dve.wait_ge(s["row_mm"], t + 1)
                order.then(dve.scalar_tensor_tensor(dexp[:, :, :], h4(pg), -1.0, bcast(dmask, 1, H), ALU.mult, ALU.add))
                dve.tensor_tensor(dexp[:, :, :], dexp[:, :, :], bcast(g4[:, 0, bass.ds(t, 1), :].rearrange("p a h -> p (a h)"), 2, P), ALU.add).then_inc(s["dexp_ready"], 1)
                dve.wait_ge(s["decay_ready"], t + 1)
                dve.wait_ge(s["kk_mm"], t + 1)
                order.then(dve.tensor_tensor(intra[:, :, :], h4(px), decay[:, :, :], ALU.mult))
                order.then(dve.tensor_tensor(dstr[:, :, :], decay[:, :, :], bcast(strict, 1, H), ALU.mult))
                order.then(dve.tensor_tensor(dstr[:, :, :], dstr[:, :, :], wide(beta), ALU.mult))
                dve.tensor_tensor(m[:, :, :], h4(pc), dstr[:, :, :], ALU.mult).then_inc(s["m_ready"], 1)
                dve.wait_ge(s["m_ready"], t + 1)
                order.then(dve.tensor_tensor(x[:, :, :], m[:, :, :], bcast(lev, 1, H), ALU.mult))
                order.then(dve.scalar_tensor_tensor(x[:, :, :], x[:, :, :], -1.0, bcast(ident, 1, H), ALU.mult, ALU.add))
                dve.wait_ge(s["mT_mm"], t + 1)
                order.then(dve.tensor_copy(mT[:, :, :], h4(pq)))
                order.then(dve.tensor_tensor(xT[:, :, :], mT[:, :, :], bcast(levT[:, 0, :], 1, H), ALU.mult))
                order.then(dve.scalar_tensor_tensor(xT[:, :, :], xT[:, :, :], -1.0, bcast(ident, 1, H), ALU.mult, ALU.add))
                for l in range(5):
                    dve.tensor_tensor(cT[:, :, :], mT[:, :, :], bcast(levT[:, l + 1, :], 1, H), ALU.mult).then_inc(s["c_ready"], 1)
                    dve.wait_ge(s["x_mm"], t * 5 + l + 1)
                    dve.tensor_tensor(x[:, :, :], x[:, :, :], h4(pg), ALU.subtract)
                    dve.tensor_tensor(xT[:, :, :], xT[:, :, :], h4(pc), ALU.subtract).then_inc(s["x_ready"], 1)
                    dve.wait_ge(s["x_ready"], t * 5 + l + 1)
                dve.wait_ge(s["uw_mm"], t + 1)
                order.then(dve.tensor_copy(u[:, :, :], h4(pc)))
                for c in range(2):
                    r = slice(c * CHUNK, (c + 1) * CHUNK)
                    dve.wait_ge(s["vp_mm"], 2 * t + c + 1)
                    dve.tensor_tensor(vnew[r, :, :], u[r, :, :], h4(pe_)[r], ALU.subtract).then_inc(s["vnew_ready"], 1)
                    dve.wait_ge(s["o_mm"], 2 * t + c + 1)
                    order.then(dve.tensor_tensor(state[:, :, :], state[:, :, :], bcast(dch[:, c, bass.ds(t, 1), :].rearrange("p a h -> p (a h)"), 2, P), ALU.mult))
                    dve.tensor_tensor(state[:, :, :], state[:, :, :], h4(pq), ALU.add).then_inc(s["state_ready"], 1)
                    dve.wait_ge(s["state_ready"], 2 * t + c + 2)
                order.then(dve.tensor_copy(o[:, :, :], h4(po)))
                order.then(dve.tensor_tensor(osq[:, :, :], o[:, :, :], o[:, :, :], ALU.mult))
                dve.tensor_reduce(oss[:, :], osq[:, :, :], AX.X, ALU.add).then_inc(s["oss_ready"], 1)
                order.then(dve.tensor_tensor(o[:, :, :], o[:, :, :], bcast(gon[:, :], 1, H), ALU.mult))
                dve.wait_ge(s["z_ready"], t + 1)
                order.then(dve.tensor_tensor(o[:, :, :], o[:, :, :], zs[:, :, :], ALU.mult))
                dve.wait_ge(s["oroot_ready"], t + 1)
                order.then(dve.reciprocal(orinv[:, :], oroot[:, :]))
                dve.tensor_tensor(mix[:, bass.ds(t, 1), W:2 * W].rearrange("p a (h n) -> p (a h) n", n=P), o[:, :, :], bcast(orinv[:, :], 2, P), ALU.mult).then_inc(s["block_done"], 1)
                assert order.n == VSTEPS


def shape_constants():
    i = np.arange(P)
    same = (i[:, None] // CHUNK) == (i[None, :] // CHUNK)
    j_le_i = i[:, None] <= i[None, :]
    even = np.repeat((i < CHUNK)[:, None], P, 1)
    tri = np.stack([same & j_le_i, same, even, ~even], 1)
    lower = same & (i[:, None] >= i[None, :])
    lev = [(i[:, None] // (2 * b) == i[None, :] // (2 * b)) & (i[:, None] // b % 2 == 1) & (i[None, :] // b % 2 == 0) for b in (1, 2, 4, 8, 16, 32)]
    rel = np.arange(NREL) - (NEAR - 1)
    half, exact = REL_BUCKETS // 2, REL_BUCKETS // 4
    n = np.abs(rel)
    large = exact + (np.log(np.maximum(n, exact).astype(np.float32) / np.float32(exact)) / np.float32(math.log(REL_MAX_DIST / exact)) * np.float32(half - exact)).astype(np.int32)
    bucket = np.where(rel > 0, half, 0) + np.where(n < exact, n, np.minimum(large, half - 1))
    b = np.arange(REL_BUCKETS)[:, None]
    relhot = (b == bucket[None, :]).astype(np.float32) - (b == half - 1).astype(np.float32)
    f = lambda z: np.ascontiguousarray(z).astype(np.float32)
    return {
        "ident": f(np.eye(P)), "flip": f(np.eye(P)[::-1]), "ones": f(np.ones((P, P))), "tri": f(tri),
        "dmask": f(np.where(lower, 0, MASKED)), "strict": f(lower & (i[:, None] > i[None, :])),
        "lev": f(lev[0]), "levT": f(np.stack([z.T for z in lev], 1)),
        "relhot": f(relhot), "iota": f(np.broadcast_to(i[None, :], (P, P))),
    }


def sparse_prepare(nc, a, proj, gains, consts, idxT, qiT, qT, kT, v, widx, near):
    with ExitStack() as ctx:
        sb = lambda n, sh: ctx.enter_context(nc.sbuf_tensor(n, sh, F32))
        w = {n: sb(f"sp_{n}", [P, 2, 512]) for n in ("w_iq", "w_uq", "w_uk", "w_uv")}
        latT = sb("sp_latT", [P, 4, SEQ])
        keys = sb("sp_keys", [P, NT, 2, IDX_DIM])
        junk = sb("sp_junk", [P, 2, 256])
        ssq, root, rinv, epst = sb("sp_ssq", [P, 3, NT]), sb("sp_root", [P, 3, NT]), sb("sp_rinv", [P, 3, NT]), sb("sp_eps", [P, 1])
        relb, rowb = sb("sp_relb", [REL_BUCKETS, A_HEADS]), sb("sp_rowb", [A_HEADS, NREL])
        shifted = sb("sp_shifted", [P, A_HEADS, NEAR])
        pt = [ctx.enter_context(nc.psum_tensor(f"sp{i}", [P, 512], F32)) for i in range(8)]
        s = ctx.enter_context(phase(nc, "sparse_prep", "w_iq w_uq w_uk w_uv relb_loaded bias_mm bias_ready bias_stored near_loaded eps_ready squared rooted vorder normed transposed lat_ready proj_mm evac"))
        block = ctx.enter_context(nc.Block())
        banks = [(j, half) for j in range(5) for half in range(2)]
        heads = [("w_iq", 0, qiT, 1.0, m, half) for m in range(4) for half in range(2)] + \
                [("w_uq", 0, qT, A_DIM ** -0.5, m, half) for m in range(4) for half in range(2)] + \
                [("w_uk", 2, kT, 1.0, m, half) for m in range(4) for half in range(2)]

        @block.sync
        def _(sp):
            sp.dma_start(relb[:, :], a["rel_bias"]).then_inc(s["relb_loaded"], 16)
            for n in w:
                sp.dma_start(w[n][:, :, :], a[n].rearrange("(k p) c -> p k c", p=P)).then_inc(s[n], 16)
            sp.wait_ge(s["bias_ready"], 1)
            sp.dma_start(a["bias_rows"], rowb[:, :]).then_inc(s["bias_stored"], 16)
            sp.wait_ge(s["bias_stored"], 16)
            sp.dma_start(shifted[:, :, :], bass.AP(a["bias_rows"].tensor, 0, [[1, P], [NREL, A_HEADS], [1, NEAR]])).then_inc(s["near_loaded"], 16)

        @block.scalar
        def _(act):
            n = 0
            for g, (col, width) in enumerate(((0, A_LORA), (A_LORA, A_LORA), (N_IDX, IDX_DIM))):
                for t in range(NT):
                    if n >= 2:
                        act.wait_ge(s["squared"], n - 1)
                    act.activation(junk[:, n % 2, 0:width], proj[:, t, col:col + width], ACT.Square, accum_out=ssq[:, g, t:t + 1]).then_inc(s["squared"], 1)
                    n += 1
            act.wait_ge(s["squared"], n)
            act.wait_ge(s["eps_ready"], 1)
            act.activation(root[:, 0:2], ssq[:, 0:2], ACT.Sqrt, bias=epst[:, :], scale=1.0 / A_LORA).then_inc(s["rooted"], 1)
            act.activation(root[:, 2], ssq[:, 2], ACT.Sqrt, bias=epst[:, :], scale=1.0 / IDX_DIM).then_inc(s["rooted"], 1)
            for i, (j, half) in enumerate(banks):
                act.wait_ge(s["transposed"], i + 1)
                out = latT[:, j] if j < 4 else idxT
                act.activation(out[:, half * 512:(half + 1) * 512], pt[i % 8][:, :], ACT.Copy, scale=gains[:, j:j + 1]).then_inc(s["lat_ready"], 1)

        @block.tensor
        def _(pe):
            pe.wait_ge(s["relb_loaded"], 16)
            pe.matmul(pt[7][0:A_HEADS, 0:NREL], lhsT=relb[:, :], rhs=consts["relhot"], start=True, stop=True).then_inc(s["bias_mm"], 1)
            pe.wait_ge(s["normed"], 3)
            pe.wait_ge(s["bias_ready"], 1)
            for i, (j, half) in enumerate(banks):
                if i >= 8:
                    pe.wait_ge(s["lat_ready"], i - 7)
                for b in range(4):
                    t = half * 4 + b
                    src = proj[:, t, j * P:(j + 1) * P] if j < 4 else keys[:, t].rearrange("p a d -> p (a d)")
                    last = pe.transpose(pt[i % 8][:, b * P:(b + 1) * P], src, consts["ident"])
                last.then_inc(s["transposed"], 1)
            pe.wait_ge(s["lat_ready"], len(banks))
            for i, (name, src, dst, scale, m, half) in enumerate(heads):
                pe.wait_ge(s[name], 16)
                if i >= 8:
                    pe.wait_ge(s["evac"], i - 7)
                for k in range(2):
                    last = pe.matmul(pt[i % 8][:, :], lhsT=w[name][:, k, m * P:(m + 1) * P], rhs=latT[:, src + k, half * 512:(half + 1) * 512], start=(k == 0), stop=(k == 1))
                last.then_inc(s["proj_mm"], 1)
            pe.wait_ge(s["w_uv"], 16)
            for t in range(NT):
                i = len(heads) + t
                pe.wait_ge(s["evac"], i - 7)
                for k in range(2):
                    last = pe.matmul(pt[i % 8][:, :], lhsT=latT[:, 2 + k, t * P:(t + 1) * P], rhs=w["w_uv"][:, k, :], start=(k == 0), stop=(k == 1))
                last.then_inc(s["proj_mm"], 1)
            pe.wait_ge(s["near_loaded"], 16)
            for j in range(4):
                i = len(heads) + NT + j
                pe.wait_ge(s["evac"], i - 7)
                pe.matmul(pt[i % 8][:, :], lhsT=consts["flip"], rhs=shifted[:, 2 * j:2 * j + 2, :].rearrange("p h c -> p (h c)"), start=True, stop=True).then_inc(s["proj_mm"], 1)

        @block.vector
        def _(dve):
            order = Order(dve, s["vorder"])
            dve.memset(epst[:, :], EPS).then_inc(s["eps_ready"], 1)
            dve.wait_ge(s["bias_mm"], 1)
            dve.tensor_copy(rowb[:, :], pt[7][0:A_HEADS, 0:NREL]).then_inc(s["bias_ready"], 1)
            dve.tensor_scalar(widx, proj[:, :, N_IDX + IDX_DIM:N_A], (IDX_HEADS * IDX_DIM) ** -0.5, None, ALU.mult)
            dve.wait_ge(s["rooted"], 2)
            order.then(dve.reciprocal(rinv[:, :, :], root[:, :, :]))
            for g in range(2):
                dve.tensor_tensor(proj[:, :, g * A_LORA:(g + 1) * A_LORA], proj[:, :, g * A_LORA:(g + 1) * A_LORA], bcast(rinv[:, g], 2, A_LORA), ALU.mult).then_inc(s["normed"], 1)
            for twice in range(2):
                last = dve.tensor_tensor(keys[:, :, twice, :], proj[:, :, N_IDX:N_IDX + IDX_DIM], bcast(rinv[:, 2], 2, IDX_DIM), ALU.mult)
            last.then_inc(s["normed"], 1)
            for i, (name, src, dst, scale, m, half) in enumerate(heads):
                dve.wait_ge(s["proj_mm"], i + 1)
                dve.tensor_scalar(dst[:, m, half * 512:(half + 1) * 512], pt[i % 8][:, :], scale, None, ALU.mult).then_inc(s["evac"], 1)
            for t in range(NT):
                i = len(heads) + t
                dve.wait_ge(s["proj_mm"], i + 1)
                dve.tensor_copy(v[:, t, :], pt[i % 8][:, :]).then_inc(s["evac"], 1)
            for j in range(4):
                i = len(heads) + NT + j
                dve.wait_ge(s["proj_mm"], i + 1)
                dve.tensor_copy(near[:, 2 * j:2 * j + 2, :].rearrange("p h c -> p (h c)"), pt[i % 8][:, :]).then_inc(s["evac"], 1)


def sparse_attention(nc, idxT, qiT, qT, kT, v, widx, near, mix, ident):
    H = A_HEADS
    with ExitStack() as ctx:
        sb = lambda n, sh: ctx.enter_context(nc.sbuf_tensor(n, sh, F32))
        score, mask, relu = sb("sa_score", [P, SEQ]), sb("sa_mask", [P, SEQ]), sb("sa_relu", [P, 2, SEQ])
        top8 = sb("sa_top8", [P, 8])
        logit = sb("sa_logit", [P, 2, SEQ])
        probT = sb("sa_probT", [P, 2, NT, P])
        nmax, rsum, rinv = sb("sa_nmax", [P, 2, H]), sb("sa_rsum", [P, 2, H]), sb("sa_rinv", [P, H])
        psS = ctx.enter_context(nc.psum_tensor("sa_ps", [P, 2, 1024], F32))
        psT = ctx.enter_context(nc.psum_tensor("sa_psT", [P, 1024], F32))
        psO = ctx.enter_context(nc.psum_tensor("sa_psO", [P, 2, 512], F32))
        s = ctx.enter_context(phase(nc, "sparse", "dots_mm relu_done relu_used vorder logit_done max_ready exp_done prob_mm prob_ready out_mm out_done"))
        block = ctx.enter_context(nc.Block())
        SPARSE0 = TOPK // P
        uses, relus, logits = [], 0, 0
        for b in range(NT):
            if b >= SPARSE0:
                for h in range(H):
                    uses.append((b, "index", h, relus))
                    relus += 1
            for h in range(H):
                uses.append((b, "head", h, logits))
                logits += 1

        @block.tensor
        def _(pe):
            def transpose_probs(n):
                b, h = divmod(n, H)
                pe.wait_ge(s["exp_done"], n + 1)
                if n >= 1:
                    pe.wait_ge(s["prob_ready"], n)
                for j in range(b + 1):
                    last = pe.transpose(psT[:, j * P:(j + 1) * P], logit[:, n % 2, j * P:(j + 1) * P], ident)
                last.then_inc(s["prob_mm"], 1)

            def weigh_values(n):
                b, h = divmod(n, H)
                pe.wait_ge(s["prob_ready"], n + 1)
                if h == 0 and b >= 2:
                    pe.wait_ge(s["out_done"], b - 1)
                for j in range(b + 1):
                    last = pe.matmul(psO[:, b % 2, h * A_DIM:(h + 1) * A_DIM], lhsT=probT[:, n % 2, j, :], rhs=v[:, j, h * A_DIM:(h + 1) * A_DIM], start=(j == 0), stop=(j == b))
                last.then_inc(s["out_mm"], 1)

            for u, (b, kind, h, n) in enumerate(uses):
                W = (b + 1) * P
                if u >= 2:
                    _, before, _, m = uses[u - 2]
                    pe.wait_ge(s["relu_done" if before == "index" else "logit_done"], m + 1)
                r = slice((h % 2) * A_DIM, (h % 2 + 1) * A_DIM)
                query, key = (qiT, idxT) if kind == "index" else (qT, kT[:, h // 2])
                for c in range(0, W, 512):
                    e = min(W, c + 512)
                    last = pe.matmul(psS[:, u % 2, c:e], lhsT=query[r, h // 2, b * P:(b + 1) * P], rhs=key[r, c:e], start=True, stop=True)
                last.then_inc(s["dots_mm"], 1)
                if kind == "head":
                    if n >= 1:
                        transpose_probs(n - 1)
                    if n >= 2:
                        weigh_values(n - 2)
            transpose_probs(logits - 1)
            weigh_values(logits - 2)
            weigh_values(logits - 1)

        @block.scalar
        def _(act):
            def probs_out(n):
                b = n // H
                act.wait_ge(s["prob_mm"], n + 1)
                if n >= 2:
                    act.wait_ge(s["out_mm"], n - 1)
                act.activation(probT[:, n % 2, 0:b + 1, :].rearrange("p j q -> p (j q)"), psT[:, 0:(b + 1) * P], ACT.Copy).then_inc(s["prob_ready"], 1)

            for u, (b, kind, h, n) in enumerate(uses):
                W = (b + 1) * P
                if kind == "index":
                    act.wait_ge(s["dots_mm"], u + 1)
                    if n >= 2:
                        act.wait_ge(s["relu_used"], n - 1)
                    act.activation(relu[:, n % 2, 0:W], psS[:, u % 2, 0:W], ACT.Relu).then_inc(s["relu_done"], 1)
                else:
                    act.wait_ge(s["max_ready"], n + 1)
                    act.activation(logit[:, n % 2, 0:W], logit[:, n % 2, 0:W], ACT.Exp, bias=nmax[:, b % 2, h:h + 1], accum_out=rsum[:, b % 2, h:h + 1]).then_inc(s["exp_done"], 1)
                    if n >= 1:
                        probs_out(n - 1)
            probs_out(logits - 1)

        @block.vector
        def _(dve):
            order = Order(dve, s["vorder"])

            def outputs(b):
                dve.wait_ge(s["out_mm"], H * (b + 1))
                order.then(dve.reciprocal(rinv[:, :], rsum[:, b % 2, :]))
                dve.tensor_tensor(mix[:, b, 0:H * A_DIM].rearrange("p (h d) -> p h d", h=H), psO[:, b % 2, :].rearrange("p (h d) -> p h d", h=H), bcast(rinv[:, :], 2, A_DIM), ALU.mult).then_inc(s["out_done"], 1)

            for u, (b, kind, h, n) in enumerate(uses):
                W = (b + 1) * P
                if kind == "index":
                    dve.wait_ge(s["relu_done"], n + 1)
                    if h == 0:
                        ins = dve.tensor_scalar(score[:, 0:W], relu[:, n % 2, 0:W], widx[:, b, h:h + 1], None, ALU.mult)
                    else:
                        ins = dve.scalar_tensor_tensor(score[:, 0:W], relu[:, n % 2, 0:W], widx[:, b, h:h + 1], score[:, 0:W], ALU.mult, ALU.add)
                    ins.then_inc(s["relu_used"], 1)
                    dve.wait_ge(s["relu_used"], n + 1)
                    continue
                if h == 0:
                    if b >= SPARSE0:
                        order.then(dve.memset(score[0:CHUNK, W - CHUNK:W], INADMISSIBLE))
                        for _ in range(TOPK // 8):
                            order.then(dve.max(top8[:, :], score[:, 0:W]))
                            order.then(dve.match_replace(score[:, 0:W], top8[:, :], score[:, 0:W], TAKEN))
                        order.then(dve.tensor_scalar(mask[:, 0:W], score[:, 0:W], -1e38, MASKED, ALU.is_gt, ALU.mult))
                    else:
                        order.then(dve.memset(mask[:, 0:W], 0.0))
                        order.then(dve.memset(mask[0:CHUNK, W - CHUNK:W], MASKED))
                if h == 3 and b >= 1:
                    outputs(b - 1)
                dve.wait_ge(s["dots_mm"], u + 1)
                if n >= 2:
                    dve.wait_ge(s["prob_mm"], n - 1)
                dve.tensor_tensor(logit[:, n % 2, 0:W], psS[:, u % 2, 0:W], mask[:, 0:W], ALU.add).then_inc(s["logit_done"], 1)
                dve.wait_ge(s["logit_done"], n + 1)
                lo = max(0, W - NEAR)
                tail = logit[:, n % 2, lo:W]
                order.then(dve.tensor_tensor(tail, tail, near[:, h, NEAR - (W - lo):NEAR], ALU.add))
                dve.tensor_reduce(nmax[:, b % 2, h:h + 1], logit[:, n % 2, 0:W], AX.X, ALU.max, negate=True).then_inc(s["max_ready"], 1)
            outputs(NT - 1)


def mix_out(nc, a, mix, x, ident):
    with ExitStack() as ctx:
        sb = lambda n, sh: ctx.enter_context(nc.sbuf_tensor(n, sh, F32))
        w = sb("mo_w", [P, DK, D_MODEL])
        mixT = sb("mo_mixT", [P, DK, SEQ])
        pst = ctx.enter_context(nc.psum_tensor("mo_t", [P, 4, 512], F32))
        psy = ctx.enter_context(nc.psum_tensor("mo_y", [P, 4, 512], F32))
        s = ctx.enter_context(phase(nc, "mix_out", "w_loaded x_loaded transposed mixT_ready y_mm y_added"))
        block = ctx.enter_context(nc.Block())

        @block.sync
        def _(sp):
            sp.dma_start(w[:, :, :], a["w_out"].rearrange("(k p) c -> p k c", p=P)).then_inc(s["w_loaded"], 16)
            sp.dma_start(x[:, :, :], a["x"].rearrange("(t p) c -> p t c", p=P)).then_inc(s["x_loaded"], 16)

        @block.tensor
        def _(pe):
            for b in range(2 * DK):
                half, k = divmod(b, DK)
                if b >= 4:
                    pe.wait_ge(s["mixT_ready"], b - 3)
                for j in range(4):
                    last = pe.transpose(pst[:, b % 4, j * P:(j + 1) * P], mix[:, half * 4 + j, k * P:(k + 1) * P], ident)
                last.then_inc(s["transposed"], 1)
            pe.wait_ge(s["w_loaded"], 16)
            for n in range(2 * NT):
                t, half = divmod(n, 2)
                pe.wait_ge(s["mixT_ready"], DK if t < 4 else 2 * DK)
                if n >= 4:
                    pe.wait_ge(s["y_added"], n - 3)
                for k in range(DK):
                    last = pe.matmul(psy[:, n % 4, :], lhsT=mixT[:, k, t * P:(t + 1) * P], rhs=w[:, k, half * 512:(half + 1) * 512], start=(k == 0), stop=(k == DK - 1))
                last.then_inc(s["y_mm"], 1)

        @block.scalar
        def _(act):
            for b in range(2 * DK):
                half, k = divmod(b, DK)
                act.wait_ge(s["transposed"], b + 1)
                act.activation(mixT[:, k, half * 512:(half + 1) * 512], pst[:, b % 4, :], ACT.Copy).then_inc(s["mixT_ready"], 1)

        @block.vector
        def _(dve):
            dve.wait_ge(s["x_loaded"], 16)
            for n in range(2 * NT):
                t, half = divmod(n, 2)
                xr = x[:, t, half * 512:(half + 1) * 512]
                dve.wait_ge(s["y_mm"], n + 1)
                dve.tensor_tensor(xr, xr, psy[:, n % 4, :], ALU.add).then_inc(s["y_added"], 1)


def cross_project(nc, a, hT, memT, qT, kT, v):
    with ExitStack() as ctx:
        w = {n: ctx.enter_context(nc.sbuf_tensor(f"cp_{n}", [P, DK, 512], F32)) for n in ("wk_x", "wv_x", "wq_x")}
        ps = ctx.enter_context(nc.psum_tensor("cp_ps", [P, 4, 512], F32))
        s = ctx.enter_context(phase(nc, "cross_proj", "wk_x wv_x wq_x proj_mm evac"))
        block = ctx.enter_context(nc.Block())
        jobs = [("wk_x", lambda k, h=h: w["wk_x"][:, k, h * P:(h + 1) * P], lambda k: memT[:, k, :], kT[:, h, :], MEM) for h in range(X_HEADS)]
        jobs += [("wv_x", lambda k, m=m: memT[:, k, m * P:(m + 1) * P], lambda k: w["wv_x"][:, k, :], v[:, m, :], 512) for m in range(MEM // P)]
        jobs += [("wq_x", lambda k, h=h: w["wq_x"][:, k, h * P:(h + 1) * P], lambda k, g=g: hT[:, k, g * 512:(g + 1) * 512], qT[:, h, g * 512:(g + 1) * 512], 512)
                 for h in range(X_HEADS) for g in range(2)]

        @block.sync
        def _(sp):
            for n in w:
                sp.dma_start(w[n][:, :, :], a[n].rearrange("(k p) c -> p k c", p=P)).then_inc(s[n], 16)

        @block.tensor
        def _(pe):
            for i, (name, lhsT, rhs, out, width) in enumerate(jobs):
                pe.wait_ge(s[name], 16)
                if i >= 4:
                    pe.wait_ge(s["evac"], i - 3)
                for k in range(DK):
                    last = pe.matmul(ps[:, i % 4, 0:width], lhsT=lhsT(k), rhs=rhs(k), start=(k == 0), stop=(k == DK - 1))
                last.then_inc(s["proj_mm"], 1)

        @block.vector
        def _(dve):
            for i, (name, lhsT, rhs, out, width) in enumerate(jobs):
                dve.wait_ge(s["proj_mm"], i + 1)
                dve.tensor_copy(out, ps[:, i % 4, 0:width]).then_inc(s["evac"], 1)


def cross_attend(nc, a, qT, kT, v, x, ident):
    H, SCALE = X_HEADS, X_DIM ** -0.5
    with ExitStack() as ctx:
        sb = lambda n, sh: ctx.enter_context(nc.sbuf_tensor(n, sh, F32))
        wo = sb("ca_wo", [P, H, D_MODEL])
        prob = sb("ca_prob", [P, 2, H, MEM])
        probT = sb("ca_probT", [P, H, 2, P])
        oT = sb("ca_oT", [P, H, P])
        nmax, rsum, rinv = sb("ca_nmax", [P, H]), sb("ca_rsum", [P, H]), sb("ca_rinv", [P, H])
        psL = ctx.enter_context(nc.psum_tensor("ca_l", [P, H, MEM], F32))
        psT = ctx.enter_context(nc.psum_tensor("ca_t", [P, H, 2, P], F32))
        psO = ctx.enter_context(nc.psum_tensor("ca_o", [P, H, P], F32))
        psY = ctx.enter_context(nc.psum_tensor("ca_y", [P, 2, 512], F32))
        s = ctx.enter_context(phase(nc, "cross", "wo_loaded logit_mm vorder max_ready exp_done prob_ready probT_mm probT_ready o_mm oT_ready y_mm y_added"))
        block = ctx.enter_context(nc.Block())

        @block.sync
        def _(sp):
            sp.dma_start(wo[:, :, :], a["wo_x"].rearrange("(h p) c -> p h c", p=P)).then_inc(s["wo_loaded"], 16)

        @block.tensor
        def _(pe):
            def logits(t):
                if t >= 1:
                    pe.wait_ge(s["exp_done"], t)
                for h in range(H):
                    last = pe.matmul(psL[:, h, :], lhsT=qT[:, h, t * P:(t + 1) * P], rhs=kT[:, h, :], start=True, stop=True)
                last.then_inc(s["logit_mm"], 1)

            logits(0)
            pe.wait_ge(s["wo_loaded"], 16)
            for t in range(NT):
                if t + 1 < NT:
                    logits(t + 1)
                pe.wait_ge(s["prob_ready"], t + 1)
                for h in range(H):
                    for m in range(2):
                        last = pe.transpose(psT[:, h, m, :], prob[:, t % 2, h, m * P:(m + 1) * P], ident)
                last.then_inc(s["probT_mm"], 1)
                pe.wait_ge(s["probT_ready"], t + 1)
                for h in range(H):
                    for m in range(2):
                        last = pe.matmul(psO[:, h, :], lhsT=v[:, m, h * P:(h + 1) * P], rhs=probT[:, h, m, :], start=(m == 0), stop=(m == 1))
                last.then_inc(s["o_mm"], 1)
                pe.wait_ge(s["oT_ready"], t + 1)
                if t >= 1:
                    pe.wait_ge(s["y_added"], t)
                for half in range(2):
                    for h in range(H):
                        last = pe.matmul(psY[:, half, :], lhsT=oT[:, h, :], rhs=wo[:, h, half * 512:(half + 1) * 512], start=(h == 0), stop=(h == H - 1))
                last.then_inc(s["y_mm"], 1)

        @block.scalar
        def _(act):
            for t in range(NT):
                act.wait_ge(s["max_ready"], t + 1)
                if t >= 2:
                    act.wait_ge(s["probT_mm"], t - 1)
                for h in range(H):
                    last = act.activation(prob[:, t % 2, h, :], psL[:, h, :], ACT.Exp, bias=nmax[:, h:h + 1], scale=SCALE, accum_out=rsum[:, h:h + 1])
                last.then_inc(s["exp_done"], 1)
                act.wait_ge(s["probT_mm"], t + 1)
                act.activation(probT[:, :, :, :], psT[:, :, :, :], ACT.Copy).then_inc(s["probT_ready"], 1)
                act.wait_ge(s["o_mm"], t + 1)
                act.activation(oT[:, :, :], psO[:, :, :], ACT.Copy).then_inc(s["oT_ready"], 1)

        @block.vector
        def _(dve):
            order = Order(dve, s["vorder"])
            for t in range(NT):
                dve.wait_ge(s["logit_mm"], t + 1)
                order.then(dve.tensor_reduce(nmax[:, :], psL[:, :, :], AX.X, ALU.max))
                dve.tensor_scalar(nmax[:, :], nmax[:, :], -SCALE, None, ALU.mult).then_inc(s["max_ready"], 1)
                dve.wait_ge(s["exp_done"], t + 1)
                order.then(dve.reciprocal(rinv[:, :], rsum[:, :]))
                dve.tensor_tensor(prob[:, t % 2], prob[:, t % 2], bcast(rinv[:, :], 2, MEM), ALU.mult).then_inc(s["prob_ready"], 1)
                dve.wait_ge(s["y_mm"], t + 1)
                dve.tensor_tensor(x[:, t, :], x[:, t, :], psY[:, :, :].rearrange("p a n -> p (a n)"), ALU.add).then_inc(s["y_added"], 1)


def route_scores(nc, a, hT, top, topi):
    NS = 2 * P_HEADS
    with ExitStack() as ctx:
        sb = lambda n, sh: ctx.enter_context(nc.sbuf_tensor(n, sh, F32))
        w, keys = sb("rs_w", [P, 2, DK, P]), sb("rs_keys", [P, NS, N_KEYS])
        qT, sc = sb("rs_qT", [P, 2, SEQ]), sb("rs_sc", [P, 2, NT, N_KEYS])
        psq = ctx.enter_context(nc.psum_tensor("rs_q", [P, 2, 1024], F32))
        pss = ctx.enter_context(nc.psum_tensor("rs_s", [P, 2, 1024], F32))
        s = ctx.enter_context(phase(nc, "route", "keys_loaded w0 w1 kept q_mm q_ready s_mm s_ready vorder picked"))
        block = ctx.enter_context(nc.Block())
        w_pq = a["w_pq"].rearrange("(k p) c -> p k c", p=P)

        @block.sync
        def _(sp):
            for i in range(NS):
                if i >= 2:
                    sp.wait_ge(s["q_mm"], i - 1)
                sp.dma_start(w[:, i % 2], w_pq[:, :, i * P:(i + 1) * P]).then_inc(s[f"w{i % 2}"], 16)
                if i == 1:
                    sp.dma_start(keys[:, :, :], a["sub_keys"]).then_inc(s["keys_loaded"], 16)
                    sp.dma_start(a["h_kept"], hT[:, :, :]).then_inc(s["kept"], 16)
            sp.wait_ge(s["kept"], 16)

        @block.tensor
        def _(pe):
            def scores(i):
                pe.wait_ge(s["q_ready"], i + 1)
                if i >= 2:
                    pe.wait_ge(s["s_ready"], i - 1)
                for t in range(NT):
                    last = pe.matmul(pss[:, i % 2, t * P:(t + 1) * P], lhsT=qT[:, i % 2, t * P:(t + 1) * P], rhs=keys[:, i, :], start=True, stop=True)
                last.then_inc(s["s_mm"], 1)

            for i in range(NS):
                pe.wait_ge(s[f"w{i % 2}"], 16 * (i // 2 + 1))
                if i >= 2:
                    pe.wait_ge(s["q_ready"], i - 1)
                for half in range(2):
                    for k in range(DK):
                        last = pe.matmul(psq[:, i % 2, half * 512:(half + 1) * 512], lhsT=w[:, i % 2, k, :], rhs=hT[:, k, half * 512:(half + 1) * 512], start=(k == 0), stop=(k == DK - 1))
                last.then_inc(s["q_mm"], 1)
                if i == 0:
                    pe.wait_ge(s["keys_loaded"], 16)
                else:
                    scores(i - 1)
            scores(NS - 1)

        @block.scalar
        def _(act):
            def scores_out(i):
                act.wait_ge(s["s_mm"], i + 1)
                if i >= 2:
                    act.wait_ge(s["picked"], i - 1)
                act.activation(sc[:, i % 2].rearrange("p t k -> p (t k)"), pss[:, i % 2, :], ACT.Copy).then_inc(s["s_ready"], 1)

            for i in range(NS):
                act.wait_ge(s["q_mm"], i + 1)
                if i >= 2:
                    act.wait_ge(s["s_mm"], i - 1)
                act.activation(qT[:, i % 2, :], psq[:, i % 2, :], ACT.Copy).then_inc(s["q_ready"], 1)
                if i >= 1:
                    scores_out(i - 1)
            scores_out(NS - 1)

        @block.vector
        def _(dve):
            order = Order(dve, s["vorder"])
            for i in range(NS):
                dve.wait_ge(s["s_ready"], i + 1)
                for r in range(2):
                    part = slice(8 * r, 8 * r + 8)
                    for t in range(NT):
                        last = dve.max(top[:, t, i, part], sc[:, i % 2, t, :])
                    order.then(last)
                    for t in range(NT):
                        last = dve.max_index(topi[:, t, i, part], top[:, t, i, part], sc[:, i % 2, t, :])
                    if r == 0:
                        for t in range(NT):
                            last = dve.match_replace(sc[:, i % 2, t, :], top[:, t, i, part], sc[:, i % 2, t, :], TAKEN)
                        order.then(last)
                last.then_inc(s["picked"], 1)


def route_combine(nc, top, topi, routeT, consts):
    H, K = P_HEADS, P_TOPK
    ident, iota = consts["ident"], consts["iota"]
    with ExitStack() as ctx:
        sb = lambda n, sh, dt=F32: ctx.enter_context(nc.sbuf_tensor(n, sh, dt))
        keyf = sb("rc_keyf", [P, NT, 2 * H, K])
        cand, hot = sb("rc_cand", [P, H, K * K]), sb("rc_hot", [P, 2, H * K, K])
        best, pos = sb("rc_best", [P, H, K]), sb("rc_pos", [P, H * K], U32)
        digit, digitf = sb("rc_digit", [P, 2, H * K], U32), sb("rc_digitf", [P, 2, H * K])
        sel = sb("rc_sel", [P, 2, 3, H * K])
        gsum, ginv = sb("rc_gsum", [P, H]), sb("rc_ginv", [P, H])
        ps = ctx.enter_context(nc.psum_tensor("rc_ps", [P, 2, 512], F32))
        s = ctx.enter_context(phase(nc, "combine", "vorder shifted exp_done sel_ready transposed route_ready"))
        block = ctx.enter_context(nc.Block())

        @block.vector
        def _(dve):
            order = Order(dve, s["vorder"])
            order.then(dve.tensor_copy(keyf[:, :, :, :], topi))
            for t in range(NT):
                pair = lambda z, half: z[:, t, half::2, :]
                c4 = cand[:, :, :].rearrange("p h (i j) -> p h i j", i=K)
                order.then(dve.tensor_tensor(c4, bcast(pair(top, 0), 3, K), bcast(pair(top, 1), 2, K), ALU.add))
                for r in range(2):
                    part = slice(8 * r, 8 * r + 8)
                    for h in range(H):
                        last = dve.max(best[:, h, part], cand[:, h, :])
                    order.then(last)
                    for h in range(H):
                        last = dve.max_index(pos[:, h * K + 8 * r:h * K + 8 * r + 8], best[:, h, part], cand[:, h, :])
                    if r == 0:
                        for h in range(H):
                            last = dve.match_replace(cand[:, h, :], best[:, h, part], cand[:, h, :], TAKEN)
                    order.then(last)
                if t >= 2:
                    dve.wait_ge(s["transposed"], t - 1)
                gate = sel[:, t % 2, 2, :].rearrange("p (h k) -> p h k", h=H)
                dve.tensor_tensor(gate, best[:, :, :], bcast(best[:, :, 0], 2, K), ALU.subtract).then_inc(s["shifted"], 1)
                dve.tensor_scalar(digit[:, 0, :], pos[:, :], 4, None, ALU.logical_shift_right)
                order.then(dve.tensor_scalar(digit[:, 1, :], pos[:, :], K - 1, None, ALU.bitwise_and))
                order.then(dve.tensor_copy(digitf[:, :, :], digit[:, :, :]))
                for half in range(2):
                    last = dve.tensor_tensor(hot[:, half], bcast(digitf[:, half, :], 2, K), bcast(iota[:, 0:K], 1, H * K), ALU.is_equal)
                order.then(last)
                for half in range(2):
                    h4 = hot[:, half].rearrange("p (h k) j -> p h k j", h=H)
                    last = dve.tensor_tensor(h4, h4, bcast(pair(keyf, half), 2, K), ALU.mult)
                order.then(last)
                for half in range(2):
                    dve.tensor_reduce(sel[:, t % 2, half, :], hot[:, half], AX.X, ALU.add)
                dve.wait_ge(s["exp_done"], t + 1)
                order.then(dve.tensor_reduce(gsum[:, :], gate, AX.X, ALU.add))
                order.then(dve.reciprocal(ginv[:, :], gsum[:, :]))
                dve.tensor_tensor(gate, gate, bcast(ginv[:, :], 2, K), ALU.mult).then_inc(s["sel_ready"], 1)

        @block.scalar
        def _(act):
            for t in range(NT):
                act.wait_ge(s["shifted"], t + 1)
                act.activation(sel[:, t % 2, 2, :], sel[:, t % 2, 2, :], ACT.Exp).then_inc(s["exp_done"], 1)
                if t >= 1:
                    act.wait_ge(s["transposed"], t)
                    act.activation(routeT[:, :, (t - 1) * P:t * P], ps[:, (t - 1) % 2, 0:3 * P].rearrange("p (a n) -> p a n", a=3), ACT.Copy).then_inc(s["route_ready"], 1)
            act.wait_ge(s["transposed"], NT)
            act.activation(routeT[:, :, (NT - 1) * P:], ps[:, (NT - 1) % 2, 0:3 * P].rearrange("p (a n) -> p a n", a=3), ACT.Copy).then_inc(s["route_ready"], 1)

        @block.tensor
        def _(pe):
            for t in range(NT):
                pe.wait_ge(s["sel_ready"], t + 1)
                if t >= 2:
                    pe.wait_ge(s["route_ready"], t - 1)
                for i in range(3):
                    last = pe.transpose(ps[:, t % 2, i * P:(i + 1) * P], sel[:, t % 2, i, :], ident)
                last.then_inc(s["transposed"], 1)


def build_gates(nc, a, routeT, iota):
    T, SLOTS = 4, 4
    GROUPS = P // T
    with ExitStack() as ctx:
        sb = lambda n, sh: ctx.enter_context(nc.sbuf_tensor(n, sh, F32))
        hot1, hot2 = sb("bg_hot1", [P, 2, T, P]), sb("bg_hot2", [P, 2, T, P])
        gates = sb("bg_gates", [P, 2, N_KEYS, P])
        ps = ctx.enter_context(nc.psum_tensor("bg_ps", [P, SLOTS, T, P], F32))
        s = ctx.enter_context(phase(nc, "gates", "hot_ready gate_mm evac stored0 stored1"))
        block = ctx.enter_context(nc.Block())
        U = 4

        @block.vector
        def _(dve):
            dve.sem_inc(s["gate_mm"], 2)
            with dve.Fori(0, NT * GROUPS // U) as i:
                for u in range(U):
                    dve.wait_ge(s["gate_mm"], i * U + u + 1)
                    for j in range(T):
                        n = (i * U + u) * T + j
                        at = lambda c: routeT[:, c, bass.ds(n, 1)]
                        dve.tensor_scalar(hot1[:, u % 2, j, :], iota, at(0), at(2), ALU.is_equal, ALU.mult)
                        last = dve.tensor_scalar(hot2[:, u % 2, j, :], iota, at(1), None, ALU.is_equal)
                    last.then_inc(s["hot_ready"], 1)

        @block.tensor
        def _(pe):
            pe.sem_inc(s["evac"], SLOTS)
            with pe.Fori(0, NT * GROUPS // U) as i:
                for u in range(U):
                    pe.wait_ge(s["hot_ready"], i * U + u + 1)
                    pe.wait_ge(s["evac"], i * U + u + 1)
                    for j in range(T):
                        last = pe.matmul(ps[:, u % SLOTS, j, :], lhsT=hot2[:, u % 2, j, :], rhs=hot1[:, u % 2, j, :], start=True, stop=True)
                    last.then_inc(s["gate_mm"], 1)

        @block.scalar
        def _(act):
            for p in range(2):
                act.sem_inc(s[f"stored{p}"], 16)
            with act.Fori(0, NT // 2) as i:
                for p in range(2):
                    act.wait_ge(s[f"stored{p}"], i * 16 + 16)
                    with act.Fori(0, GROUPS // U) as g:
                        for u in range(U):
                            n = (i * 2 + p) * GROUPS + g * U + u
                            act.wait_ge(s["gate_mm"], n + 3)
                            act.activation(gates[:, p, :, bass.ds((g * U + u) * T, T)], ps[:, u % SLOTS, :, :].rearrange("j n i -> j i n"), ACT.Copy).then_inc(s["evac"], 1)

        @block.sync
        def _(sp):
            with sp.Fori(0, NT // 2) as i:
                for p in range(2):
                    sp.wait_ge(s["evac"], (i * 2 + p + 1) * GROUPS + SLOTS)
                    sp.dma_start(a["gates"][:, :, bass.ds((i * 2 + p) * P, P)].rearrange("i j n -> j i n"), gates[:, p]).then_inc(s[f"stored{p}"], 16)
            for p in range(2):
                sp.wait_ge(s[f"stored{p}"], 16 * (NT // 2 + 1))


def experts(nc, a, hT, x):
    G = 4
    NG = N_KEYS // G
    with ExitStack() as ctx:
        sb = lambda n, sh: ctx.enter_context(nc.sbuf_tensor(n, sh, F32))
        u_sb = sb("ex_u", [P, 2, DK, P])
        v_sb = sb("ex_v", [P, 2, G, D_MODEL])
        g_sb = sb("ex_g", [P, 2, SEQ])
        act_sb = sb("ex_act", [P, 2, SEQ])
        wgt = sb("ex_wgt", [P, 2, G, SEQ])
        psA = ctx.enter_context(nc.psum_tensor("ex_a", [P, 2, 1024], F32))
        psY = ctx.enter_context(nc.psum_tensor("ex_y", [P, 4, 512], F32))
        s = ctx.enter_context(phase(nc, "experts", "h_loaded u0 u1 g0 g1 v0 v1 act_mm gelu_done wgt_ready y_mm y_added"))
        block = ctx.enter_context(nc.Block())
        NY = 4

        @block.sync
        def _(sp):
            sp.dma_start(hT[:, :, :], a["h_kept"]).then_inc(s["h_loaded"], 16)

            def load(g, p, peeled=None):
                for c in range(G):
                    n = g * G + c
                    b = c % 2
                    if not (peeled == 0 and c < 2):
                        sp.wait_ge(s["act_mm"], n - 1)
                    sp.dma_start(u_sb[:, b], a["u_emb"][bass.ds(n, 1)].rearrange("a p k e -> p (a k) e")).then_inc(s[f"u{b}"], 16)
                    if not (peeled == 0 and c < 2):
                        sp.wait_ge(s["wgt_ready"], n - 1)
                    sp.dma_start(g_sb[:, b], a["gates"][bass.ds(n, 1)].rearrange("a j n -> j (a n)")).then_inc(s[f"g{b}"], 16)
                    if c == 1:
                        if peeled is None:
                            sp.wait_ge(s["y_mm"], (g - 1) * 16)
                        sp.dma_start(v_sb[:, p], a["v_emb"][bass.ds(g, 1)].rearrange("a c e d -> e (a c) d")).then_inc(s[f"v{p}"], 16)

            load(0, 0, 0)
            load(1, 1, 1)
            with sp.Fori(1, NG // 2) as i:
                for p in range(2):
                    load(i * 2 + p, p)

        def first(pe, g, c, peeled=None):
            n = g * G + c
            b = c % 2
            pe.wait_ge(s[f"u{b}"], (n - b) // 2 * 16 + 16 if isinstance(n, int) else (g * 2 + c // 2) * 16 + 16)
            if not (peeled == 0 and c < 2):
                pe.wait_ge(s["gelu_done"], n - 1)
            for half in range(2):
                for k in range(DK):
                    last = pe.matmul(psA[:, b, half * 512:(half + 1) * 512], lhsT=u_sb[:, b, k, :], rhs=hT[:, k, half * 512:(half + 1) * 512], start=(k == 0), stop=(k == DK - 1))
            last.then_inc(s["act_mm"], 1)

        def second(pe, g, p, q, parity_count, peeled=None):
            if q == 0:
                pe.wait_ge(s[f"v{p}"], parity_count * 16 + 16)
                pe.wait_ge(s["wgt_ready"], g * G + G)
            for y in range(4):
                t, half = 2 * q + y // 2, y % 2
                if not (peeled == 0 and q == 0):
                    pe.wait_ge(s["y_added"], g * 16 + q * 4 + y - 3)
                for c in range(G):
                    last = pe.matmul(psY[:, y, :], lhsT=wgt[:, p, c, t * P:(t + 1) * P], rhs=v_sb[:, p, c, half * 512:(half + 1) * 512], start=(c == 0), stop=(c == G - 1))
                last.then_inc(s["y_mm"], 1)

        @block.tensor
        def _(pe):
            pe.wait_ge(s["h_loaded"], 16)
            for c in range(G):
                first(pe, 0, c, 0)
            for c in range(G):
                first(pe, 1, c)
                second(pe, 0, 0, c, 0, 0)
            with pe.Fori(1, NG // 2) as i:
                for p in range(2):
                    for c in range(G):
                        first(pe, i * 2 + p, c)
                        second(pe, i * 2 + p - 1, 1 - p, c, i - 1 + p)
            for c in range(G):
                second(pe, NG - 1, 1, c, NG // 2 - 1)

        @block.scalar
        def _(act):
            def gelu(g, c, peeled=None):
                n = g * G + c
                act.wait_ge(s["act_mm"], n + 1)
                if not (peeled == 0 and c < 2):
                    act.wait_ge(s["wgt_ready"], n - 1)
                act.activation(act_sb[:, c % 2, :], psA[:, c % 2, :], ACT.Gelu).then_inc(s["gelu_done"], 1)

            for g in range(2):
                for c in range(G):
                    gelu(g, c, g)
            with act.Fori(1, NG // 2) as i:
                for p in range(2):
                    for c in range(G):
                        gelu(i * 2 + p, c)

        @block.vector
        def _(dve):
            def weigh(g, p, c, peeled=None):
                n = g * G + c
                b = c % 2
                dve.wait_ge(s["gelu_done"], n + 1)
                dve.wait_ge(s[f"g{b}"], (g * 2 + c // 2) * 16 + 16)
                if c == 0 and peeled is None:
                    dve.wait_ge(s["y_mm"], (g - 1) * 16)
                dve.tensor_tensor(wgt[:, p, c, :], act_sb[:, b, :], g_sb[:, b, :], ALU.mult).then_inc(s["wgt_ready"], 1)

            def add(g, q):
                for y in range(4):
                    t, half = 2 * q + y // 2, y % 2
                    xr = x[:, t, half * 512:(half + 1) * 512]
                    dve.wait_ge(s["y_mm"], g * 16 + q * 4 + y + 1)
                    dve.tensor_tensor(xr, xr, psY[:, y, :], ALU.add).then_inc(s["y_added"], 1)

            for c in range(G):
                weigh(0, 0, c, 0)
            for c in range(G):
                weigh(1, 1, c, 1)
                add(0, c)
            with dve.Fori(1, NG // 2) as i:
                for p in range(2):
                    for c in range(G):
                        weigh(i * 2 + p, p, c)
                        add(i * 2 + p - 1, c)
            for c in range(G):
                add(NG - 1, c)


def final_norm(nc, a, x, out):
    with ExitStack() as ctx:
        sb = lambda n, sh: ctx.enter_context(nc.sbuf_tensor(n, sh, F32))
        gain, junk, y = sb("fn_gain", [P, D_MODEL]), sb("fn_junk", [P, 2, D_MODEL]), sb("fn_y", [P, NT, D_MODEL])
        ssq, root, rinv, epst = sb("fn_ssq", [P, NT]), sb("fn_root", [P, NT]), sb("fn_rinv", [P, NT]), sb("fn_eps", [P, 1])
        s = ctx.enter_context(phase(nc, "final", "gain_loaded eps_ready squared rooted inverted y_ready stored"))
        block = ctx.enter_context(nc.Block())

        @block.sync
        def _(sp):
            sp.dma_start(gain[:, :], a["g_final"].partition_broadcast(P)).then_inc(s["gain_loaded"], 16)
            for t in range(NT):
                sp.wait_ge(s["y_ready"], t + 1)
                sp.dma_start(out[t * P:(t + 1) * P, :], y[:, t, :]).then_inc(s["stored"], 16)
            sp.wait_ge(s["stored"], 16 * NT)

        @block.scalar
        def _(act):
            for t in range(NT):
                if t >= 2:
                    act.wait_ge(s["squared"], t - 1)
                act.activation(junk[:, t % 2, :], x[:, t, :], ACT.Square, accum_out=ssq[:, t:t + 1]).then_inc(s["squared"], 1)
            act.wait_ge(s["squared"], NT)
            act.wait_ge(s["eps_ready"], 1)
            act.activation(root[:, :], ssq[:, :], ACT.Sqrt, bias=epst[:, :], scale=1.0 / D_MODEL).then_inc(s["rooted"], 1)

        @block.vector
        def _(dve):
            dve.memset(epst[:, :], EPS).then_inc(s["eps_ready"], 1)
            dve.wait_ge(s["gain_loaded"], 16)
            dve.wait_ge(s["rooted"], 1)
            dve.reciprocal(rinv[:, :], root[:, :]).then_inc(s["inverted"], 1)
            dve.wait_ge(s["inverted"], 1)
            for t in range(NT):
                dve.scalar_tensor_tensor(y[:, t, :], x[:, t, :], rinv[:, t:t + 1], gain[:, :], ALU.mult, ALU.mult).then_inc(s["y_ready"], 1)


CONSTANTS = ("ident", "flip", "ones", "relhot", "iota")
DELTA_CONSTANTS = ("tri", "dmask", "strict", "lev", "levT")
GAINS = {"g_mix": DK, "g_cross": DK, "g_mem": DK, "g_ffn": DK, "g_lat": 5}


def hybrid_block(nc, a, out, probe=None):
    probe = probe or (lambda *args: None)
    whole = lambda t: t[tuple(slice(None) for _ in t.shape)]
    with ExitStack() as ctx:
        def sb(stack, name, shape, dt=F32):
            return stack.enter_context(nc.sbuf_tensor(name, shape, dt))

        small = {n: sb(ctx, f"c_{n}", list(a[f"c_{n}"].shape)) for n in CONSTANTS}
        small |= {n: sb(ctx, f"s_{n}", [P, w]) for n, w in GAINS.items()}
        load_all(nc, "constants", [(whole(t), a[f"c_{n}" if n in CONSTANTS else n]) for n, t in small.items()])
        consts = {n: whole(t) for n, t in small.items()}
        ident = consts["ident"]
        stream = sb(ctx, "stream", [P, NT, D_MODEL])
        wide = sb(ctx, "wide", [P, DK, SEQ])
        gain = lambda n: small[n]

        norm_transposed(nc, "norm_mix", wide, a["x"], gain("g_mix"), ident, stream, NT)
        with ExitStack() as mixer:
            proj = sb(mixer, "proj", [P, NT, N_COLS])
            with ExitStack() as sub:
                nat = sb(sub, "nat", [P, NT, 3 * B_QK])
                project(nc, a, stream, nat, proj, ident)
                delta = {n: sb(sub, f"c_{n}", list(a[f"c_{n}"].shape)) for n in DELTA_CONSTANTS}
                load_all(nc, "delta_constants", [(whole(t), a[f"c_{n}"]) for n, t in delta.items()])
                delta_net(nc, a, proj, nat, wide, stream, consts | {n: whole(t) for n, t in delta.items()})
            idxT, qiT = sb(mixer, "idxT", [P, SEQ]), sb(mixer, "qiT", [P, 4, SEQ])
            v, widx, near = sb(mixer, "v", [P, NT, 512]), sb(mixer, "widx", [P, NT, IDX_HEADS]), sb(mixer, "near", [P, A_HEADS, NEAR])
            qT, kT = stream[:, 0:4, :], stream[:, 4:8, :]
            sparse_prepare(nc, a, proj, small["g_lat"], consts, idxT[:, :], qiT, qT, kT, v, widx[:, :, :], near[:, :, :])
            sparse_attention(nc, idxT[:, :], qiT, qT, kT, v, widx, near, wide, ident)
        probe("mix", wide)
        mix_out(nc, a, wide, stream, ident)
        probe("x1", stream)

        with ExitStack() as cross:
            memT = sb(cross, "memT", [P, DK, MEM])
            xqT, xkT, xv = sb(cross, "xqT", [P, X_HEADS, SEQ]), sb(cross, "xkT", [P, X_HEADS, MEM]), sb(cross, "xv", [P, MEM // P, 512])
            norm_transposed(nc, "norm_cross", stream, None, gain("g_cross"), ident, wide, NT)
            with nc.sbuf_tensor("mem_in", [P, MEM // P, D_MODEL], F32) as mem_in:
                norm_transposed(nc, "norm_mem", mem_in, a["mem"], gain("g_mem"), ident, memT, MEM // P)
            cross_project(nc, a, wide, memT, xqT, xkT, xv)
            cross_attend(nc, a, xqT, xkT, xv, stream, ident)
        probe("x2", stream)

        norm_transposed(nc, "norm_ffn", stream, None, gain("g_ffn"), ident, wide, NT)
        with ExitStack() as route:
            top = sb(route, "top", [P, NT, 2 * P_HEADS, P_TOPK])
            topi = sb(route, "topi", [P, NT, 2 * P_HEADS, P_TOPK], U32)
            route_scores(nc, a, wide, top, topi)
            routeT = wide[:, 0:3, :]
            route_combine(nc, top, topi[:, :, :, :], routeT, consts)
        probe("routeT", wide)
        build_gates(nc, a, routeT, consts["iota"])
        experts(nc, a, wide, stream)
        final_norm(nc, a, stream, out)


def kernel(**inputs):
    import concourse.bacc as bacc
    from concourse.bass_utils import run_bass_kernel_spmd

    g = {n: np.asarray(v) for n, v in inputs.items()}
    column = lambda v: v.reshape(-1, P).T
    arrays = {
        "x": g["x"][0], "mem": g["mem"][0], "w_in": g["w_in"][0],
        "g_mix": column(g["g_mix"][0]), "g_cross": column(g["g_cross"][0]), "g_mem": column(g["g_mem"][0]), "g_ffn": column(g["g_ffn"][0]),
        "g_lat": np.stack([*g["g_cq"][0].reshape(2, P), *g["g_ckv"][0].reshape(2, P), np.tile(g["g_kidx"][0], 2)], 1),
        "w_uq": g["w_uq"][0].reshape(A_LORA, 512), "w_iq": g["w_iq"][0].reshape(A_LORA, 512),
        "w_uk": g["w_uk"][0].reshape(A_LORA, 512), "w_uv": g["w_uv"][0].reshape(A_LORA, 512),
        "rel_bias": g["rel_bias"],
        "conv_w": g["conv_w"][0].reshape(CONV, 3 * B_QK // P, P).transpose(2, 1, 0),
        "A_log": g["A_log"][0], "dt_bias": g["dt_bias"][0], "g_onorm": g["g_onorm"][0], "w_out": g["w_out"][0],
        "wq_x": g["wq_x"][0].reshape(D_MODEL, 512), "wk_x": g["wk_x"][0].reshape(D_MODEL, 512), "wv_x": g["wv_x"][0].reshape(D_MODEL, 512),
        "wo_x": g["wo_x"][0].reshape(512, D_MODEL),
        "w_pq": g["w_pq"][0].reshape(D_MODEL, 2 * P_HEADS * P),
        "sub_keys": g["sub_keys"][0].reshape(2 * P_HEADS, N_KEYS, P).transpose(2, 0, 1),
        "u_emb": g["u_emb"][0].reshape(N_KEYS, P, DK, P).transpose(0, 3, 2, 1),
        "v_emb": g["v_emb"][0].reshape(N_KEYS // 4, 4, P, D_MODEL),
        "g_final": g["g_final"],
    } | {f"c_{n}": v for n, v in shape_constants().items()}
    arrays = {n: np.ascontiguousarray(v) for n, v in arrays.items()}

    nc = bacc.Bacc("TRN2", target_bir_lowering=False, num_devices=1)
    a = {n: nc.dram_tensor(f"in_{n}", v.shape, F32, kind="ExternalInput").ap() for n, v in arrays.items()}
    a["bias_rows"] = nc.dram_tensor("bias_rows", (A_HEADS, NREL), F32).ap()
    a["h_kept"] = nc.dram_tensor("h_kept", (P, DK, SEQ), F32).ap()
    a["gates"] = nc.dram_tensor("gates", (N_KEYS, P, SEQ), F32).ap()
    out = nc.dram_tensor("out_x", (SEQ, D_MODEL), F32, kind="ExternalOutput").ap()
    hybrid_block(nc, a, out)
    r = run_bass_kernel_spmd(nc, [{f"in_{n}": v for n, v in arrays.items()}], core_ids=[0])
    return r.results[0]["out_x"].reshape(1, SEQ, D_MODEL)
```

```python
from contextlib import ExitStack, contextmanager
import math

import numpy as np
import concourse.bass as bass
from concourse import mybir

P = 128
D_MODEL, SEQ = 1024, 1024
NT = SEQ // P
DK = D_MODEL // P
CHUNK = 64
EPS = 1e-6
A_HEADS, A_DIM, A_LORA = 8, 64, 256
IDX_HEADS, IDX_DIM, TOPK = 8, 64, 256
B_HEADS, B_DIM = 4, 128
B_QK = B_HEADS * B_DIM
CONV = 4
MEM, X_HEADS, X_DIM = 256, 4, 128
P_HEADS, N_KEYS, P_TOPK = 8, 128, 16
REL_BUCKETS, REL_MAX_DIST = 32, 128
NEAR = 2 * P
NREL = 3 * P
COL_IDX = 2 * A_LORA
COL_QKV = COL_IDX + IDX_DIM + IDX_HEADS
COL_Z = COL_QKV + 3 * B_QK
COL_AB = COL_Z + B_QK
IN_COLS = COL_AB + 2 * B_HEADS
N_IDX = COL_IDX
N_A = N_IDX + IDX_DIM + IDX_HEADS
N_B = N_A + B_HEADS
N_Z = N_B + B_HEADS
N_COLS = N_Z + B_QK
MASKED = -1e30
TAKEN = -3e38
INADMISSIBLE = -2e30

F32 = mybir.dt.float32
U32 = mybir.dt.uint32
F32R = mybir.dt.float32r
ALU = mybir.AluOpType
ACT = mybir.ActivationFunctionType
AX = mybir.AxisListType


@contextmanager
def phase(nc, name, signals):
    sems = {n: nc.alloc_semaphore(f"{name}_{n}") for n in signals.split()}
    yield sems
    nc.clear_and_free_semaphores(list(sems.values()))
    nc.all_engine_barrier()


class Order:

    def __init__(self, eng, sem, base=0):
        self.eng, self.sem, self.base, self.n = eng, sem, base, 0

    def then(self, ins):
        self.n += 1
        ins.then_inc(self.sem, 1)
        self.eng.wait_ge(self.sem, self.base + self.n)


def bcast(ap, axis, n):
    shape = list(ap.shape)
    shape.insert(axis, n)
    return ap.unsqueeze(axis).to_broadcast(shape)


def wait(eng, sem, value):
    if not isinstance(value, int) or value > 0:
        eng.wait_ge(sem, value)


def product(pe, out, lhsT, rhs, chunks):
    for k in range(chunks):
        (lh, ll), (rh, rl) = lhsT(k), rhs(k)
        pe.matmul(out, lhsT=lh, rhs=rh, start=(k == 0), stop=False)
        pe.matmul(out, lhsT=lh, rhs=rl, start=False, stop=False)
        last = pe.matmul(out, lhsT=ll, rhs=rh, start=False, stop=(k == chunks - 1))
    return last


def load_all(nc, name, pairs):
    with phase(nc, name, "loaded") as s, nc.Block() as block:
        @block.sync
        def _(sp):
            for dst, src in pairs:
                sp.dma_start(dst, src).then_inc(s["loaded"], 16)
            sp.wait_ge(s["loaded"], 16 * len(pairs))


def norm_transposed(nc, name, src, dram, gain, ident, outT, tiles, outL=None):
    with ExitStack() as ctx:
        sb = lambda n, sh: ctx.enter_context(nc.sbuf_tensor(f"{name}_{n}", sh, F32))
        ps = ctx.enter_context(nc.psum_tensor(f"{name}_ps", [P, 4, 512], F32))
        normed = sb("normed", [P, tiles, D_MODEL])
        junk = sb("junk", [P, 2, D_MODEL])
        ssq = sb("ssq", [P, tiles])
        root = sb("root", [P, tiles])
        rinv = sb("rinv", [P, tiles])
        epst = sb("eps", [P, 1])
        per = min(4, tiles)
        groups = tiles // per
        s = ctx.enter_context(phase(nc, name, "eps_ready squared rooted inverted scaled transposed evac_v evac_s " + " ".join(f"src{t}" for t in range(tiles))))
        block = ctx.enter_context(nc.Block())

        @block.sync
        def _(sp):
            if dram is not None:
                for t in range(tiles):
                    sp.dma_start(src[:, t, :], dram[t * P:(t + 1) * P, :]).then_inc(s[f"src{t}"], 16)

        @block.scalar
        def _(act):
            for t in range(tiles):
                if dram is not None:
                    act.wait_ge(s[f"src{t}"], 16)
                if t >= 2:
                    act.wait_ge(s["squared"], t - 1)
                act.activation(junk[:, t % 2, :], src[:, t, :], ACT.Square, accum_out=ssq[:, t:t + 1]).then_inc(s["squared"], 1)
            act.wait_ge(s["squared"], tiles)
            act.wait_ge(s["eps_ready"], 1)
            act.activation(root[:, :], ssq[:, :], ACT.Sqrt, bias=epst[:, :], scale=1.0 / D_MODEL).then_inc(s["rooted"], 1)
            for b in range(0 if outL else 1, groups * DK, 1 if outL else 2):
                k, g = b // groups, b % groups
                act.wait_ge(s["transposed"], b + 1)
                act.activation(outT[:, k, g * per * P:(g + 1) * per * P], ps[:, b % 4, 0:per * P], ACT.Copy, scale=gain[:, k:k + 1]).then_inc(s["evac_s"], 1)

        @block.vector
        def _(dve):
            dve.memset(epst[:, :], EPS).then_inc(s["eps_ready"], 1)
            dve.wait_ge(s["rooted"], 1)
            dve.reciprocal(rinv[:, :], root[:, :]).then_inc(s["inverted"], 1)
            dve.wait_ge(s["inverted"], 1)
            for t in range(tiles):
                dve.tensor_scalar(normed[:, t, :], src[:, t, :], rinv[:, t:t + 1], None, ALU.mult).then_inc(s["scaled"], 1)
            if outL:
                for b in range(groups * DK):
                    k, g = b // groups, b % groups
                    cols = slice(g * per * P, (g + 1) * per * P)
                    dve.wait_ge(s["evac_s"], b + 1)
                    dve.scalar_tensor_tensor(outL[:, k, cols], ps[:, b % 4, 0:per * P], gain[:, k:k + 1], outT[:, k, cols].bitcast(F32), ALU.mult, ALU.subtract).then_inc(s["evac_v"], 1)
                return
            for b in range(0, groups * DK, 2):
                k, g = b // groups, b % groups
                dve.wait_ge(s["transposed"], b + 1)
                dve.tensor_scalar(outT[:, k, g * per * P:(g + 1) * per * P], ps[:, b % 4, 0:per * P], gain[:, k:k + 1], None, ALU.mult).then_inc(s["evac_v"], 1)

        @block.tensor
        def _(pe):
            for b in range(groups * DK):
                k, g = b // groups, b % groups
                pe.wait_ge(s["scaled"], (g + 1) * per)
                if b >= 4:
                    if outL:
                        pe.wait_ge(s["evac_v"], b - 3)
                    else:
                        pe.wait_ge(s["evac_s"] if b % 2 else s["evac_v"], (b - 4) // 2 + 1)
                for j in range(per):
                    last = pe.transpose(ps[:, b % 4, j * P:(j + 1) * P], normed[:, g * per + j, k * P:(k + 1) * P], ident)
                last.then_inc(s["transposed"], 1)


def project(nc, a, hT, nat, proj, ident):
    w_in = a["w_in"].rearrange("(k p) c -> p k c", p=P)
    chunks = 3 * B_QK // P
    with ExitStack() as ctx:
        sb = lambda n, sh: ctx.enter_context(nc.sbuf_tensor(n, sh, F32))
        w1 = sb("w1", [P, DK, 512])
        w2 = sb("w2", [P, DK, 80])
        wc = sb("wc", [P, 2, DK, P])
        raw = sb("raw", [P, 2, CONV - 1 + SEQ])
        conv = sb("conv", [P, 2, SEQ])
        cw = sb("cw", [P, chunks, CONV])
        psn = ctx.enter_context(nc.psum_tensor("psn", [P, 4, 512], F32))
        pst = ctx.enter_context(nc.psum_tensor("pst", [P, 2, 1024], F32))
        s = ctx.enter_context(phase(nc, "project", "cw_loaded wc0 wc1 w1_loaded w2_loaded w3_loaded padded chunk_done raw_ready conv_step conv_done silu_done nat_done nat_evac tok_done tok_evac"))
        block = ctx.enter_context(nc.Block())
        groups = [(w1, "w1_loaded", 16, 0, 512), (w2, "w2_loaded", 32, N_IDX, 80), (w1, "w3_loaded", 16, N_Z, 512)]

        @block.sync
        def _(sp):
            sp.dma_start(cw[:, :, :], a["conv_w"]).then_inc(s["cw_loaded"], 16)
            for c in range(chunks):
                if c >= 2:
                    sp.wait_ge(s["chunk_done"], c - 1)
                sp.dma_start(wc[:, c % 2], w_in[:, :, COL_QKV + c * P:COL_QKV + (c + 1) * P]).then_inc(s[f"wc{c % 2}"], 16)
                if c == 1:
                    sp.dma_start(w1[:, :, :], w_in[:, :, 0:512]).then_inc(s["w1_loaded"], 16)
                    sp.dma_start(w2[:, :, 0:72], w_in[:, :, COL_IDX:COL_QKV]).then_inc(s["w2_loaded"], 16)
                    sp.dma_start(w2[:, :, 72:80], w_in[:, :, COL_AB:IN_COLS]).then_inc(s["w2_loaded"], 16)
            sp.wait_ge(s["tok_done"], NT)
            sp.dma_start(w1[:, :, :], w_in[:, :, COL_Z:COL_AB]).then_inc(s["w3_loaded"], 16)

        @block.tensor
        def _(pe):
            def to_token_major(c):
                pe.wait_ge(s["silu_done"], c + 1)
                if c >= 2:
                    pe.wait_ge(s["nat_evac"], c - 1)
                for t in range(NT):
                    last = pe.transpose(pst[:, c % 2, t * P:(t + 1) * P], conv[:, c % 2, t * P:(t + 1) * P], ident)
                last.then_inc(s["nat_done"], 1)

            for c in range(chunks):
                pe.wait_ge(s[f"wc{c % 2}"], 16 * (c // 2 + 1))
                if c >= 2:
                    pe.wait_ge(s["raw_ready"], c - 1)
                for half in range(2):
                    for k in range(DK):
                        last = pe.matmul(psn[:, 2 * (c % 2) + half, :], lhsT=wc[:, c % 2, k, :], rhs=hT[:, k, half * 512:(half + 1) * 512], start=(k == 0), stop=(k == DK - 1))
                last.then_inc(s["chunk_done"], 1)
                if c >= 1:
                    to_token_major(c - 1)
            to_token_major(chunks - 1)
            pe.wait_ge(s["raw_ready"], chunks)
            n = 0
            for w, loaded, count, col, width in groups:
                pe.wait_ge(s[loaded], count)
                for t in range(NT):
                    if n >= 4:
                        pe.wait_ge(s["tok_evac"], n - 3)
                    for k in range(DK):
                        last = pe.matmul(psn[:, n % 4, 0:width], lhsT=hT[:, k, t * P:(t + 1) * P], rhs=w[:, k, :], start=(k == 0), stop=(k == DK - 1))
                    last.then_inc(s["tok_done"], 1)
                    n += 1

        @block.scalar
        def _(act):
            for c in range(chunks):
                act.wait_ge(s["chunk_done"], c + 1)
                if c == 0:
                    act.wait_ge(s["padded"], 1)
                if c >= 2:
                    act.wait_ge(s["conv_done"], c - 1)
                act.activation(raw[:, c % 2, CONV - 1:], psn[:, 2 * (c % 2):2 * (c % 2) + 2, :].rearrange("p a n -> p (a n)"), ACT.Copy).then_inc(s["raw_ready"], 1)
                act.wait_ge(s["conv_done"], c + 1)
                act.activation(conv[:, c % 2, :], conv[:, c % 2, :], ACT.Silu).then_inc(s["silu_done"], 1)
            n = 0
            for w, loaded, count, col, width in groups:
                for t in range(NT):
                    act.wait_ge(s["tok_done"], n + 1)
                    act.activation(proj[:, t, col:col + width], psn[:, n % 4, 0:width], ACT.Copy).then_inc(s["tok_evac"], 1)
                    n += 1

        @block.vector
        def _(dve):
            order = Order(dve, s["conv_step"])
            dve.memset(raw[:, :, 0:CONV - 1], 0.0).then_inc(s["padded"], 1)
            dve.wait_ge(s["cw_loaded"], 16)

            def evacuate(c):
                dve.wait_ge(s["nat_done"], c + 1)
                dve.tensor_copy(nat[:, :, c * P:(c + 1) * P], pst[:, c % 2, :].rearrange("p (t n) -> p t n", t=NT)).then_inc(s["nat_evac"], 1)

            for c in range(chunks):
                dve.wait_ge(s["raw_ready"], c + 1)
                if c >= 2:
                    dve.wait_ge(s["nat_done"], c - 1)
                out = conv[:, c % 2, :]
                order.then(dve.tensor_scalar(out, raw[:, c % 2, 0:SEQ], cw[:, c, 0:1], None, ALU.mult))
                for i in range(1, CONV):
                    ins = dve.scalar_tensor_tensor(out, raw[:, c % 2, i:i + SEQ], cw[:, c, i:i + 1], out, ALU.mult, ALU.add)
                    if i < CONV - 1:
                        order.then(ins)
                ins.then_inc(s["conv_done"], 1)
                if c >= 1:
                    evacuate(c - 1)
            evacuate(chunks - 1)


def delta_net(nc, a, proj, nat, mix, scratch, consts):
    H, W = B_HEADS, B_HEADS * P
    ident, tri, dmask, strict, lev, levT = (consts[n] for n in ("ident", "tri", "dmask", "strict", "lev", "levT"))
    with ExitStack() as ctx:
        sb = lambda n, sh: ctx.enter_context(nc.sbuf_tensor(n, sh, F32))
        pt = [ctx.enter_context(nc.psum_tensor(f"dn{i}", [P, 512], F32)) for i in range(8)]
        pq, pk, pd, pg, pc, px, pe_, po = pt
        h4 = lambda x: x[:, :].rearrange("p (h n) -> p h n", h=H)
        dtb, alog, gon = sb("dtb", [P, H]), sb("alog", [P, H]), sb("gon", [P, P])
        abs_ = sb("ab_abs", [P, NT, H])
        soft = sb("ab_soft", [P, NT, H])
        gate = sb("ab_gate", [P, NT, H])
        beta = sb("beta", [P, NT, H])
        g4 = sb("g4", [P, 4, NT, H])
        eg = sb("eg", [P, NT, H])
        etail = sb("etail", [P, NT, H])
        dch = sb("dch", [P, 2, NT, H])
        beg = sb("beg", [P, NT, H])
        epst = sb("dn_eps", [P, 1])
        sq = sb("dn_sq", [P, 2 * H, P])
        ssq, root, rinv = sb("dn_ssq", [P, 2 * H]), sb("dn_root", [P, 2 * H]), sb("dn_rinv", [P, 2 * H])
        qk = sb("dn_qk", [P, 2 * H, P])
        qd, vb, kbg, ktail, diag = (sb(f"dn_{n}", [P, H, P]) for n in ("qd", "vb", "kbg", "ktail", "diag"))
        qT, kT, qdT = (sb(f"dn_{n}", [P, H, P]) for n in ("qT", "kT", "qdT"))
        dexp, decay, dstr, m, intra, mT, intraT = (sb(f"dn_{n}", [P, H, P]) for n in ("dexp", "decay", "dstr", "m", "intra", "mT", "intraT"))
        tiles = (scratch[:, i // 2, (i % 2) * W:(i % 2 + 1) * W].rearrange("p (h n) -> p h n", h=H) for i in range(2 * NT))
        x, xT, cT, y, u, wT, vnew, state, o, osq, zs = (next(tiles) for _ in range(11))
        oss, oroot, orinv = sb("dn_oss", [P, H]), sb("dn_oroot", [P, H]), sb("dn_orinv", [P, H])
        s = ctx.enter_context(phase(nc, "delta",
            "rows_loaded dt_added abs_done negexp_done plus_one_done log_done alog_done gate_ready sums_mm sums_ready gate_exps beta_ready "
            "vorder aorder ssq_ready root_ready nat_ready diag_ready transposed qT_ready row_mm kk_mm dexp_ready "
            "decay_ready m_ready mT_mm intraT_ready c_ready y_mm y_ready x_mm x_ready uw_mm wT_ready u_ready "
            "vp_mm vnew_ready o_mm su_mm state_ready oss_ready oroot_ready z_ready block_done"))
        block = ctx.enter_context(nc.Block())
        VSTEPS = 24

        @block.sync
        def _(sp):
            sp.dma_start(dtb[:, :], a["dt_bias"].partition_broadcast(P)).then_inc(s["rows_loaded"], 16)
            sp.dma_start(alog[:, :], a["A_log"].partition_broadcast(P)).then_inc(s["rows_loaded"], 16)
            sp.dma_start(gon[:, :], a["g_onorm"].partition_broadcast(P)).then_inc(s["rows_loaded"], 16)

        @block.scalar
        def _(act):
            act.wait_ge(s["rows_loaded"], 48)
            act.activation(alog[:, :], alog[:, :], ACT.Exp).then_inc(s["alog_done"], 1)
            act.activation(beta[:, :, :], proj[:, :, N_B:N_B + H], ACT.Sigmoid).then_inc(s["beta_ready"], 1)
            act.wait_ge(s["dt_added"], 1)
            act.activation(abs_[:, :, :], gate[:, :, :], ACT.Abs).then_inc(s["abs_done"], 1)
            act.wait_ge(s["abs_done"], 1)
            act.activation(soft[:, :, :], abs_[:, :, :], ACT.Exp, scale=-1.0).then_inc(s["negexp_done"], 1)
            act.wait_ge(s["plus_one_done"], 1)
            act.activation(soft[:, :, :], soft[:, :, :], ACT.Ln).then_inc(s["log_done"], 1)
            act.wait_ge(s["sums_ready"], 2)
            act.activation(eg[:, :, :], g4[:, 0], ACT.Exp)
            act.activation(etail[:, :, :], etail[:, :, :], ACT.Exp)
            act.activation(dch[:, :, :, :], g4[:, 2:4], ACT.Exp).then_inc(s["gate_exps"], 1)
            with act.Fori(0, NT) as t:
                act.wait_ge(s["ssq_ready"], t + 1)
                act.activation(root[:, :], ssq[:, :], ACT.Sqrt, bias=epst[:, :]).then_inc(s["root_ready"], 1)
                act.wait_ge(s["transposed"], t + 1)
                act.activation(qT[:, :, :], h4(pq), ACT.Copy)
                act.activation(kT[:, :, :], h4(pk), ACT.Copy)
                act.activation(qdT[:, :, :], h4(pd), ACT.Copy).then_inc(s["qT_ready"], 1)
                act.wait_ge(s["dexp_ready"], t + 1)
                act.activation(decay[:, :, :], dexp[:, :, :], ACT.Exp).then_inc(s["decay_ready"], 1)
                act.wait_ge(s["mT_mm"], t + 1)
                act.activation(intraT[:, :, :], h4(pk), ACT.Copy).then_inc(s["intraT_ready"], 1)
                for l in range(5):
                    act.wait_ge(s["y_mm"], t * 5 + l + 1)
                    act.activation(y[:, :, :], h4(pd), ACT.Copy).then_inc(s["y_ready"], 1)
                act.wait_ge(s["uw_mm"], t + 1)
                act.activation(wT[:, :, :], h4(px), ACT.Copy).then_inc(s["wT_ready"], 1)
                act.activation(zs[:, :, :], proj[:, bass.ds(t, 1), N_Z:].rearrange("p a (h n) -> p (a h) n", h=H), ACT.Silu).then_inc(s["z_ready"], 1)
                act.wait_ge(s["oss_ready"], t + 1)
                act.activation(oroot[:, :], oss[:, :], ACT.Sqrt, bias=epst[:, :], scale=1.0 / B_DIM).then_inc(s["oroot_ready"], 1)

        @block.tensor
        def _(pe):
            pe.wait_ge(s["gate_ready"], 1)
            for i in range(4):
                last = pe.matmul(pg[:, i * 32:(i + 1) * 32], lhsT=tri[:, i, :], rhs=gate[:, :, :].rearrange("p t h -> p (t h)"), start=True, stop=True)
            last.then_inc(s["sums_mm"], 1)
            with pe.Fori(0, NT) as t:
                pe.wait_ge(s["nat_ready"], t + 1)
                for h in range(H):
                    pe.transpose(h4(pq)[:, h], qk[:, h, :], ident)
                for h in range(H):
                    pe.transpose(h4(pk)[:, h], qk[:, H + h, :], ident)
                for h in range(H):
                    last = pe.transpose(h4(pd)[:, h], qd[:, h, :], ident)
                last.then_inc(s["transposed"], 1)
                pe.wait_ge(s["diag_ready"], t + 1)
                pe.matmul(pg[:, :], lhsT=consts["ones"], rhs=diag[:, :, :].rearrange("p h n -> p (h n)"), start=True, stop=True).then_inc(s["row_mm"], 1)
                pe.wait_ge(s["qT_ready"], t + 1)
                for h in range(H):
                    pe.matmul(h4(pc)[:, h], lhsT=kT[:, h, :], rhs=kT[:, h, :], start=True, stop=True)
                for h in range(H):
                    last = pe.matmul(h4(px)[:, h], lhsT=qT[:, h, :], rhs=kT[:, h, :], start=True, stop=True)
                last.then_inc(s["kk_mm"], 1)
                pe.wait_ge(s["m_ready"], t + 1)
                for h in range(H):
                    pe.transpose(h4(pq)[:, h], m[:, h, :], ident)
                for h in range(H):
                    last = pe.transpose(h4(pk)[:, h], intra[:, h, :], ident)
                last.then_inc(s["mT_mm"], 1)
                for l in range(5):
                    pe.wait_ge(s["c_ready"], t * 5 + l + 1)
                    for h in range(H):
                        last = pe.matmul(h4(pd)[:, h], lhsT=cT[:, h, :], rhs=x[:, h, :], start=True, stop=True)
                    last.then_inc(s["y_mm"], 1)
                    pe.wait_ge(s["y_ready"], t * 5 + l + 1)
                    for h in range(H):
                        pe.matmul(h4(pg)[:, h], lhsT=xT[:, h, :], rhs=y[:, h, :], start=True, stop=True)
                    for h in range(H):
                        last = pe.matmul(h4(pc)[:, h], lhsT=y[:, h, :], rhs=xT[:, h, :], start=True, stop=True)
                    last.then_inc(s["x_mm"], 1)
                pe.wait_ge(s["x_ready"], t * 5 + 5)
                for h in range(H):
                    pe.matmul(h4(pc)[:, h], lhsT=xT[:, h, :], rhs=vb[:, h, :], start=True, stop=True)
                for h in range(H):
                    last = pe.matmul(h4(px)[:, h], lhsT=kbg[:, h, :], rhs=xT[:, h, :], start=True, stop=True)
                last.then_inc(s["uw_mm"], 1)
                pe.wait_ge(s["wT_ready"], t + 1)
                for c in range(2):
                    r = slice(c * CHUNK, (c + 1) * CHUNK)
                    pe.wait_ge(s["state_ready"], 2 * t + c + 1)
                    for h in range(H):
                        last = pe.matmul(h4(pe_)[r, h], lhsT=wT[:, h, r], rhs=state[:, h, :], start=True, stop=True)
                    last.then_inc(s["vp_mm"], 1)
                    pe.wait_ge(s["vnew_ready"], 2 * t + c + 1)
                    for h in range(H):
                        last = pe.matmul(h4(pq)[:, h], lhsT=ktail[r, h, :], rhs=vnew[r, h, :], start=True, stop=True)
                    last.then_inc(s["su_mm"], 1)
                    for h in range(H):
                        pe.matmul(h4(po)[r, h], lhsT=qdT[:, h, r], rhs=state[:, h, :], start=True, stop=False)
                        last = pe.matmul(h4(po)[r, h], lhsT=intraT[r, h, r], rhs=vnew[r, h, :], start=False, stop=True)
                    last.then_inc(s["o_mm"], 1)

        @block.vector
        def _(dve):
            order = Order(dve, s["vorder"])
            ab = proj[:, :, N_A:N_A + H]
            row = lambda r: bcast(r[:, :], 1, NT)
            dve.memset(epst[:, :], EPS)
            order.then(dve.memset(state[:, :, :], 0.0))
            dve.wait_ge(s["rows_loaded"], 48)
            dve.tensor_tensor(gate[:, :, :], ab, row(dtb), ALU.add).then_inc(s["dt_added"], 1)
            dve.wait_ge(s["negexp_done"], 1)
            dve.tensor_scalar(soft[:, :, :], soft[:, :, :], 1.0, None, ALU.add).then_inc(s["plus_one_done"], 1)
            dve.wait_ge(s["log_done"], 1)
            order.then(dve.scalar_tensor_tensor(soft[:, :, :], gate[:, :, :], 0.0, soft[:, :, :], ALU.max, ALU.add))
            dve.wait_ge(s["alog_done"], 1)
            dve.scalar_tensor_tensor(gate[:, :, :], soft[:, :, :], -1.0, row(alog), ALU.mult, ALU.mult).then_inc(s["gate_ready"], 1)
            dve.wait_ge(s["sums_mm"], 1)
            dve.tensor_copy(g4[:, :, :, :].rearrange("p a t h -> p (a t h)"), pg[:, 0:128]).then_inc(s["sums_ready"], 1)
            dve.wait_ge(s["sums_ready"], 1)
            dve.tensor_tensor(etail[:, :, :], g4[:, 1], g4[:, 0], ALU.subtract).then_inc(s["sums_ready"], 1)
            dve.wait_ge(s["gate_exps"], 1)
            dve.wait_ge(s["beta_ready"], 1)
            order.then(dve.tensor_tensor(beg[:, :, :], beta[:, :, :], eg[:, :, :], ALU.mult))
            base = order.n
            dve.sem_inc(s["state_ready"], 1)
            with dve.Fori(0, NT) as t:
                order = Order(dve, s["vorder"], t * VSTEPS + base)
                one = lambda z: z[:, bass.ds(t, 1), :].rearrange("p a h -> p (a h)")
                wide = lambda z: bcast(one(z), 2, P)
                qkt = nat[:, bass.ds(t, 1), 0:2 * W].rearrange("p a (h n) -> p (a h) n", n=P)
                vt = nat[:, bass.ds(t, 1), 2 * W:3 * W].rearrange("p a (h n) -> p (a h) n", n=P)
                order.then(dve.tensor_tensor(sq[:, :, :], qkt, qkt, ALU.mult))
                dve.tensor_reduce(ssq[:, :], sq[:, :, :], AX.X, ALU.add).then_inc(s["ssq_ready"], 1)
                order.then(dve.tensor_tensor(diag[:, :, :], bcast(ident, 1, H), bcast(g4[:, 0, bass.ds(t, 1), :].rearrange("p a h -> p (a h)"), 2, P), ALU.mult))
                dve.sem_inc(s["diag_ready"], 1)
                order.then(dve.tensor_tensor(vb[:, :, :], vt, wide(beta), ALU.mult))
                dve.wait_ge(s["root_ready"], t + 1)
                order.then(dve.reciprocal(rinv[:, :], root[:, :]))
                order.then(dve.tensor_scalar(rinv[:, 0:H], rinv[:, 0:H], B_DIM ** -0.5, None, ALU.mult))
                order.then(dve.tensor_tensor(qk[:, :, :], qkt, bcast(rinv[:, :], 2, P), ALU.mult))
                dve.tensor_tensor(qd[:, :, :], qk[:, 0:H, :], wide(eg), ALU.mult).then_inc(s["nat_ready"], 1)
                dve.tensor_tensor(kbg[:, :, :], qk[:, H:, :], wide(beg), ALU.mult)
                order.then(dve.tensor_tensor(ktail[:, :, :], qk[:, H:, :], wide(etail), ALU.mult))
                dve.wait_ge(s["row_mm"], t + 1)
                order.then(dve.scalar_tensor_tensor(dexp[:, :, :], h4(pg), -1.0, bcast(dmask, 1, H), ALU.mult, ALU.add))
                dve.tensor_tensor(dexp[:, :, :], dexp[:, :, :], bcast(g4[:, 0, bass.ds(t, 1), :].rearrange("p a h -> p (a h)"), 2, P), ALU.add).then_inc(s["dexp_ready"], 1)
                dve.wait_ge(s["decay_ready"], t + 1)
                dve.wait_ge(s["kk_mm"], t + 1)
                order.then(dve.tensor_tensor(intra[:, :, :], h4(px), decay[:, :, :], ALU.mult))
                order.then(dve.tensor_tensor(dstr[:, :, :], decay[:, :, :], bcast(strict, 1, H), ALU.mult))
                order.then(dve.tensor_tensor(dstr[:, :, :], dstr[:, :, :], wide(beta), ALU.mult))
                dve.tensor_tensor(m[:, :, :], h4(pc), dstr[:, :, :], ALU.mult).then_inc(s["m_ready"], 1)
                dve.wait_ge(s["m_ready"], t + 1)
                order.then(dve.tensor_tensor(x[:, :, :], m[:, :, :], bcast(lev, 1, H), ALU.mult))
                order.then(dve.scalar_tensor_tensor(x[:, :, :], x[:, :, :], -1.0, bcast(ident, 1, H), ALU.mult, ALU.add))
                dve.wait_ge(s["mT_mm"], t + 1)
                order.then(dve.tensor_copy(mT[:, :, :], h4(pq)))
                order.then(dve.tensor_tensor(xT[:, :, :], mT[:, :, :], bcast(levT[:, 0, :], 1, H), ALU.mult))
                order.then(dve.scalar_tensor_tensor(xT[:, :, :], xT[:, :, :], -1.0, bcast(ident, 1, H), ALU.mult, ALU.add))
                for l in range(5):
                    dve.tensor_tensor(cT[:, :, :], mT[:, :, :], bcast(levT[:, l + 1, :], 1, H), ALU.mult).then_inc(s["c_ready"], 1)
                    dve.wait_ge(s["x_mm"], t * 5 + l + 1)
                    dve.tensor_tensor(x[:, :, :], x[:, :, :], h4(pg), ALU.subtract)
                    dve.tensor_tensor(xT[:, :, :], xT[:, :, :], h4(pc), ALU.subtract).then_inc(s["x_ready"], 1)
                    dve.wait_ge(s["x_ready"], t * 5 + l + 1)
                dve.wait_ge(s["uw_mm"], t + 1)
                order.then(dve.tensor_copy(u[:, :, :], h4(pc)))
                for c in range(2):
                    r = slice(c * CHUNK, (c + 1) * CHUNK)
                    dve.wait_ge(s["vp_mm"], 2 * t + c + 1)
                    dve.tensor_tensor(vnew[r, :, :], u[r, :, :], h4(pe_)[r], ALU.subtract).then_inc(s["vnew_ready"], 1)
                    dve.wait_ge(s["o_mm"], 2 * t + c + 1)
                    order.then(dve.tensor_tensor(state[:, :, :], state[:, :, :], bcast(dch[:, c, bass.ds(t, 1), :].rearrange("p a h -> p (a h)"), 2, P), ALU.mult))
                    dve.tensor_tensor(state[:, :, :], state[:, :, :], h4(pq), ALU.add).then_inc(s["state_ready"], 1)
                    dve.wait_ge(s["state_ready"], 2 * t + c + 2)
                order.then(dve.tensor_copy(o[:, :, :], h4(po)))
                order.then(dve.tensor_tensor(osq[:, :, :], o[:, :, :], o[:, :, :], ALU.mult))
                dve.tensor_reduce(oss[:, :], osq[:, :, :], AX.X, ALU.add).then_inc(s["oss_ready"], 1)
                order.then(dve.tensor_tensor(o[:, :, :], o[:, :, :], bcast(gon[:, :], 1, H), ALU.mult))
                dve.wait_ge(s["z_ready"], t + 1)
                order.then(dve.tensor_tensor(o[:, :, :], o[:, :, :], zs[:, :, :], ALU.mult))
                dve.wait_ge(s["oroot_ready"], t + 1)
                order.then(dve.reciprocal(orinv[:, :], oroot[:, :]))
                dve.tensor_tensor(mix[:, bass.ds(t, 1), W:2 * W].rearrange("p a (h n) -> p (a h) n", n=P), o[:, :, :], bcast(orinv[:, :], 2, P), ALU.mult).then_inc(s["block_done"], 1)
                assert order.n == VSTEPS


def shape_constants():
    i = np.arange(P)
    same = (i[:, None] // CHUNK) == (i[None, :] // CHUNK)
    j_le_i = i[:, None] <= i[None, :]
    even = np.repeat((i < CHUNK)[:, None], P, 1)
    tri = np.stack([same & j_le_i, same, even, ~even], 1)
    lower = same & (i[:, None] >= i[None, :])
    lev = [(i[:, None] // (2 * b) == i[None, :] // (2 * b)) & (i[:, None] // b % 2 == 1) & (i[None, :] // b % 2 == 0) for b in (1, 2, 4, 8, 16, 32)]
    rel = np.arange(NREL) - (NEAR - 1)
    half, exact = REL_BUCKETS // 2, REL_BUCKETS // 4
    n = np.abs(rel)
    large = exact + (np.log(np.maximum(n, exact).astype(np.float32) / np.float32(exact)) / np.float32(math.log(REL_MAX_DIST / exact)) * np.float32(half - exact)).astype(np.int32)
    bucket = np.where(rel > 0, half, 0) + np.where(n < exact, n, np.minimum(large, half - 1))
    b = np.arange(REL_BUCKETS)[:, None]
    relhot = (b == bucket[None, :]).astype(np.float32) - (b == half - 1).astype(np.float32)
    f = lambda z: np.ascontiguousarray(z).astype(np.float32)
    return {
        "ident": f(np.eye(P)), "flip": f(np.eye(P)[::-1]), "ones": f(np.ones((P, P))), "tri": f(tri),
        "dmask": f(np.where(lower, 0, MASKED)), "strict": f(lower & (i[:, None] > i[None, :])),
        "lev": f(lev[0]), "levT": f(np.stack([z.T for z in lev], 1)),
        "row_starts": f(np.broadcast_to(np.concatenate([[0], np.arange(16, 72, 8), np.arange(72, 80)]), (P, P_TOPK))),
        "relhot": f(relhot), "iota": f(np.broadcast_to(i[None, :], (P, P))),
    }


def sparse_prepare(nc, a, proj, gains, consts, idxT, qiT, qT, kT, v, widx, near):
    with ExitStack() as ctx:
        sb = lambda n, sh: ctx.enter_context(nc.sbuf_tensor(n, sh, F32))
        w = {n: sb(f"sp_{n}", [P, 2, 512]) for n in ("w_iq", "w_uq", "w_uk", "w_uv")}
        latT = sb("sp_latT", [P, 4, SEQ])
        keys = sb("sp_keys", [P, NT, 2, IDX_DIM])
        junk = sb("sp_junk", [P, 2, 256])
        ssq, root, rinv, epst = sb("sp_ssq", [P, 3, NT]), sb("sp_root", [P, 3, NT]), sb("sp_rinv", [P, 3, NT]), sb("sp_eps", [P, 1])
        relb, rowb = sb("sp_relb", [REL_BUCKETS, A_HEADS]), sb("sp_rowb", [A_HEADS, NREL])
        shifted = sb("sp_shifted", [P, A_HEADS, NEAR])
        pt = [ctx.enter_context(nc.psum_tensor(f"sp{i}", [P, 512], F32)) for i in range(8)]
        s = ctx.enter_context(phase(nc, "sparse_prep", "w_iq w_uq w_uk w_uv relb_loaded bias_mm bias_ready bias_stored near_loaded eps_ready squared rooted vorder normed transposed lat_ready proj_mm evac"))
        block = ctx.enter_context(nc.Block())
        banks = [(j, half) for j in range(5) for half in range(2)]
        heads = [("w_iq", 0, qiT, 1.0, m, half) for m in range(4) for half in range(2)] + \
                [("w_uq", 0, qT, A_DIM ** -0.5, m, half) for m in range(4) for half in range(2)] + \
                [("w_uk", 2, kT, 1.0, m, half) for m in range(4) for half in range(2)]

        @block.sync
        def _(sp):
            sp.dma_start(relb[:, :], a["rel_bias"]).then_inc(s["relb_loaded"], 16)
            for n in w:
                sp.dma_start(w[n][:, :, :], a[n].rearrange("(k p) c -> p k c", p=P)).then_inc(s[n], 16)
            sp.wait_ge(s["bias_ready"], 1)
            sp.dma_start(a["bias_rows"], rowb[:, :]).then_inc(s["bias_stored"], 16)
            sp.wait_ge(s["bias_stored"], 16)
            sp.dma_start(shifted[:, :, :], bass.AP(a["bias_rows"].tensor, 0, [[1, P], [NREL, A_HEADS], [1, NEAR]])).then_inc(s["near_loaded"], 16)

        @block.scalar
        def _(act):
            n = 0
            for g, (col, width) in enumerate(((0, A_LORA), (A_LORA, A_LORA), (N_IDX, IDX_DIM))):
                for t in range(NT):
                    if n >= 2:
                        act.wait_ge(s["squared"], n - 1)
                    act.activation(junk[:, n % 2, 0:width], proj[:, t, col:col + width], ACT.Square, accum_out=ssq[:, g, t:t + 1]).then_inc(s["squared"], 1)
                    n += 1
            act.wait_ge(s["squared"], n)
            act.wait_ge(s["eps_ready"], 1)
            act.activation(root[:, 0:2], ssq[:, 0:2], ACT.Sqrt, bias=epst[:, :], scale=1.0 / A_LORA).then_inc(s["rooted"], 1)
            act.activation(root[:, 2], ssq[:, 2], ACT.Sqrt, bias=epst[:, :], scale=1.0 / IDX_DIM).then_inc(s["rooted"], 1)
            for i, (j, half) in enumerate(banks):
                act.wait_ge(s["transposed"], i + 1)
                out = latT[:, j] if j < 4 else idxT
                act.activation(out[:, half * 512:(half + 1) * 512], pt[i % 8][:, :], ACT.Copy, scale=gains[:, j:j + 1]).then_inc(s["lat_ready"], 1)

        @block.tensor
        def _(pe):
            pe.wait_ge(s["relb_loaded"], 16)
            pe.matmul(pt[7][0:A_HEADS, 0:NREL], lhsT=relb[:, :], rhs=consts["relhot"], start=True, stop=True).then_inc(s["bias_mm"], 1)
            pe.wait_ge(s["normed"], 3)
            pe.wait_ge(s["bias_ready"], 1)
            for i, (j, half) in enumerate(banks):
                if i >= 8:
                    pe.wait_ge(s["lat_ready"], i - 7)
                for b in range(4):
                    t = half * 4 + b
                    src = proj[:, t, j * P:(j + 1) * P] if j < 4 else keys[:, t].rearrange("p a d -> p (a d)")
                    last = pe.transpose(pt[i % 8][:, b * P:(b + 1) * P], src, consts["ident"])
                last.then_inc(s["transposed"], 1)
            pe.wait_ge(s["lat_ready"], len(banks))
            for i, (name, src, dst, scale, m, half) in enumerate(heads):
                pe.wait_ge(s[name], 16)
                if i >= 8:
                    pe.wait_ge(s["evac"], i - 7)
                for k in range(2):
                    last = pe.matmul(pt[i % 8][:, :], lhsT=w[name][:, k, m * P:(m + 1) * P], rhs=latT[:, src + k, half * 512:(half + 1) * 512], start=(k == 0), stop=(k == 1))
                last.then_inc(s["proj_mm"], 1)
            pe.wait_ge(s["w_uv"], 16)
            for t in range(NT):
                i = len(heads) + t
                pe.wait_ge(s["evac"], i - 7)
                for k in range(2):
                    last = pe.matmul(pt[i % 8][:, :], lhsT=latT[:, 2 + k, t * P:(t + 1) * P], rhs=w["w_uv"][:, k, :], start=(k == 0), stop=(k == 1))
                last.then_inc(s["proj_mm"], 1)
            pe.wait_ge(s["near_loaded"], 16)
            for j in range(4):
                i = len(heads) + NT + j
                pe.wait_ge(s["evac"], i - 7)
                pe.matmul(pt[i % 8][:, :], lhsT=consts["flip"], rhs=shifted[:, 2 * j:2 * j + 2, :].rearrange("p h c -> p (h c)"), start=True, stop=True).then_inc(s["proj_mm"], 1)

        @block.vector
        def _(dve):
            order = Order(dve, s["vorder"])
            dve.memset(epst[:, :], EPS).then_inc(s["eps_ready"], 1)
            dve.wait_ge(s["bias_mm"], 1)
            dve.tensor_copy(rowb[:, :], pt[7][0:A_HEADS, 0:NREL]).then_inc(s["bias_ready"], 1)
            dve.tensor_scalar(widx, proj[:, :, N_IDX + IDX_DIM:N_A], (IDX_HEADS * IDX_DIM) ** -0.5, None, ALU.mult)
            dve.wait_ge(s["rooted"], 2)
            order.then(dve.reciprocal(rinv[:, :, :], root[:, :, :]))
            for g in range(2):
                dve.tensor_tensor(proj[:, :, g * A_LORA:(g + 1) * A_LORA], proj[:, :, g * A_LORA:(g + 1) * A_LORA], bcast(rinv[:, g], 2, A_LORA), ALU.mult).then_inc(s["normed"], 1)
            for twice in range(2):
                last = dve.tensor_tensor(keys[:, :, twice, :], proj[:, :, N_IDX:N_IDX + IDX_DIM], bcast(rinv[:, 2], 2, IDX_DIM), ALU.mult)
            last.then_inc(s["normed"], 1)
            for i, (name, src, dst, scale, m, half) in enumerate(heads):
                dve.wait_ge(s["proj_mm"], i + 1)
                dve.tensor_scalar(dst[:, m, half * 512:(half + 1) * 512], pt[i % 8][:, :], scale, None, ALU.mult).then_inc(s["evac"], 1)
            for t in range(NT):
                i = len(heads) + t
                dve.wait_ge(s["proj_mm"], i + 1)
                dve.tensor_copy(v[:, t, :], pt[i % 8][:, :]).then_inc(s["evac"], 1)
            for j in range(4):
                i = len(heads) + NT + j
                dve.wait_ge(s["proj_mm"], i + 1)
                dve.tensor_copy(near[:, 2 * j:2 * j + 2, :].rearrange("p h c -> p (h c)"), pt[i % 8][:, :]).then_inc(s["evac"], 1)


def sparse_attention(nc, idxT, qiT, qT, kT, v, widx, near, mix, ident):
    H = A_HEADS
    with ExitStack() as ctx:
        sb = lambda n, sh: ctx.enter_context(nc.sbuf_tensor(n, sh, F32))
        score, mask, relu = sb("sa_score", [P, SEQ]), sb("sa_mask", [P, SEQ]), sb("sa_relu", [P, 2, SEQ])
        top8 = sb("sa_top8", [P, 8])
        logit = sb("sa_logit", [P, 2, SEQ])
        probT = sb("sa_probT", [P, 2, NT, P])
        nmax, rsum, rinv = sb("sa_nmax", [P, 2, H]), sb("sa_rsum", [P, 2, H]), sb("sa_rinv", [P, H])
        psS = ctx.enter_context(nc.psum_tensor("sa_ps", [P, 2, 1024], F32))
        psT = ctx.enter_context(nc.psum_tensor("sa_psT", [P, 1024], F32))
        psO = ctx.enter_context(nc.psum_tensor("sa_psO", [P, 2, 512], F32))
        s = ctx.enter_context(phase(nc, "sparse", "dots_mm relu_done relu_used vorder logit_done max_ready exp_done prob_mm prob_ready out_mm out_done"))
        block = ctx.enter_context(nc.Block())
        SPARSE0 = TOPK // P
        uses, relus, logits = [], 0, 0
        for b in range(NT):
            if b >= SPARSE0:
                for h in range(H):
                    uses.append((b, "index", h, relus))
                    relus += 1
            for h in range(H):
                uses.append((b, "head", h, logits))
                logits += 1

        @block.tensor
        def _(pe):
            def transpose_probs(n):
                b, h = divmod(n, H)
                pe.wait_ge(s["exp_done"], n + 1)
                if n >= 1:
                    pe.wait_ge(s["prob_ready"], n)
                for j in range(b + 1):
                    last = pe.transpose(psT[:, j * P:(j + 1) * P], logit[:, n % 2, j * P:(j + 1) * P], ident)
                last.then_inc(s["prob_mm"], 1)

            def weigh_values(n):
                b, h = divmod(n, H)
                pe.wait_ge(s["prob_ready"], n + 1)
                if h == 0 and b >= 2:
                    pe.wait_ge(s["out_done"], b - 1)
                for j in range(b + 1):
                    last = pe.matmul(psO[:, b % 2, h * A_DIM:(h + 1) * A_DIM], lhsT=probT[:, n % 2, j, :], rhs=v[:, j, h * A_DIM:(h + 1) * A_DIM], start=(j == 0), stop=(j == b))
                last.then_inc(s["out_mm"], 1)

            for u, (b, kind, h, n) in enumerate(uses):
                W = (b + 1) * P
                if u >= 2:
                    _, before, _, m = uses[u - 2]
                    pe.wait_ge(s["relu_done" if before == "index" else "logit_done"], m + 1)
                r = slice((h % 2) * A_DIM, (h % 2 + 1) * A_DIM)
                query, key = (qiT, idxT) if kind == "index" else (qT, kT[:, h // 2])
                for c in range(0, W, 512):
                    e = min(W, c + 512)
                    last = pe.matmul(psS[:, u % 2, c:e], lhsT=query[r, h // 2, b * P:(b + 1) * P], rhs=key[r, c:e], start=True, stop=True)
                last.then_inc(s["dots_mm"], 1)
                if kind == "head":
                    if n >= 1:
                        transpose_probs(n - 1)
                    if n >= 2:
                        weigh_values(n - 2)
            transpose_probs(logits - 1)
            weigh_values(logits - 2)
            weigh_values(logits - 1)

        @block.scalar
        def _(act):
            def probs_out(n):
                b = n // H
                act.wait_ge(s["prob_mm"], n + 1)
                if n >= 2:
                    act.wait_ge(s["out_mm"], n - 1)
                act.activation(probT[:, n % 2, 0:b + 1, :].rearrange("p j q -> p (j q)"), psT[:, 0:(b + 1) * P], ACT.Copy).then_inc(s["prob_ready"], 1)

            for u, (b, kind, h, n) in enumerate(uses):
                W = (b + 1) * P
                if kind == "index":
                    act.wait_ge(s["dots_mm"], u + 1)
                    if n >= 2:
                        act.wait_ge(s["relu_used"], n - 1)
                    act.activation(relu[:, n % 2, 0:W], psS[:, u % 2, 0:W], ACT.Relu).then_inc(s["relu_done"], 1)
                else:
                    act.wait_ge(s["max_ready"], n + 1)
                    act.activation(logit[:, n % 2, 0:W], logit[:, n % 2, 0:W], ACT.Exp, bias=nmax[:, b % 2, h:h + 1], accum_out=rsum[:, b % 2, h:h + 1]).then_inc(s["exp_done"], 1)
                    if n >= 1:
                        probs_out(n - 1)
            probs_out(logits - 1)

        @block.vector
        def _(dve):
            order = Order(dve, s["vorder"])

            def outputs(b):
                dve.wait_ge(s["out_mm"], H * (b + 1))
                order.then(dve.reciprocal(rinv[:, :], rsum[:, b % 2, :]))
                dve.tensor_tensor(mix[:, b, 0:H * A_DIM].rearrange("p (h d) -> p h d", h=H), psO[:, b % 2, :].rearrange("p (h d) -> p h d", h=H), bcast(rinv[:, :], 2, A_DIM), ALU.mult).then_inc(s["out_done"], 1)

            for u, (b, kind, h, n) in enumerate(uses):
                W = (b + 1) * P
                if kind == "index":
                    dve.wait_ge(s["relu_done"], n + 1)
                    if h == 0:
                        ins = dve.tensor_scalar(score[:, 0:W], relu[:, n % 2, 0:W], widx[:, b, h:h + 1], None, ALU.mult)
                    else:
                        ins = dve.scalar_tensor_tensor(score[:, 0:W], relu[:, n % 2, 0:W], widx[:, b, h:h + 1], score[:, 0:W], ALU.mult, ALU.add)
                    ins.then_inc(s["relu_used"], 1)
                    dve.wait_ge(s["relu_used"], n + 1)
                    continue
                if h == 0:
                    if b >= SPARSE0:
                        order.then(dve.memset(score[0:CHUNK, W - CHUNK:W], INADMISSIBLE))
                        for _ in range(TOPK // 8):
                            order.then(dve.max(top8[:, :], score[:, 0:W]))
                            order.then(dve.match_replace(score[:, 0:W], top8[:, :], score[:, 0:W], TAKEN))
                        order.then(dve.tensor_scalar(mask[:, 0:W], score[:, 0:W], -1e38, MASKED, ALU.is_gt, ALU.mult))
                    else:
                        order.then(dve.memset(mask[:, 0:W], 0.0))
                        order.then(dve.memset(mask[0:CHUNK, W - CHUNK:W], MASKED))
                if h == 3 and b >= 1:
                    outputs(b - 1)
                dve.wait_ge(s["dots_mm"], u + 1)
                if n >= 2:
                    dve.wait_ge(s["prob_mm"], n - 1)
                dve.tensor_tensor(logit[:, n % 2, 0:W], psS[:, u % 2, 0:W], mask[:, 0:W], ALU.add).then_inc(s["logit_done"], 1)
                dve.wait_ge(s["logit_done"], n + 1)
                lo = max(0, W - NEAR)
                tail = logit[:, n % 2, lo:W]
                order.then(dve.tensor_tensor(tail, tail, near[:, h, NEAR - (W - lo):NEAR], ALU.add))
                dve.tensor_reduce(nmax[:, b % 2, h:h + 1], logit[:, n % 2, 0:W], AX.X, ALU.max, negate=True).then_inc(s["max_ready"], 1)
            outputs(NT - 1)


def mix_out(nc, a, mix, x, ident):
    with ExitStack() as ctx:
        sb = lambda n, sh: ctx.enter_context(nc.sbuf_tensor(n, sh, F32))
        w = sb("mo_w", [P, DK, D_MODEL])
        mixT = sb("mo_mixT", [P, DK, SEQ])
        pst = ctx.enter_context(nc.psum_tensor("mo_t", [P, 4, 512], F32))
        psy = ctx.enter_context(nc.psum_tensor("mo_y", [P, 4, 512], F32))
        s = ctx.enter_context(phase(nc, "mix_out", "w_loaded x_loaded transposed mixT_ready y_mm y_added"))
        block = ctx.enter_context(nc.Block())

        @block.sync
        def _(sp):
            sp.dma_start(w[:, :, :], a["w_out"].rearrange("(k p) c -> p k c", p=P)).then_inc(s["w_loaded"], 16)
            sp.dma_start(x[:, :, :], a["x"].rearrange("(t p) c -> p t c", p=P)).then_inc(s["x_loaded"], 16)

        @block.tensor
        def _(pe):
            for b in range(2 * DK):
                half, k = divmod(b, DK)
                if b >= 4:
                    pe.wait_ge(s["mixT_ready"], b - 3)
                for j in range(4):
                    last = pe.transpose(pst[:, b % 4, j * P:(j + 1) * P], mix[:, half * 4 + j, k * P:(k + 1) * P], ident)
                last.then_inc(s["transposed"], 1)
            pe.wait_ge(s["w_loaded"], 16)
            for n in range(2 * NT):
                t, half = divmod(n, 2)
                pe.wait_ge(s["mixT_ready"], DK if t < 4 else 2 * DK)
                if n >= 4:
                    pe.wait_ge(s["y_added"], n - 3)
                for k in range(DK):
                    last = pe.matmul(psy[:, n % 4, :], lhsT=mixT[:, k, t * P:(t + 1) * P], rhs=w[:, k, half * 512:(half + 1) * 512], start=(k == 0), stop=(k == DK - 1))
                last.then_inc(s["y_mm"], 1)

        @block.scalar
        def _(act):
            for b in range(2 * DK):
                half, k = divmod(b, DK)
                act.wait_ge(s["transposed"], b + 1)
                act.activation(mixT[:, k, half * 512:(half + 1) * 512], pst[:, b % 4, :], ACT.Copy).then_inc(s["mixT_ready"], 1)

        @block.vector
        def _(dve):
            dve.wait_ge(s["x_loaded"], 16)
            for n in range(2 * NT):
                t, half = divmod(n, 2)
                xr = x[:, t, half * 512:(half + 1) * 512]
                dve.wait_ge(s["y_mm"], n + 1)
                dve.tensor_tensor(xr, xr, psy[:, n % 4, :], ALU.add).then_inc(s["y_added"], 1)


def cross_project(nc, a, hT, memT, qT, kT, v):
    with ExitStack() as ctx:
        w = {n: ctx.enter_context(nc.sbuf_tensor(f"cp_{n}", [P, DK, 512], F32)) for n in ("wk_x", "wv_x", "wq_x")}
        ps = ctx.enter_context(nc.psum_tensor("cp_ps", [P, 4, 512], F32))
        s = ctx.enter_context(phase(nc, "cross_proj", "wk_x wv_x wq_x proj_mm evac"))
        block = ctx.enter_context(nc.Block())
        jobs = [("wk_x", lambda k, h=h: w["wk_x"][:, k, h * P:(h + 1) * P], lambda k: memT[:, k, :], kT[:, h, :], MEM) for h in range(X_HEADS)]
        jobs += [("wv_x", lambda k, m=m: memT[:, k, m * P:(m + 1) * P], lambda k: w["wv_x"][:, k, :], v[:, m, :], 512) for m in range(MEM // P)]
        jobs += [("wq_x", lambda k, h=h: w["wq_x"][:, k, h * P:(h + 1) * P], lambda k, g=g: hT[:, k, g * 512:(g + 1) * 512], qT[:, h, g * 512:(g + 1) * 512], 512)
                 for h in range(X_HEADS) for g in range(2)]

        @block.sync
        def _(sp):
            for n in w:
                sp.dma_start(w[n][:, :, :], a[n].rearrange("(k p) c -> p k c", p=P)).then_inc(s[n], 16)

        @block.tensor
        def _(pe):
            for i, (name, lhsT, rhs, out, width) in enumerate(jobs):
                pe.wait_ge(s[name], 16)
                if i >= 4:
                    pe.wait_ge(s["evac"], i - 3)
                for k in range(DK):
                    last = pe.matmul(ps[:, i % 4, 0:width], lhsT=lhsT(k), rhs=rhs(k), start=(k == 0), stop=(k == DK - 1))
                last.then_inc(s["proj_mm"], 1)

        @block.vector
        def _(dve):
            for i, (name, lhsT, rhs, out, width) in enumerate(jobs):
                dve.wait_ge(s["proj_mm"], i + 1)
                dve.tensor_copy(out, ps[:, i % 4, 0:width]).then_inc(s["evac"], 1)


def cross_attend(nc, a, qT, kT, v, x, ident):
    H, SCALE = X_HEADS, X_DIM ** -0.5
    with ExitStack() as ctx:
        sb = lambda n, sh: ctx.enter_context(nc.sbuf_tensor(n, sh, F32))
        wo = sb("ca_wo", [P, H, D_MODEL])
        prob = sb("ca_prob", [P, 2, H, MEM])
        probT = sb("ca_probT", [P, H, 2, P])
        oT = sb("ca_oT", [P, H, P])
        nmax, rsum, rinv = sb("ca_nmax", [P, H]), sb("ca_rsum", [P, H]), sb("ca_rinv", [P, H])
        psL = ctx.enter_context(nc.psum_tensor("ca_l", [P, H, MEM], F32))
        psT = ctx.enter_context(nc.psum_tensor("ca_t", [P, H, 2, P], F32))
        psO = ctx.enter_context(nc.psum_tensor("ca_o", [P, H, P], F32))
        psY = ctx.enter_context(nc.psum_tensor("ca_y", [P, 2, 512], F32))
        s = ctx.enter_context(phase(nc, "cross", "wo_loaded logit_mm vorder max_ready exp_done prob_ready probT_mm probT_ready o_mm oT_ready y_mm y_added"))
        block = ctx.enter_context(nc.Block())

        @block.sync
        def _(sp):
            sp.dma_start(wo[:, :, :], a["wo_x"].rearrange("(h p) c -> p h c", p=P)).then_inc(s["wo_loaded"], 16)

        @block.tensor
        def _(pe):
            def logits(t):
                if t >= 1:
                    pe.wait_ge(s["exp_done"], t)
                for h in range(H):
                    last = pe.matmul(psL[:, h, :], lhsT=qT[:, h, t * P:(t + 1) * P], rhs=kT[:, h, :], start=True, stop=True)
                last.then_inc(s["logit_mm"], 1)

            logits(0)
            pe.wait_ge(s["wo_loaded"], 16)
            for t in range(NT):
                if t + 1 < NT:
                    logits(t + 1)
                pe.wait_ge(s["prob_ready"], t + 1)
                for h in range(H):
                    for m in range(2):
                        last = pe.transpose(psT[:, h, m, :], prob[:, t % 2, h, m * P:(m + 1) * P], ident)
                last.then_inc(s["probT_mm"], 1)
                pe.wait_ge(s["probT_ready"], t + 1)
                for h in range(H):
                    for m in range(2):
                        last = pe.matmul(psO[:, h, :], lhsT=v[:, m, h * P:(h + 1) * P], rhs=probT[:, h, m, :], start=(m == 0), stop=(m == 1))
                last.then_inc(s["o_mm"], 1)
                pe.wait_ge(s["oT_ready"], t + 1)
                if t >= 1:
                    pe.wait_ge(s["y_added"], t)
                for half in range(2):
                    for h in range(H):
                        last = pe.matmul(psY[:, half, :], lhsT=oT[:, h, :], rhs=wo[:, h, half * 512:(half + 1) * 512], start=(h == 0), stop=(h == H - 1))
                last.then_inc(s["y_mm"], 1)

        @block.scalar
        def _(act):
            for t in range(NT):
                act.wait_ge(s["max_ready"], t + 1)
                if t >= 2:
                    act.wait_ge(s["probT_mm"], t - 1)
                for h in range(H):
                    last = act.activation(prob[:, t % 2, h, :], psL[:, h, :], ACT.Exp, bias=nmax[:, h:h + 1], scale=SCALE, accum_out=rsum[:, h:h + 1])
                last.then_inc(s["exp_done"], 1)
                act.wait_ge(s["probT_mm"], t + 1)
                act.activation(probT[:, :, :, :], psT[:, :, :, :], ACT.Copy).then_inc(s["probT_ready"], 1)
                act.wait_ge(s["o_mm"], t + 1)
                act.activation(oT[:, :, :], psO[:, :, :], ACT.Copy).then_inc(s["oT_ready"], 1)

        @block.vector
        def _(dve):
            order = Order(dve, s["vorder"])
            for t in range(NT):
                dve.wait_ge(s["logit_mm"], t + 1)
                order.then(dve.tensor_reduce(nmax[:, :], psL[:, :, :], AX.X, ALU.max))
                dve.tensor_scalar(nmax[:, :], nmax[:, :], -SCALE, None, ALU.mult).then_inc(s["max_ready"], 1)
                dve.wait_ge(s["exp_done"], t + 1)
                order.then(dve.reciprocal(rinv[:, :], rsum[:, :]))
                dve.tensor_tensor(prob[:, t % 2], prob[:, t % 2], bcast(rinv[:, :], 2, MEM), ALU.mult).then_inc(s["prob_ready"], 1)
                dve.wait_ge(s["y_mm"], t + 1)
                dve.tensor_tensor(x[:, t, :], x[:, t, :], psY[:, :, :].rearrange("p a n -> p (a n)"), ALU.add).then_inc(s["y_added"], 1)


def route_scores(nc, a, hT, hL, top, topi):
    NS = 2 * P_HEADS
    with ExitStack() as ctx:
        sb = lambda n, sh: ctx.enter_context(nc.sbuf_tensor(n, sh, F32))
        w, keys = sb("rs_w", [P, 2, DK, P]), sb("rs_keys", [P, NS, N_KEYS])
        wh, wl = (ctx.enter_context(nc.sbuf_tensor(f"rs_{n}", [P, 2, DK, P], F32R)) for n in ("wh", "wl"))
        qT, sc = sb("rs_qT", [P, 2, SEQ]), sb("rs_sc", [P, 2, NT, N_KEYS])
        psq = ctx.enter_context(nc.psum_tensor("rs_q", [P, 2, 1024], F32))
        pss = ctx.enter_context(nc.psum_tensor("rs_s", [P, 2, 1024], F32))
        s = ctx.enter_context(phase(nc, "route", "keys_loaded w0 w1 w_high w_low kept q_mm q_ready s_mm s_ready vorder picked"))
        block = ctx.enter_context(nc.Block())
        w_pq = a["w_pq"].rearrange("(k p) c -> p k c", p=P)

        @block.sync
        def _(sp):
            for i in range(NS):
                if i >= 2:
                    sp.wait_ge(s["w_low"], i - 1)
                sp.dma_start(w[:, i % 2], w_pq[:, :, i * P:(i + 1) * P]).then_inc(s[f"w{i % 2}"], 16)
                if i == 1:
                    sp.dma_start(keys[:, :, :], a["sub_keys"]).then_inc(s["keys_loaded"], 16)
                    sp.dma_start(a["h_high"], hT[:, :, :].bitcast(F32)).then_inc(s["kept"], 16)
                    sp.dma_start(a["h_low"], hL[:, :, :].bitcast(F32)).then_inc(s["kept"], 16)
            sp.wait_ge(s["kept"], 32)

        @block.tensor
        def _(pe):
            def scores(i):
                pe.wait_ge(s["q_ready"], i + 1)
                if i >= 2:
                    pe.wait_ge(s["s_ready"], i - 1)
                for t in range(NT):
                    last = pe.matmul(pss[:, i % 2, t * P:(t + 1) * P], lhsT=qT[:, i % 2, t * P:(t + 1) * P], rhs=keys[:, i, :], start=True, stop=True)
                last.then_inc(s["s_mm"], 1)

            for i in range(NS):
                pe.wait_ge(s["w_low"], i + 1)
                if i >= 2:
                    pe.wait_ge(s["q_ready"], i - 1)
                for half in range(2):
                    cols = slice(half * 512, (half + 1) * 512)
                    last = product(pe, psq[:, i % 2, cols], lambda k: (wh[:, i % 2, k, :], wl[:, i % 2, k, :]), lambda k: (hT[:, k, cols], hL[:, k, cols]), DK)
                last.then_inc(s["q_mm"], 1)
                if i == 0:
                    pe.wait_ge(s["keys_loaded"], 16)
                else:
                    scores(i - 1)
            scores(NS - 1)

        @block.scalar
        def _(act):
            def scores_out(i):
                act.wait_ge(s["s_mm"], i + 1)
                if i >= 2:
                    act.wait_ge(s["picked"], i - 1)
                act.activation(sc[:, i % 2].rearrange("p t k -> p (t k)"), pss[:, i % 2, :], ACT.Copy).then_inc(s["s_ready"], 1)

            def weights_high(i):
                act.wait_ge(s[f"w{i % 2}"], 16 * (i // 2 + 1))
                if i >= 2:
                    act.wait_ge(s["q_mm"], i - 1)
                act.activation(wh[:, i % 2], w[:, i % 2], ACT.Copy).then_inc(s["w_high"], 1)

            weights_high(0)
            for i in range(NS):
                if i + 1 < NS:
                    weights_high(i + 1)
                act.wait_ge(s["q_mm"], i + 1)
                if i >= 2:
                    act.wait_ge(s["s_mm"], i - 1)
                act.activation(qT[:, i % 2, :], psq[:, i % 2, :], ACT.Copy).then_inc(s["q_ready"], 1)
                if i >= 1:
                    scores_out(i - 1)
            scores_out(NS - 1)

        @block.vector
        def _(dve):
            order = Order(dve, s["vorder"])

            def weights_low(i):
                dve.wait_ge(s["w_high"], i + 1)
                dve.tensor_tensor(wl[:, i % 2], w[:, i % 2], wh[:, i % 2].bitcast(F32), ALU.subtract).then_inc(s["w_low"], 1)

            weights_low(0)
            weights_low(1)
            for i in range(NS):
                if i + 2 < NS:
                    weights_low(i + 2)
                dve.wait_ge(s["s_ready"], i + 1)
                for r in range(2):
                    part = slice(8 * r, 8 * r + 8)
                    for t in range(NT):
                        last = dve.max(top[:, t, i, part], sc[:, i % 2, t, :])
                    order.then(last)
                    for t in range(NT):
                        last = dve.max_index(topi[:, t, i, part], top[:, t, i, part], sc[:, i % 2, t, :])
                    if r == 0:
                        for t in range(NT):
                            last = dve.match_replace(sc[:, i % 2, t, :], top[:, t, i, part], sc[:, i % 2, t, :], TAKEN)
                        order.then(last)
                last.then_inc(s["picked"], 1)


def route_gates(nc, a, top, topi, consts):
    H, K, W = P_HEADS, P_TOPK, 8
    NC = K + (W - 1) * W + (K - W)
    LAST = NC - (K - W)
    T, SLOTS = 8, 4
    UNITS = P // T
    UH = UNITS // 2
    HALF = P // 2
    ident, iota, starts = consts["ident"], consts["iota"], consts["row_starts"]
    with ExitStack() as ctx:
        sb = lambda n, sh, dt=F32: ctx.enter_context(nc.sbuf_tensor(n, sh, dt))
        routeT = sb("rg_routeT", [P, 2, 3, P])
        keyf = sb("rg_keyf", [P, NT, 2 * H, K])
        cand, hot = sb("rg_cand", [P, H, NC]), sb("rg_hot", [P, 2, H * K, K])
        best, pos = sb("rg_best", [P, H, K]), sb("rg_pos", [P, H * K], U32)
        low3, posf, low3f, col = sb("rg_low3", [P, H * K], U32), sb("rg_posf", [P, H * K]), sb("rg_low3f", [P, H * K]), sb("rg_col", [P, H * K])
        colr = sb("rg_colr", [P, H * K])
        sel = sb("rg_sel", [P, 2, 3, H * K])
        gsum, ginv = sb("rg_gsum", [P, H]), sb("rg_ginv", [P, H])
        hot1, hot2 = sb("rg_hot1", [P, SLOTS, T, P]), sb("rg_hot2", [P, SLOTS, T, P])
        gates = sb("rg_gates", [P, 2, N_KEYS, HALF])
        psR = ctx.enter_context(nc.psum_tensor("rg_r", [P, 2, 512], F32))
        ps = ctx.enter_context(nc.psum_tensor("rg_ps", [P, 2, T, P], F32))
        s = ctx.enter_context(phase(nc, "gates", "vorder porder keyf_ready col_ready hot_weighed shifted exp_done sel_ready transposed route_ready hot1_made hot1_ready hot2_ready gate_mm evac stored0 stored1"))
        block = ctx.enter_context(nc.Block())
        pair = lambda z, t, half: z[:, t, half::2, :]
        hot4 = lambda half: hot[:, half].rearrange("p (h k) j -> p h k j", h=H)

        @block.vector
        def _(dve):
            order = Order(dve, s["vorder"])
            order.then(dve.tensor_copy(keyf[:, :, :, :], topi))
            rows = keyf[:, :, 0::2, :].rearrange("p t h k -> p (t h) k")
            for i in range(K - 1, 0, -1):
                last = dve.tensor_tensor(rows[:, :, i], rows[:, :, i], rows[:, :, i - 1], ALU.subtract)
                order.then(last)
            dve.sem_inc(s["keyf_ready"], 1)
            dve.sem_inc(s["gate_mm"], SLOTS)

            def choose(t):
                s1, s2 = pair(top, t, 0), pair(top, t, 1)
                dve.tensor_tensor(cand[:, :, 0:K], bcast(s1[:, :, 0], 2, K), s2, ALU.add)
                dve.tensor_tensor(cand[:, :, K:LAST].rearrange("p h (i j) -> p h i j", j=W), bcast(s1[:, :, 1:W], 3, W), bcast(s2[:, :, 0:W], 2, W - 1), ALU.add)
                order.then(dve.tensor_tensor(cand[:, :, LAST:], s1[:, :, W:], bcast(s2[:, :, 0], 2, K - W), ALU.add))
                for r in range(2):
                    part = slice(8 * r, 8 * r + 8)
                    for h in range(H):
                        last = dve.max(best[:, h, part], cand[:, h, :])
                    order.then(last)
                    yield
                    for h in range(H):
                        last = dve.max_index(pos[:, h * K + 8 * r:h * K + 8 * r + 8], best[:, h, part], cand[:, h, :])
                    if r == 0:
                        for h in range(H):
                            last = dve.match_replace(cand[:, h, :], best[:, h, part], cand[:, h, :], TAKEN)
                    order.then(last)
                    yield
                if t >= 2:
                    dve.wait_ge(s["transposed"], t - 1)
                gate = sel[:, t % 2, 2, :].rearrange("p (h k) -> p h k", h=H)
                dve.tensor_tensor(gate, best[:, :, :], bcast(best[:, :, 0], 2, K), ALU.subtract).then_inc(s["shifted"], 1)
                dve.tensor_copy(posf[:, :], pos[:, :])
                order.then(dve.tensor_scalar(low3[:, :], pos[:, :], W - 1, None, ALU.bitwise_and))
                order.then(dve.tensor_copy(low3f[:, :], low3[:, :]))
                dve.scalar_tensor_tensor(colr[:, :], posf[:, :], float(K), posf[:, :], ALU.is_lt, ALU.mult)
                order.then(dve.scalar_tensor_tensor(low3f[:, :], posf[:, :], float(K), low3f[:, :], ALU.is_ge, ALU.mult))
                order.then(dve.scalar_tensor_tensor(low3f[:, :], posf[:, :], float(LAST), low3f[:, :], ALU.is_lt, ALU.mult))
                if t >= 1:
                    dve.wait_ge(s["hot_weighed"], t)
                dve.tensor_tensor(col[:, :], colr[:, :], low3f[:, :], ALU.add).then_inc(s["col_ready"], 1)
                yield
                order.then(dve.tensor_tensor(hot[:, 0], bcast(posf[:, :], 2, K), bcast(starts, 1, H * K), ALU.is_ge))
                yield
                order.then(dve.tensor_tensor(hot4(0), hot4(0), bcast(pair(keyf, t, 0), 2, K), ALU.mult))
                yield
                dve.tensor_reduce(sel[:, t % 2, 0, :], hot[:, 0], AX.X, ALU.add)
                yield
                dve.wait_ge(s["exp_done"], t + 1)
                order.then(dve.tensor_reduce(gsum[:, :], gate, AX.X, ALU.add))
                order.then(dve.reciprocal(ginv[:, :], gsum[:, :]))
                order.then(dve.tensor_tensor(gate, gate, bcast(ginv[:, :], 2, K), ALU.mult))
                yield
                dve.wait_ge(s["hot_weighed"], t + 1)
                dve.tensor_reduce(sel[:, t % 2, 1, :], hot[:, 1], AX.X, ALU.add).then_inc(s["sel_ready"], 1)
                dve.wait_ge(s["sel_ready"], t + 1)

            def one_hots(t):
                for m in range(UNITS):
                    dve.wait_ge(s["gate_mm"], t * UNITS + m + 1)
                    for c, hot_, ready in ((0, hot1, "hot1_made"), (1, hot2, "hot2_ready")):
                        key = routeT[:, t % 2, c, m * T:(m + 1) * T]
                        dve.tensor_tensor(hot_[:, m % SLOTS], bcast(iota, 1, T), bcast(key, 2, P), ALU.is_equal).then_inc(s[ready], 1)
                    yield

            for _ in choose(0):
                pass
            for t in range(NT):
                dve.wait_ge(s["route_ready"], t + 1)
                later = choose(t + 1) if t + 1 < NT else iter(())
                for _ in one_hots(t):
                    next(later, None)
                assert next(later, None) is None and next(later, "done") == "done"

        @block.gpsimd
        def _(pool):
            order = Order(pool, s["porder"])

            def second_keys(t):
                pool.wait_ge(s["col_ready"], t + 1)
                if t >= 1:
                    pool.wait_ge(s["sel_ready"], t)
                order.then(pool.tensor_tensor(hot[:, 1], bcast(col[:, :], 2, K), bcast(iota[:, 0:K], 1, H * K), ALU.subtract))
                order.then(pool.tensor_scalar(hot[:, 1], hot[:, 1], 0.0, None, ALU.is_equal))
                pool.tensor_tensor(hot4(1), hot4(1), bcast(pair(keyf, t, 1), 2, K), ALU.mult).then_inc(s["hot_weighed"], 1)

            pool.wait_ge(s["keyf_ready"], 1)
            for t in range(NT):
                second_keys(t)

        @block.tensor
        def _(pe):
            def transposes(t):
                pe.wait_ge(s["sel_ready"], t + 1)
                if t >= 2:
                    pe.wait_ge(s["route_ready"], t - 1)
                for i in range(3):
                    last = pe.transpose(psR[:, t % 2, i * P:(i + 1) * P], sel[:, t % 2, i, :], ident)
                last.then_inc(s["transposed"], 1)

            pe.sem_inc(s["evac"], 2)
            def units(t, g):
                for u in range(SLOTS):
                    n = g * SLOTS + (t * UNITS + u + 1)
                    pe.wait_ge(s["hot1_ready"], n)
                    pe.wait_ge(s["hot2_ready"], n)
                    pe.wait_ge(s["evac"], n)
                    for j in range(T):
                        last = pe.matmul(ps[:, u % 2, j, :], lhsT=hot2[:, u, j, :], rhs=hot1[:, u, j, :], start=True, stop=True)
                    last.then_inc(s["gate_mm"], 1)

            transposes(0)
            for t in range(NT):
                with pe.Fori(0, UNITS // SLOTS - 1) as g:
                    units(t, g)
                if t + 1 < NT:
                    transposes(t + 1)
                units(t, UNITS // SLOTS - 1)

        @block.scalar
        def _(act):
            def exps(t):
                act.wait_ge(s["shifted"], t + 1)
                act.activation(sel[:, t % 2, 2, :], sel[:, t % 2, 2, :], ACT.Exp).then_inc(s["exp_done"], 1)

            def routes(t):
                act.wait_ge(s["transposed"], t + 1)
                if t >= 2:
                    act.wait_ge(s["gate_mm"], SLOTS + (t - 1) * UNITS)
                act.activation(routeT[:, t % 2], psR[:, t % 2, 0:3 * P].rearrange("p (a n) -> p a n", a=3), ACT.Copy).then_inc(s["route_ready"], 1)

            def scale(t, m):
                act.wait_ge(s["hot1_made"], m + (t * UNITS + 1))
                for j in range(T):
                    rows = hot1[:, bass.ds(m % SLOTS, 1), j, :].rearrange("p a k -> p (a k)") if not isinstance(m, int) else hot1[:, m % SLOTS, j, :]
                    last = act.activation(rows, rows, ACT.Copy, scale=routeT[:, t % 2, 2, bass.ds(m * T + j, 1)])
                last.then_inc(s["hot1_ready"], 1)

            def leave(t, p, m, slot):
                act.wait_ge(s["gate_mm"], m + (SLOTS + (2 * t + p) * UH + 1))
                act.activation(gates[:, p, :, bass.ds(m * T, T)], ps[:, slot].rearrange("j n i -> j i n"), ACT.Copy).then_inc(s["evac"], 1)

            for p in range(2):
                act.sem_inc(s[f"stored{p}"], 16)
            exps(0)
            routes(0)
            for t in range(NT):
                for p in range(2):
                    if p == 0 and t >= 1:
                        leave(t - 1, 1, UH - 1, 1)
                    scale(t, p * UH)
                    if p == 1 and t + 1 < NT:
                        exps(t + 1)
                    if p == 1:
                        leave(t, 0, UH - 1, 1)
                    act.wait_ge(s[f"stored{p}"], t * 16 + 16)
                    for m in range(1, UH):
                        scale(t, p * UH + m)
                        leave(t, p, m - 1, (m - 1) % 2)
                        if p == 1 and m == UH - 2 and t + 1 < NT:
                            routes(t + 1)
            leave(NT - 1, 1, UH - 1, 1)

        @block.sync
        def _(sp):
            for t in range(NT):
                for p in range(2):
                    sp.wait_ge(s["evac"], (2 * t + p + 1) * UH + 2)
                    sp.dma_start(a["gates"][2 * t + p], gates[:, p]).then_inc(s[f"stored{p}"], 16)
            for p in range(2):
                sp.wait_ge(s[f"stored{p}"], 16 * (NT + 1))


def experts(nc, a, x):
    G = 2
    NG = N_KEYS // G
    NY = 2 * NT // G
    with ExitStack() as ctx:
        sb = lambda n, sh, dt=F32: ctx.enter_context(nc.sbuf_tensor(n, sh, dt))
        hh, hl = sb("ex_hh", [P, DK, SEQ], F32R), sb("ex_hl", [P, DK, SEQ], F32R)
        u_sb, v_sb, g_sb = sb("ex_u", [P, DK, P]), sb("ex_v", [P, D_MODEL]), sb("ex_g", [P, SEQ])
        act_sb = sb("ex_act", [P, SEQ])
        uh, ul = sb("ex_uh", [P, 2, DK, P], F32R), sb("ex_ul", [P, 2, DK, P], F32R)
        vh, vl = sb("ex_vh", [P, 2, G, D_MODEL], F32R), sb("ex_vl", [P, 2, G, D_MODEL], F32R)
        wh, wl = sb("ex_wh", [P, 2, G, SEQ], F32R), sb("ex_wl", [P, 2, G, SEQ], F32R)
        psA = ctx.enter_context(nc.psum_tensor("ex_a", [P, 2, 1024], F32))
        psY = ctx.enter_context(nc.psum_tensor("ex_y", [P, 4, 512], F32))
        s = ctx.enter_context(phase(nc, "experts", "h_loaded u_loaded v_loaded g_loaded u_high u_low v_high v_low act_mm gelu_done weighed w_high w_low y_mm y_added"))
        block = ctx.enter_context(nc.Block())

        def chunks(eng, slot):
            for n in range(4):
                slot(n, n)
            with eng.Fori(1, N_KEYS // 4 - 1) as i:
                for j in range(4):
                    slot(i * 4 + j, j)
            for n in range(N_KEYS - 4, N_KEYS):
                slot(n, n % 4)

        def groups_second_done(eng, n, j, back):
            wait(eng, s["y_mm"], (n - j % 2) * NY - (back - 1) * G * NY)

        @block.sync
        def _(sp):
            sp.dma_start(hh[:, :, :].bitcast(F32), a["h_high"]).then_inc(s["h_loaded"], 16)
            sp.dma_start(hl[:, :, :].bitcast(F32), a["h_low"]).then_inc(s["h_loaded"], 16)

            def loads(n, j):
                wait(sp, s["u_low"], n)
                sp.dma_start(u_sb[:, :, :], a["u_emb"][bass.ds(n, 1)].rearrange("a p k e -> p (a k) e")).then_inc(s["u_loaded"], 16)
                wait(sp, s["v_low"], n)
                sp.dma_start(v_sb[:, :], a["v_emb"][bass.ds(n, 1)].rearrange("a e d -> e (a d)")).then_inc(s["v_loaded"], 16)
                wait(sp, s["weighed"], n)
                sp.dma_start(g_sb[:, :].rearrange("j (b n) -> j b n", n=P // 2), a["gates"][:, :, bass.ds(n, 1), :].rearrange("b j a n -> j (b a) n")).then_inc(s["g_loaded"], 16)

            chunks(sp, loads)

        @block.tensor
        def _(pe):
            def first(n, j):
                pe.wait_ge(s["u_low"], n + 1)
                wait(pe, s["gelu_done"], n - 1)
                for half in range(2):
                    cols = slice(half * 512, (half + 1) * 512)
                    last = product(pe, psA[:, j % 2, cols], lambda k: (uh[:, j % 2, k, :], ul[:, j % 2, k, :]), lambda k: (hh[:, k, cols], hl[:, k, cols]), DK)
                last.then_inc(s["act_mm"], 1)

            def second(n, j):
                q, p = j % 2, 1 - j // 2
                if q == 0:
                    pe.wait_ge(s["v_low"], n)
                    pe.wait_ge(s["w_low"], n)
                for y in range(NY):
                    t, half = (q * NY + y) // 2, y % 2
                    toks, cols = slice(t * P, (t + 1) * P), slice(half * 512, (half + 1) * 512)
                    wait(pe, s["y_added"], (n - G) * NY + y - 3)
                    product(pe, psY[:, y % 4, :], lambda c: (wh[:, p, c, toks], wl[:, p, c, toks]), lambda c: (vh[:, p, c, cols], vl[:, p, c, cols]), G).then_inc(s["y_mm"], 1)

            def slot(n, j):
                first(n, j)
                if not isinstance(n, int) or n >= G:
                    second(n, j)

            pe.wait_ge(s["h_loaded"], 32)
            chunks(pe, slot)
            for n in range(N_KEYS, N_KEYS + G):
                second(n, n % 4)

        @block.scalar
        def _(act):
            def u_high(n, j):
                act.wait_ge(s["u_loaded"], n * 16 + 16)
                wait(act, s["act_mm"], n - 1)
                act.activation(uh[:, j % 2], u_sb[:, :, :], ACT.Copy).then_inc(s["u_high"], 1)

            def slot(n, j):
                if not (isinstance(n, int) and n == N_KEYS - 1):
                    u_high(n + 1, (j + 1) % 4)
                act.wait_ge(s["v_loaded"], n * 16 + 16)
                groups_second_done(act, n, j, 2)
                act.activation(vh[:, j // 2, j % 2, :], v_sb[:, :], ACT.Copy).then_inc(s["v_high"], 1)
                act.wait_ge(s["act_mm"], n + 1)
                wait(act, s["w_low"], n)
                act.activation(act_sb[:, :], psA[:, j % 2, :], ACT.Gelu).then_inc(s["gelu_done"], 1)
                act.wait_ge(s["weighed"], n + 1)
                act.activation(wh[:, j // 2, j % 2, :], act_sb[:, :], ACT.Copy).then_inc(s["w_high"], 1)

            u_high(0, 0)
            chunks(act, slot)

        @block.vector
        def _(dve):
            def low(out, whole, high):
                return dve.tensor_tensor(out, whole, high.bitcast(F32), ALU.subtract)

            def u_low(n, j):
                dve.wait_ge(s["u_high"], n + 1)
                low(ul[:, j % 2], u_sb[:, :, :], uh[:, j % 2]).then_inc(s["u_low"], 1)

            def add(n, j):
                for y in range(NY):
                    t, half = ((j % 2) * NY + y) // 2, y % 2
                    xr = x[:, t, half * 512:(half + 1) * 512]
                    dve.wait_ge(s["y_mm"], (n - G) * NY + y + 1)
                    dve.tensor_tensor(xr, xr, psY[:, y % 4, :], ALU.add).then_inc(s["y_added"], 1)

            def slot(n, j):
                if not (isinstance(n, int) and n == N_KEYS - 1):
                    u_low(n + 1, (j + 1) % 4)
                dve.wait_ge(s["v_high"], n + 1)
                low(vl[:, j // 2, j % 2, :], v_sb[:, :], vh[:, j // 2, j % 2, :]).then_inc(s["v_low"], 1)
                dve.wait_ge(s["gelu_done"], n + 1)
                dve.wait_ge(s["g_loaded"], n * 16 + 16)
                dve.tensor_tensor(act_sb[:, :], act_sb[:, :], g_sb[:, :], ALU.mult).then_inc(s["weighed"], 1)
                dve.wait_ge(s["w_high"], n + 1)
                low(wl[:, j // 2, j % 2, :], act_sb[:, :], wh[:, j // 2, j % 2, :]).then_inc(s["w_low"], 1)
                if not isinstance(n, int) or n >= G:
                    add(n, j)

            u_low(0, 0)
            chunks(dve, slot)
            for n in range(N_KEYS, N_KEYS + G):
                add(n, n % 4)


def final_norm(nc, a, x, out):
    with ExitStack() as ctx:
        sb = lambda n, sh: ctx.enter_context(nc.sbuf_tensor(n, sh, F32))
        gain, junk, y = sb("fn_gain", [P, D_MODEL]), sb("fn_junk", [P, 2, D_MODEL]), sb("fn_y", [P, NT, D_MODEL])
        ssq, root, rinv, epst = sb("fn_ssq", [P, NT]), sb("fn_root", [P, NT]), sb("fn_rinv", [P, NT]), sb("fn_eps", [P, 1])
        s = ctx.enter_context(phase(nc, "final", "gain_loaded eps_ready squared rooted inverted y_ready stored"))
        block = ctx.enter_context(nc.Block())

        @block.sync
        def _(sp):
            sp.dma_start(gain[:, :], a["g_final"].partition_broadcast(P)).then_inc(s["gain_loaded"], 16)
            for t in range(NT):
                sp.wait_ge(s["y_ready"], t + 1)
                sp.dma_start(out[t * P:(t + 1) * P, :], y[:, t, :]).then_inc(s["stored"], 16)
            sp.wait_ge(s["stored"], 16 * NT)

        @block.scalar
        def _(act):
            for t in range(NT):
                if t >= 2:
                    act.wait_ge(s["squared"], t - 1)
                act.activation(junk[:, t % 2, :], x[:, t, :], ACT.Square, accum_out=ssq[:, t:t + 1]).then_inc(s["squared"], 1)
            act.wait_ge(s["squared"], NT)
            act.wait_ge(s["eps_ready"], 1)
            act.activation(root[:, :], ssq[:, :], ACT.Sqrt, bias=epst[:, :], scale=1.0 / D_MODEL).then_inc(s["rooted"], 1)

        @block.vector
        def _(dve):
            dve.memset(epst[:, :], EPS).then_inc(s["eps_ready"], 1)
            dve.wait_ge(s["gain_loaded"], 16)
            dve.wait_ge(s["rooted"], 1)
            dve.reciprocal(rinv[:, :], root[:, :]).then_inc(s["inverted"], 1)
            dve.wait_ge(s["inverted"], 1)
            for t in range(NT):
                dve.scalar_tensor_tensor(y[:, t, :], x[:, t, :], rinv[:, t:t + 1], gain[:, :], ALU.mult, ALU.mult).then_inc(s["y_ready"], 1)


CONSTANTS = ("ident", "flip", "ones", "relhot", "iota", "row_starts")
DELTA_CONSTANTS = ("tri", "dmask", "strict", "lev", "levT")
GAINS = {"g_mix": DK, "g_cross": DK, "g_mem": DK, "g_ffn": DK, "g_lat": 5}


def hybrid_block(nc, a, out, probe=None):
    probe = probe or (lambda *args: None)
    whole = lambda t: t[tuple(slice(None) for _ in t.shape)]
    with ExitStack() as ctx:
        def sb(stack, name, shape, dt=F32):
            return stack.enter_context(nc.sbuf_tensor(name, shape, dt))

        small = {n: sb(ctx, f"c_{n}", list(a[f"c_{n}"].shape)) for n in CONSTANTS}
        small |= {n: sb(ctx, f"s_{n}", [P, w]) for n, w in GAINS.items()}
        load_all(nc, "constants", [(whole(t), a[f"c_{n}" if n in CONSTANTS else n]) for n, t in small.items()])
        consts = {n: whole(t) for n, t in small.items()}
        ident = consts["ident"]
        stream = sb(ctx, "stream", [P, NT, D_MODEL])
        front = ctx.enter_context(ExitStack())
        wide = sb(front, "wide", [P, DK, SEQ])
        gain = lambda n: small[n]

        norm_transposed(nc, "norm_mix", wide, a["x"], gain("g_mix"), ident, stream, NT)
        with ExitStack() as mixer:
            proj = sb(mixer, "proj", [P, NT, N_COLS])
            with ExitStack() as sub:
                nat = sb(sub, "nat", [P, NT, 3 * B_QK])
                project(nc, a, stream, nat, proj, ident)
                delta = {n: sb(sub, f"c_{n}", list(a[f"c_{n}"].shape)) for n in DELTA_CONSTANTS}
                load_all(nc, "delta_constants", [(whole(t), a[f"c_{n}"]) for n, t in delta.items()])
                delta_net(nc, a, proj, nat, wide, stream, consts | {n: whole(t) for n, t in delta.items()})
            idxT, qiT = sb(mixer, "idxT", [P, SEQ]), sb(mixer, "qiT", [P, 4, SEQ])
            v, widx, near = sb(mixer, "v", [P, NT, 512]), sb(mixer, "widx", [P, NT, IDX_HEADS]), sb(mixer, "near", [P, A_HEADS, NEAR])
            qT, kT = stream[:, 0:4, :], stream[:, 4:8, :]
            sparse_prepare(nc, a, proj, small["g_lat"], consts, idxT[:, :], qiT, qT, kT, v, widx[:, :, :], near[:, :, :])
            sparse_attention(nc, idxT[:, :], qiT, qT, kT, v, widx, near, wide, ident)
        probe("mix", wide)
        mix_out(nc, a, wide, stream, ident)
        probe("x1", stream)

        with ExitStack() as cross:
            memT = sb(cross, "memT", [P, DK, MEM])
            xqT, xkT, xv = sb(cross, "xqT", [P, X_HEADS, SEQ]), sb(cross, "xkT", [P, X_HEADS, MEM]), sb(cross, "xv", [P, MEM // P, 512])
            norm_transposed(nc, "norm_cross", stream, None, gain("g_cross"), ident, wide, NT)
            with nc.sbuf_tensor("mem_in", [P, MEM // P, D_MODEL], F32) as mem_in:
                norm_transposed(nc, "norm_mem", mem_in, a["mem"], gain("g_mem"), ident, memT, MEM // P)
            cross_project(nc, a, wide, memT, xqT, xkT, xv)
            cross_attend(nc, a, xqT, xkT, xv, stream, ident)
        probe("x2", stream)

        front.close()
        with ExitStack() as route:
            top = sb(route, "top", [P, NT, 2 * P_HEADS, P_TOPK])
            topi = sb(route, "topi", [P, NT, 2 * P_HEADS, P_TOPK], U32)
            with ExitStack() as normed:
                hT, hL = sb(normed, "hT", [P, DK, SEQ], F32R), sb(normed, "hL", [P, DK, SEQ], F32R)
                norm_transposed(nc, "norm_ffn", stream, None, gain("g_ffn"), ident, hT, NT, hL)
                route_scores(nc, a, hT, hL, top, topi)
            route_gates(nc, a, top, topi[:, :, :, :], consts)
        experts(nc, a, stream)
        final_norm(nc, a, stream, out)


def kernel(**inputs):
    import concourse.bacc as bacc
    from concourse.bass_utils import run_bass_kernel_spmd

    g = {n: np.asarray(v) for n, v in inputs.items()}
    column = lambda v: v.reshape(-1, P).T
    arrays = {
        "x": g["x"][0], "mem": g["mem"][0], "w_in": g["w_in"][0],
        "g_mix": column(g["g_mix"][0]), "g_cross": column(g["g_cross"][0]), "g_mem": column(g["g_mem"][0]), "g_ffn": column(g["g_ffn"][0]),
        "g_lat": np.stack([*g["g_cq"][0].reshape(2, P), *g["g_ckv"][0].reshape(2, P), np.tile(g["g_kidx"][0], 2)], 1),
        "w_uq": g["w_uq"][0].reshape(A_LORA, 512), "w_iq": g["w_iq"][0].reshape(A_LORA, 512),
        "w_uk": g["w_uk"][0].reshape(A_LORA, 512), "w_uv": g["w_uv"][0].reshape(A_LORA, 512),
        "rel_bias": g["rel_bias"],
        "conv_w": g["conv_w"][0].reshape(CONV, 3 * B_QK // P, P).transpose(2, 1, 0),
        "A_log": g["A_log"][0], "dt_bias": g["dt_bias"][0], "g_onorm": g["g_onorm"][0], "w_out": g["w_out"][0],
        "wq_x": g["wq_x"][0].reshape(D_MODEL, 512), "wk_x": g["wk_x"][0].reshape(D_MODEL, 512), "wv_x": g["wv_x"][0].reshape(D_MODEL, 512),
        "wo_x": g["wo_x"][0].reshape(512, D_MODEL),
        "w_pq": g["w_pq"][0].reshape(D_MODEL, 2 * P_HEADS * P),
        "sub_keys": g["sub_keys"][0].reshape(2 * P_HEADS, N_KEYS, P).transpose(2, 0, 1),
        "u_emb": g["u_emb"][0].reshape(N_KEYS, P, DK, P).transpose(0, 3, 2, 1),
        "v_emb": g["v_emb"][0].reshape(N_KEYS, P, D_MODEL),
        "g_final": g["g_final"],
    } | {f"c_{n}": v for n, v in shape_constants().items()}
    arrays = {n: np.ascontiguousarray(v) for n, v in arrays.items()}

    nc = bacc.Bacc("TRN2", target_bir_lowering=False, num_devices=1)
    a = {n: nc.dram_tensor(f"in_{n}", v.shape, F32, kind="ExternalInput").ap() for n, v in arrays.items()}
    a["bias_rows"] = nc.dram_tensor("bias_rows", (A_HEADS, NREL), F32).ap()
    a["h_high"] = nc.dram_tensor("h_high", (P, DK, SEQ), F32).ap()
    a["h_low"] = nc.dram_tensor("h_low", (P, DK, SEQ), F32).ap()
    a["gates"] = nc.dram_tensor("gates", (2 * NT, P, N_KEYS, P // 2), F32).ap()
    out = nc.dram_tensor("out_x", (SEQ, D_MODEL), F32, kind="ExternalOutput").ap()
    hybrid_block(nc, a, out)
    r = run_bass_kernel_spmd(nc, [{f"in_{n}": v for n, v in arrays.items()}], core_ids=[0])
    return r.results[0]["out_x"].reshape(1, SEQ, D_MODEL)
```

```python
from contextlib import ExitStack, contextmanager
import math

import numpy as np
import concourse.bass as bass
from concourse import mybir

P = 128
D_MODEL, SEQ = 1024, 1024
NT = SEQ // P
DK = D_MODEL // P
CHUNK = 64
EPS = 1e-6
A_HEADS, A_DIM, A_LORA = 8, 64, 256
IDX_HEADS, IDX_DIM, TOPK = 8, 64, 256
B_HEADS, B_DIM = 4, 128
B_QK = B_HEADS * B_DIM
CONV = 4
MEM, X_HEADS, X_DIM = 256, 4, 128
P_HEADS, N_KEYS, P_TOPK = 8, 128, 16
REL_BUCKETS, REL_MAX_DIST = 32, 128
NEAR = 2 * P
NREL = 3 * P
COL_IDX = 2 * A_LORA
COL_QKV = COL_IDX + IDX_DIM + IDX_HEADS
COL_Z = COL_QKV + 3 * B_QK
COL_AB = COL_Z + B_QK
IN_COLS = COL_AB + 2 * B_HEADS
N_IDX = COL_IDX
N_A = N_IDX + IDX_DIM + IDX_HEADS
N_B = N_A + B_HEADS
N_COLS = N_B + B_HEADS
MASKED = -1e30
TAKEN = -3e38
INADMISSIBLE = -2e30

F32 = mybir.dt.float32
U32 = mybir.dt.uint32
F32R = mybir.dt.float32r
ALU = mybir.AluOpType
ACT = mybir.ActivationFunctionType
AX = mybir.AxisListType


@contextmanager
def phase(nc, name, signals):
    sems = {n: nc.alloc_semaphore(f"{name}_{n}") for n in signals.split()}
    yield sems
    nc.clear_and_free_semaphores(list(sems.values()))
    nc.all_engine_barrier()


class Order:

    def __init__(self, eng, sem, base=0):
        self.eng, self.sem, self.base, self.n = eng, sem, base, 0

    def then(self, ins):
        self.n += 1
        ins.then_inc(self.sem, 1)
        self.eng.wait_ge(self.sem, self.base + self.n)


def bcast(ap, axis, n):
    shape = list(ap.shape)
    shape.insert(axis, n)
    return ap.unsqueeze(axis).to_broadcast(shape)


def wait(eng, sem, value):
    if not isinstance(value, int) or value > 0:
        eng.wait_ge(sem, value)


def product(pe, out, lhsT, rhs, chunks):
    for k in range(chunks):
        (lh, ll), (rh, rl) = lhsT(k), rhs(k)
        pe.matmul(out, lhsT=lh, rhs=rh, start=(k == 0), stop=False)
        pe.matmul(out, lhsT=lh, rhs=rl, start=False, stop=False)
        last = pe.matmul(out, lhsT=ll, rhs=rh, start=False, stop=(k == chunks - 1))
    return last


def load_all(nc, name, pairs):
    with phase(nc, name, "loaded") as s, nc.Block() as block:
        @block.sync
        def _(sp):
            for dst, src in pairs:
                sp.dma_start(dst, src).then_inc(s["loaded"], 16)
            sp.wait_ge(s["loaded"], 16 * len(pairs))


def norm_transposed(nc, name, src, dram, gain, ident, outT, tiles, outL=None):
    with ExitStack() as ctx:
        sb = lambda n, sh: ctx.enter_context(nc.sbuf_tensor(f"{name}_{n}", sh, F32))
        ps = ctx.enter_context(nc.psum_tensor(f"{name}_ps", [P, 4, 512], F32))
        normed = sb("normed", [P, tiles, D_MODEL])
        junk = sb("junk", [P, 2, D_MODEL])
        ssq = sb("ssq", [P, tiles])
        root = sb("root", [P, tiles])
        rinv = sb("rinv", [P, tiles])
        epst = sb("eps", [P, 1])
        per = min(4, tiles)
        groups = tiles // per
        s = ctx.enter_context(phase(nc, name, "eps_ready squared rooted inverted scaled transposed evac_v evac_s " + " ".join(f"src{t}" for t in range(tiles))))
        block = ctx.enter_context(nc.Block())

        @block.sync
        def _(sp):
            if dram is not None:
                for t in range(tiles):
                    sp.dma_start(src[:, t, :], dram[t * P:(t + 1) * P, :]).then_inc(s[f"src{t}"], 16)

        @block.scalar
        def _(act):
            for t in range(tiles):
                if dram is not None:
                    act.wait_ge(s[f"src{t}"], 16)
                if t >= 2:
                    act.wait_ge(s["squared"], t - 1)
                act.activation(junk[:, t % 2, :], src[:, t, :], ACT.Square, accum_out=ssq[:, t:t + 1]).then_inc(s["squared"], 1)
            act.wait_ge(s["squared"], tiles)
            act.wait_ge(s["eps_ready"], 1)
            act.activation(root[:, :], ssq[:, :], ACT.Sqrt, bias=epst[:, :], scale=1.0 / D_MODEL).then_inc(s["rooted"], 1)
            for b in range(0 if outL else 1, groups * DK, 1 if outL else 2):
                k, g = b // groups, b % groups
                act.wait_ge(s["transposed"], b + 1)
                act.activation(outT[:, k, g * per * P:(g + 1) * per * P], ps[:, b % 4, 0:per * P], ACT.Copy, scale=gain[:, k:k + 1]).then_inc(s["evac_s"], 1)

        @block.vector
        def _(dve):
            dve.memset(epst[:, :], EPS).then_inc(s["eps_ready"], 1)
            dve.wait_ge(s["rooted"], 1)
            dve.reciprocal(rinv[:, :], root[:, :]).then_inc(s["inverted"], 1)
            dve.wait_ge(s["inverted"], 1)
            for t in range(tiles):
                dve.tensor_scalar(normed[:, t, :], src[:, t, :], rinv[:, t:t + 1], None, ALU.mult).then_inc(s["scaled"], 1)
            if outL:
                for b in range(groups * DK):
                    k, g = b // groups, b % groups
                    cols = slice(g * per * P, (g + 1) * per * P)
                    dve.wait_ge(s["evac_s"], b + 1)
                    dve.scalar_tensor_tensor(outL[:, k, cols], ps[:, b % 4, 0:per * P], gain[:, k:k + 1], outT[:, k, cols].bitcast(F32), ALU.mult, ALU.subtract).then_inc(s["evac_v"], 1)
                return
            for b in range(0, groups * DK, 2):
                k, g = b // groups, b % groups
                dve.wait_ge(s["transposed"], b + 1)
                dve.tensor_scalar(outT[:, k, g * per * P:(g + 1) * per * P], ps[:, b % 4, 0:per * P], gain[:, k:k + 1], None, ALU.mult).then_inc(s["evac_v"], 1)

        @block.tensor
        def _(pe):
            for b in range(groups * DK):
                k, g = b // groups, b % groups
                pe.wait_ge(s["scaled"], (g + 1) * per)
                if b >= 4:
                    if outL:
                        pe.wait_ge(s["evac_v"], b - 3)
                    else:
                        pe.wait_ge(s["evac_s"] if b % 2 else s["evac_v"], (b - 4) // 2 + 1)
                for j in range(per):
                    last = pe.transpose(ps[:, b % 4, j * P:(j + 1) * P], normed[:, g * per + j, k * P:(k + 1) * P], ident)
                last.then_inc(s["transposed"], 1)


def project(nc, a, hT, hL, lat, ident):
    w_in = a["w_in"].rearrange("(k p) c -> p k c", p=P)
    chunks = 3 * B_QK // P
    pieces = [(c, c, 256) for c in (0, 256)] + [(COL_IDX, N_IDX, 80)] + [(COL_Z + c, None, 256) for c in (0, 256)]
    with ExitStack() as ctx:
        sb = lambda n, sh, dt=F32: ctx.enter_context(nc.sbuf_tensor(n, sh, dt))
        wt = sb("pj_wt", [P, 2, DK, 256])
        wth, wtl = ([sb(f"pj_{n}{i}", [P, DK, 256], F32R) for i in range(2)] for n in ("wth", "wtl"))
        wc, wch, wcl = sb("pj_wc", [P, DK, P]), sb("pj_wch", [P, 2, DK, P], F32R), sb("pj_wcl", [P, 2, DK, P], F32R)
        raw = sb("pj_raw", [P, 2, CONV - 1 + SEQ])
        conv = sb("pj_conv", [P, 2, SEQ])
        square = sb("pj_square", [P, NT, P])
        stage = sb("pj_stage", [P, 2, NT, P])
        zstage = sb("pj_zstage", [P, 4, 256])
        ssq, root, rinv = sb("pj_ssq", [P, NT]), sb("pj_root", [P, NT]), sb("pj_rinv", [P, NT])
        cw, epst = sb("pj_cw", [P, chunks, CONV]), sb("pj_eps", [P, 1])
        psn = ctx.enter_context(nc.psum_tensor("pj_psn", [P, 4, 512], F32))
        pst = ctx.enter_context(nc.psum_tensor("pj_pst", [P, 2, 1024], F32))
        s = ctx.enter_context(phase(nc, "project", "cw_loaded wc_loaded wt_loaded0 wt_loaded1 wc_high wc_low wt_high wt_low padded chunk_done raw_ready conv_step conv_done silu_done nat_done squared summed rooted stage_ready stored0 stored1 tok_done tok_evac zstored0 zstored1 zstored2 zstored3"))
        block = ctx.enter_context(nc.Block())
        normed = 2 * B_QK // P

        @block.sync
        def _(sp):
            sp.dma_start(cw[:, :, :], a["conv_w"]).then_inc(s["cw_loaded"], 16)
            for c in range(chunks):
                wait(sp, s["wc_low"], c)
                sp.dma_start(wc[:, :, :], w_in[:, :, COL_QKV + c * P:COL_QKV + (c + 1) * P]).then_inc(s["wc_loaded"], 16)
            for i, (col, to, width) in enumerate(pieces):
                wait(sp, s["wt_low"], i - 1)
                if width == 256:
                    for half in (slice(0, DK // 2), slice(DK // 2, DK)):
                        sp.dma_start(wt[:, i % 2, half, :], w_in[:, half, col:col + width]).then_inc(s[f"wt_loaded{i % 2}"], 16)
                else:
                    sp.dma_start(wt[:, i % 2, :, 0:72], w_in[:, :, COL_IDX:COL_QKV]).then_inc(s[f"wt_loaded{i % 2}"], 16)
                    sp.dma_start(wt[:, i % 2, :, 72:80], w_in[:, :, COL_AB:IN_COLS]).then_inc(s[f"wt_loaded{i % 2}"], 16)

        @block.gpsimd
        def _(pool):
            for c in range(chunks):
                pool.wait_ge(s["stage_ready"], c + 1)
                pool.dma_start(a["nat"][:, :, c * P:(c + 1) * P].rearrange("t p n -> p t n"), stage[:, c % 2]).then_inc(s[f"stored{c % 2}"], 16)
            n = 0
            for i, (col, to, width) in enumerate(pieces):
                for t in range(NT):
                    n += 1
                    if to is None:
                        z = (i - 3) * NT + t
                        pool.wait_ge(s["tok_evac"], n)
                        pool.dma_start(a["silu_z"][t, :, (i - 3) * 256:(i - 2) * 256], zstage[:, z % 4, :]).then_inc(s[f"zstored{z % 4}"], 16)
            for p in range(2):
                pool.wait_ge(s[f"stored{p}"], 16 * chunks // 2)
            for p in range(4):
                pool.wait_ge(s[f"zstored{p}"], 16 * 4)

        @block.tensor
        def _(pe):
            def to_token_major(c):
                pe.wait_ge(s["silu_done"], c + 1)
                if c >= 2:
                    pe.wait_ge(s["stage_ready"], c - 1)
                for t in range(NT):
                    last = pe.transpose(pst[:, c % 2, t * P:(t + 1) * P], conv[:, c % 2, t * P:(t + 1) * P], ident)
                last.then_inc(s["nat_done"], 1)

            for c in range(chunks):
                pe.wait_ge(s["wc_low"], c + 1)
                if c >= 2:
                    pe.wait_ge(s["raw_ready"], c - 1)
                for half in range(2):
                    cols = slice(half * 512, (half + 1) * 512)
                    last = product(pe, psn[:, 2 * (c % 2) + half, :], lambda k: (wch[:, c % 2, k, :], wcl[:, c % 2, k, :]), lambda k: (hT[:, k, cols], hL[:, k, cols]), DK)
                last.then_inc(s["chunk_done"], 1)
                if c >= 1:
                    to_token_major(c - 1)
            to_token_major(chunks - 1)
            pe.wait_ge(s["raw_ready"], chunks)
            n = 0
            for i, (col, to, width) in enumerate(pieces):
                pe.wait_ge(s["wt_low"], i + 1)
                for t in range(NT):
                    if n >= 4:
                        pe.wait_ge(s["tok_evac"], n - 3)
                    toks = slice(t * P, (t + 1) * P)
                    product(pe, psn[:, n % 4, 0:width], lambda k: (hT[:, k, toks], hL[:, k, toks]), lambda k: (wth[i % 2][:, k, 0:width], wtl[i % 2][:, k, 0:width]), DK).then_inc(s["tok_done"], 1)
                    n += 1

        @block.scalar
        def _(act):
            def chunk_high(c):
                act.wait_ge(s["wc_loaded"], 16 * (c + 1))
                wait(act, s["chunk_done"], c - 1)
                act.activation(wch[:, c % 2], wc[:, :, :], ACT.Copy).then_inc(s["wc_high"], 1)

            def square_out(c):
                act.wait_ge(s["nat_done"], c + 1)
                wait(act, s["summed"], c)
                act.activation(square[:, :, :], pst[:, c % 2, :].rearrange("p (t n) -> p t n", t=NT), ACT.Square).then_inc(s["squared"], 1)

            def root_out(c):
                act.wait_ge(s["summed"], c + 1)
                act.activation(root[:, :], ssq[:, :], ACT.Sqrt, bias=epst[:, :]).then_inc(s["rooted"], 1)

            def piece_high(i):
                width = pieces[i][2]
                act.wait_ge(s[f"wt_loaded{i % 2}"], 32 * (i // 2 + 1))
                wait(act, s["tok_done"], (i - 1) * NT)
                act.activation(wth[i % 2][:, :, 0:width], wt[:, i % 2, :, 0:width], ACT.Copy).then_inc(s["wt_high"], 1)

            chunk_high(0)
            for c in range(chunks):
                if c + 1 < chunks:
                    chunk_high(c + 1)
                act.wait_ge(s["chunk_done"], c + 1)
                if c == 0:
                    act.wait_ge(s["padded"], 1)
                if c >= 2:
                    act.wait_ge(s["conv_done"], c - 1)
                act.activation(raw[:, c % 2, CONV - 1:], psn[:, 2 * (c % 2):2 * (c % 2) + 2, :].rearrange("p a n -> p (a n)"), ACT.Copy).then_inc(s["raw_ready"], 1)
                if 1 <= c <= normed:
                    square_out(c - 1)
                    root_out(c - 1)
                act.wait_ge(s["conv_done"], c + 1)
                act.activation(conv[:, c % 2, :], conv[:, c % 2, :], ACT.Silu).then_inc(s["silu_done"], 1)
            n = z = 0
            piece_high(0)
            for i, (col, to, width) in enumerate(pieces):
                if i + 1 < len(pieces):
                    piece_high(i + 1)
                for t in range(NT):
                    act.wait_ge(s["tok_done"], n + 1)
                    if to is not None:
                        act.activation(lat[:, t, to:to + width], psn[:, n % 4, 0:width], ACT.Copy).then_inc(s["tok_evac"], 1)
                    else:
                        if z >= 4:
                            act.wait_ge(s[f"zstored{z % 4}"], 16 * (z // 4))
                        act.activation(zstage[:, z % 4, :], psn[:, n % 4, 0:width], ACT.Silu).then_inc(s["tok_evac"], 1)
                        z += 1
                    n += 1

        @block.vector
        def _(dve):
            order = Order(dve, s["conv_step"])
            dve.memset(epst[:, :], EPS)
            dve.memset(raw[:, :, 0:CONV - 1], 0.0).then_inc(s["padded"], 1)
            dve.wait_ge(s["cw_loaded"], 16)

            def chunk_low(c):
                dve.wait_ge(s["wc_high"], c + 1)
                dve.tensor_tensor(wcl[:, c % 2], wc[:, :, :], wch[:, c % 2].bitcast(F32), ALU.subtract).then_inc(s["wc_low"], 1)

            def stage_out(c):
                src = pst[:, c % 2, :].rearrange("p (t n) -> p t n", t=NT)
                if c < normed:
                    dve.wait_ge(s["squared"], c + 1)
                    dve.tensor_reduce(ssq[:, :], square[:, :, :], AX.X, ALU.add).then_inc(s["summed"], 1)
                    dve.wait_ge(s["rooted"], c + 1)
                    order.then(dve.reciprocal(rinv[:, :], root[:, :]))
                    if c < B_HEADS:
                        order.then(dve.tensor_scalar(rinv[:, :], rinv[:, :], B_DIM ** -0.5, None, ALU.mult))
                else:
                    dve.wait_ge(s["nat_done"], c + 1)
                if c >= 2:
                    dve.wait_ge(s[f"stored{c % 2}"], 16 * (c // 2))
                if c < normed:
                    dve.tensor_tensor(stage[:, c % 2], src, bcast(rinv[:, :], 2, P), ALU.mult).then_inc(s["stage_ready"], 1)
                else:
                    dve.tensor_copy(stage[:, c % 2], src).then_inc(s["stage_ready"], 1)

            chunk_low(0)
            for c in range(chunks):
                if c + 1 < chunks:
                    chunk_low(c + 1)
                if c >= 1:
                    stage_out(c - 1)
                dve.wait_ge(s["raw_ready"], c + 1)
                if c >= 2:
                    dve.wait_ge(s["nat_done"], c - 1)
                out = conv[:, c % 2, :]
                order.then(dve.tensor_scalar(out, raw[:, c % 2, 0:SEQ], cw[:, c, 0:1], None, ALU.mult))
                for i in range(1, CONV):
                    ins = dve.scalar_tensor_tensor(out, raw[:, c % 2, i:i + SEQ], cw[:, c, i:i + 1], out, ALU.mult, ALU.add)
                    if i < CONV - 1:
                        order.then(ins)
                ins.then_inc(s["conv_done"], 1)
            stage_out(chunks - 1)
            for i, (col, to, width) in enumerate(pieces):
                dve.wait_ge(s["wt_high"], i + 1)
                dve.tensor_tensor(wtl[i % 2][:, :, 0:width], wt[:, i % 2, :, 0:width], wth[i % 2][:, :, 0:width].bitcast(F32), ALU.subtract).then_inc(s["wt_low"], 1)


def delta_gates(nc, a, lat, beta, g, eg, etail, dch, beg, tri):
    H = B_HEADS
    with ExitStack() as ctx:
        sb = lambda n, sh: ctx.enter_context(nc.sbuf_tensor(n, sh, F32))
        dtb, alog = sb("dg_dtb", [P, H]), sb("dg_alog", [P, H])
        size, soft, gate, sums = sb("dg_size", [P, NT, H]), sb("dg_soft", [P, NT, H]), sb("dg_gate", [P, NT, H]), sb("dg_sums", [P, 4, NT, H])
        ps = ctx.enter_context(nc.psum_tensor("dg_ps", [P, 128], F32))
        s = ctx.enter_context(phase(nc, "delta_gates", "rows_loaded dt_added abs_done negexp_done plus_one_done log_done alog_done soft_ready gate_ready sums_mm sums_ready tail_ready exps_done beta_ready done"))
        block = ctx.enter_context(nc.Block())

        @block.sync
        def _(sp):
            sp.dma_start(dtb[:, :], a["dt_bias"].partition_broadcast(P)).then_inc(s["rows_loaded"], 16)
            sp.dma_start(alog[:, :], a["A_log"].partition_broadcast(P)).then_inc(s["rows_loaded"], 16)

        @block.scalar
        def _(act):
            act.activation(beta[:, :, :], lat[:, :, N_B:N_B + H], ACT.Sigmoid).then_inc(s["beta_ready"], 1)
            act.wait_ge(s["rows_loaded"], 32)
            act.activation(alog[:, :], alog[:, :], ACT.Exp).then_inc(s["alog_done"], 1)
            act.wait_ge(s["dt_added"], 1)
            act.activation(size[:, :, :], gate[:, :, :], ACT.Abs).then_inc(s["abs_done"], 1)
            act.wait_ge(s["abs_done"], 1)
            act.activation(soft[:, :, :], size[:, :, :], ACT.Exp, scale=-1.0).then_inc(s["negexp_done"], 1)
            act.wait_ge(s["plus_one_done"], 1)
            act.activation(soft[:, :, :], soft[:, :, :], ACT.Ln).then_inc(s["log_done"], 1)
            act.wait_ge(s["tail_ready"], 1)
            act.activation(eg[:, :, :], g[:, :, :], ACT.Exp)
            act.activation(etail[:, :, :], etail[:, :, :], ACT.Exp)
            act.activation(dch[:, :, :, :], sums[:, 2:4], ACT.Exp).then_inc(s["exps_done"], 1)

        @block.tensor
        def _(pe):
            pe.wait_ge(s["gate_ready"], 1)
            for i in range(4):
                last = pe.matmul(ps[:, i * 32:(i + 1) * 32], lhsT=tri[:, i, :], rhs=gate[:, :, :].rearrange("p t h -> p (t h)"), start=True, stop=True)
            last.then_inc(s["sums_mm"], 1)

        @block.vector
        def _(dve):
            row = lambda r: bcast(r[:, :], 1, NT)
            dve.wait_ge(s["rows_loaded"], 32)
            dve.tensor_tensor(gate[:, :, :], lat[:, :, N_A:N_A + H], row(dtb), ALU.add).then_inc(s["dt_added"], 1)
            dve.wait_ge(s["negexp_done"], 1)
            dve.tensor_scalar(soft[:, :, :], soft[:, :, :], 1.0, None, ALU.add).then_inc(s["plus_one_done"], 1)
            dve.wait_ge(s["log_done"], 1)
            dve.scalar_tensor_tensor(soft[:, :, :], gate[:, :, :], 0.0, soft[:, :, :], ALU.max, ALU.add).then_inc(s["soft_ready"], 1)
            dve.wait_ge(s["soft_ready"], 1)
            dve.wait_ge(s["alog_done"], 1)
            dve.scalar_tensor_tensor(gate[:, :, :], soft[:, :, :], -1.0, row(alog), ALU.mult, ALU.mult).then_inc(s["gate_ready"], 1)
            dve.wait_ge(s["sums_mm"], 1)
            dve.tensor_copy(sums[:, :, :, :].rearrange("p a t h -> p (a t h)"), ps[:, :]).then_inc(s["sums_ready"], 1)
            dve.wait_ge(s["sums_ready"], 1)
            dve.tensor_copy(g[:, :, :], sums[:, 0])
            dve.tensor_tensor(etail[:, :, :], sums[:, 1], sums[:, 0], ALU.subtract).then_inc(s["tail_ready"], 1)
            dve.wait_ge(s["exps_done"], 1)
            dve.wait_ge(s["beta_ready"], 1)
            dve.tensor_tensor(beg[:, :, :], beta[:, :, :], eg[:, :, :], ALU.mult).then_inc(s["done"], 1)


def shape_constants():
    i = np.arange(P)
    same = (i[:, None] // CHUNK) == (i[None, :] // CHUNK)
    j_le_i = i[:, None] <= i[None, :]
    even = np.repeat((i < CHUNK)[:, None], P, 1)
    tri = np.stack([same & j_le_i, same, even, ~even], 1)
    lower = same & (i[:, None] >= i[None, :])
    lev = [(i[:, None] // (2 * b) == i[None, :] // (2 * b)) & (i[:, None] // b % 2 == 1) & (i[None, :] // b % 2 == 0) for b in (1, 2, 4, 8, 16, 32)]
    rel = np.arange(NREL) - (NEAR - 1)
    half, exact = REL_BUCKETS // 2, REL_BUCKETS // 4
    n = np.abs(rel)
    large = exact + (np.log(np.maximum(n, exact).astype(np.float32) / np.float32(exact)) / np.float32(math.log(REL_MAX_DIST / exact)) * np.float32(half - exact)).astype(np.int32)
    bucket = np.where(rel > 0, half, 0) + np.where(n < exact, n, np.minimum(large, half - 1))
    b = np.arange(REL_BUCKETS)[:, None]
    relhot = (b == bucket[None, :]).astype(np.float32) - (b == half - 1).astype(np.float32)
    f = lambda z: np.ascontiguousarray(z).astype(np.float32)
    return {
        "ident": f(np.eye(P)), "flip": f(np.eye(P)[::-1]), "ones": f(np.ones((P, P))), "tri": f(tri),
        "dmask": f(np.where(lower, 0, MASKED)),
        "lev": f(lev[0]), "levT": f(np.stack([z.T for z in lev], 1)),
        "row_starts": f(np.broadcast_to(np.concatenate([[0], np.arange(16, 72, 8), np.arange(72, 80)]), (P, P_TOPK))),
        "relhot": f(relhot), "iota": f(np.broadcast_to(i[None, :], (P, P))),
    }


def sparse_prepare(nc, a, proj, gains, consts, idx_keys, keys_hl, v, widx, near):
    with ExitStack() as ctx:
        sb = lambda n, sh, dt=F32: ctx.enter_context(nc.sbuf_tensor(n, sh, dt))
        w = {n: sb(f"sp_{n}", [P, 2, 512]) for n in ("w_iq", "w_uq", "w_uk", "w_uv")}
        latT = sb("sp_latT", [P, 4, SEQ])
        keys = sb("sp_keys", [P, NT, 2, IDX_DIM])
        idxT, idx_high = sb("sp_idxT", [P, SEQ]), sb("sp_idx_high", [P, SEQ], F32R)
        parts = sb("sp_parts", [P, 4, 2, 512], F32R)
        junk = sb("sp_junk", [P, 2, 256])
        ssq, root, rinv, epst = sb("sp_ssq", [P, 3, NT]), sb("sp_root", [P, 3, NT]), sb("sp_rinv", [P, 3, NT]), sb("sp_eps", [P, 1])
        relb, rowb = sb("sp_relb", [REL_BUCKETS, A_HEADS]), sb("sp_rowb", [A_HEADS, NREL])
        shifted = sb("sp_shifted", [P, A_HEADS, NEAR])
        pt = [ctx.enter_context(nc.psum_tensor(f"sp{i}", [P, 512], F32)) for i in range(8)]
        s = ctx.enter_context(phase(nc, "sparse_prep", "w_iq w_uq w_uk w_uv relb_loaded bias_mm bias_ready bias_stored near_loaded eps_ready squared rooted vorder normed transposed lat_ready idx_high_ready idx_ready proj_mm high_ready evac kept0 kept1 kept2 kept3 keys_loaded"))
        block = ctx.enter_context(nc.Block())
        banks = [(j, half) for j in range(5) for half in range(2)]
        heads = [("w_uk", 2, "k_parts", 1.0, m, half) for m in range(4) for half in range(2)] + \
                [("w_iq", 0, "qi_parts", 1.0, m, half) for m in range(4) for half in range(2)] + \
                [("w_uq", 0, "q_parts", A_DIM ** -0.5, m, half) for m in range(4) for half in range(2)]

        @block.sync
        def _(sp):
            sp.dma_start(relb[:, :], a["rel_bias"]).then_inc(s["relb_loaded"], 16)
            for n in ("w_uk", "w_iq", "w_uq", "w_uv"):
                sp.dma_start(w[n][:, :, :], a[n].rearrange("(k p) c -> p k c", p=P)).then_inc(s[n], 16)
            sp.wait_ge(s["bias_ready"], 1)
            sp.dma_start(a["bias_rows"], rowb[:, :]).then_inc(s["bias_stored"], 16)
            sp.wait_ge(s["bias_stored"], 16)
            sp.dma_start(shifted[:, :, :], bass.AP(a["bias_rows"].tensor, 0, [[1, P], [NREL, A_HEADS], [1, NEAR]])).then_inc(s["near_loaded"], 16)
            for i, (name, src, dst, scale, m, half) in enumerate(heads):
                sp.wait_ge(s["evac"], i + 1)
                for part in range(2):
                    out = a[dst][part]
                    out = out[:, m, half * 512:(half + 1) * 512] if dst == "k_parts" else out[:, half * 4:(half + 1) * 4, m, :]
                    tile = parts[:, i % 4, part, :].bitcast(F32)
                    sp.dma_start(out, tile if dst == "k_parts" else tile.rearrange("p (b n) -> p b n", n=P)).then_inc(s[f"kept{i % 4}"], 16)
                if i == 7:
                    for slot in range(4):
                        sp.wait_ge(s[f"kept{slot}"], 64)
                    for part in range(2):
                        for parity in range(2):
                            sp.dma_start(keys_hl[part * A_DIM:(part + 1) * A_DIM, parity * 4:(parity + 1) * 4, :].bitcast(F32), a["k_parts"][part, parity * A_DIM:(parity + 1) * A_DIM]).then_inc(s["keys_loaded"], 16)
            for slot in range(4):
                sp.wait_ge(s[f"kept{slot}"], 32 * len(heads) // 4)
            sp.wait_ge(s["keys_loaded"], 64)

        @block.scalar
        def _(act):
            n = 0
            for g, (col, width) in enumerate(((0, A_LORA), (A_LORA, A_LORA), (N_IDX, IDX_DIM))):
                for t in range(NT):
                    if n >= 2:
                        act.wait_ge(s["squared"], n - 1)
                    act.activation(junk[:, n % 2, 0:width], proj[:, t, col:col + width], ACT.Square, accum_out=ssq[:, g, t:t + 1]).then_inc(s["squared"], 1)
                    n += 1
            act.wait_ge(s["squared"], n)
            act.wait_ge(s["eps_ready"], 1)
            act.activation(root[:, 0:2], ssq[:, 0:2], ACT.Sqrt, bias=epst[:, :], scale=1.0 / A_LORA).then_inc(s["rooted"], 1)
            act.activation(root[:, 2], ssq[:, 2], ACT.Sqrt, bias=epst[:, :], scale=1.0 / IDX_DIM).then_inc(s["rooted"], 1)
            for i, (j, half) in enumerate(banks):
                act.wait_ge(s["transposed"], i + 1)
                out = latT[:, j] if j < 4 else idxT
                act.activation(out[:, half * 512:(half + 1) * 512], pt[i % 8][:, :], ACT.Copy, scale=gains[:, j:j + 1]).then_inc(s["lat_ready"], 1)
            act.wait_ge(s["lat_ready"], len(banks))
            act.activation(idx_high[:, :], idxT[:, :], ACT.Copy).then_inc(s["idx_high_ready"], 1)
            act.activation(idx_keys[0:IDX_DIM, :], idxT[0:IDX_DIM, :], ACT.Copy)
            for i, (name, src, dst, scale, m, half) in enumerate(heads):
                act.wait_ge(s["proj_mm"], i + 1)
                if i >= 4:
                    act.wait_ge(s[f"kept{i % 4}"], 32 * (i // 4))
                act.activation(parts[:, i % 4, 0, :], pt[i % 8][:, :], ACT.Copy, scale=scale).then_inc(s["high_ready"], 1)

        @block.tensor
        def _(pe):
            pe.wait_ge(s["relb_loaded"], 16)
            pe.matmul(pt[7][0:A_HEADS, 0:NREL], lhsT=relb[:, :], rhs=consts["relhot"], start=True, stop=True).then_inc(s["bias_mm"], 1)
            pe.wait_ge(s["normed"], 3)
            pe.wait_ge(s["bias_ready"], 1)
            for i, (j, half) in enumerate(banks):
                if i >= 8:
                    pe.wait_ge(s["lat_ready"], i - 7)
                for b in range(4):
                    t = half * 4 + b
                    src = proj[:, t, j * P:(j + 1) * P] if j < 4 else keys[:, t].rearrange("p a d -> p (a d)")
                    last = pe.transpose(pt[i % 8][:, b * P:(b + 1) * P], src, consts["ident"])
                last.then_inc(s["transposed"], 1)
            pe.wait_ge(s["lat_ready"], len(banks))
            for i, (name, src, dst, scale, m, half) in enumerate(heads):
                pe.wait_ge(s[name], 16)
                if i >= 8:
                    pe.wait_ge(s["evac"], i - 7)
                for k in range(2):
                    last = pe.matmul(pt[i % 8][:, :], lhsT=w[name][:, k, m * P:(m + 1) * P], rhs=latT[:, src + k, half * 512:(half + 1) * 512], start=(k == 0), stop=(k == 1))
                last.then_inc(s["proj_mm"], 1)
            pe.wait_ge(s["w_uv"], 16)
            for t in range(NT):
                i = len(heads) + t
                pe.wait_ge(s["evac"], i - 7)
                for k in range(2):
                    last = pe.matmul(pt[i % 8][:, :], lhsT=latT[:, 2 + k, t * P:(t + 1) * P], rhs=w["w_uv"][:, k, :], start=(k == 0), stop=(k == 1))
                last.then_inc(s["proj_mm"], 1)
            pe.wait_ge(s["near_loaded"], 16)
            for j in range(4):
                i = len(heads) + NT + j
                pe.wait_ge(s["evac"], i - 7)
                pe.matmul(pt[i % 8][:, :], lhsT=consts["flip"], rhs=shifted[:, 2 * j:2 * j + 2, :].rearrange("p h c -> p (h c)"), start=True, stop=True).then_inc(s["proj_mm"], 1)

        @block.vector
        def _(dve):
            order = Order(dve, s["vorder"])
            dve.memset(epst[:, :], EPS).then_inc(s["eps_ready"], 1)
            dve.wait_ge(s["bias_mm"], 1)
            dve.tensor_copy(rowb[:, :], pt[7][0:A_HEADS, 0:NREL]).then_inc(s["bias_ready"], 1)
            dve.tensor_scalar(widx, proj[:, :, N_IDX + IDX_DIM:N_A], (IDX_HEADS * IDX_DIM) ** -0.5, None, ALU.mult)
            dve.wait_ge(s["rooted"], 2)
            order.then(dve.reciprocal(rinv[:, :, :], root[:, :, :]))
            for g in range(2):
                dve.tensor_tensor(proj[:, :, g * A_LORA:(g + 1) * A_LORA], proj[:, :, g * A_LORA:(g + 1) * A_LORA], bcast(rinv[:, g], 2, A_LORA), ALU.mult).then_inc(s["normed"], 1)
            for twice in range(2):
                last = dve.tensor_tensor(keys[:, :, twice, :], proj[:, :, N_IDX:N_IDX + IDX_DIM], bcast(rinv[:, 2], 2, IDX_DIM), ALU.mult)
            last.then_inc(s["normed"], 1)
            dve.wait_ge(s["idx_high_ready"], 1)
            dve.tensor_tensor(idx_keys[IDX_DIM:, :], idxT[IDX_DIM:, :], idx_high[IDX_DIM:, :].bitcast(F32), ALU.subtract)
            for i, (name, src, dst, scale, m, half) in enumerate(heads):
                dve.wait_ge(s["high_ready"], i + 1)
                dve.scalar_tensor_tensor(parts[:, i % 4, 1, :], pt[i % 8][:, :], scale, parts[:, i % 4, 0, :].bitcast(F32), ALU.mult, ALU.subtract).then_inc(s["evac"], 1)
            for t in range(NT):
                i = len(heads) + t
                dve.wait_ge(s["proj_mm"], i + 1)
                dve.tensor_copy(v[:, t, :], pt[i % 8][:, :]).then_inc(s["evac"], 1)
            for j in range(4):
                i = len(heads) + NT + j
                dve.wait_ge(s["proj_mm"], i + 1)
                dve.tensor_copy(near[:, 2 * j:2 * j + 2, :].rearrange("p h c -> p (h c)"), pt[i % 8][:, :]).then_inc(s["evac"], 1)


def mixers(nc, a, heads, gatings, lat, mix, consts):
    H, B, W4 = A_HEADS, B_HEADS, B_HEADS * P
    idx_keys, keys_hl, v, widx, near = heads
    beta, g, eg, etail, dch, beg = gatings
    ident, dmask, lev, levT = (consts[n] for n in ("ident", "dmask", "lev", "levT"))
    FIRST = TOPK // P
    DELTAS = {2: (0,), 3: (1,), 4: (2,), 5: (3,), 6: (4, 5), 7: (6, 7)}
    FILL = {2: 4, 3: 4, 4: 4, 5: 3, 6: 2, 7: 2}
    HEAD_FILL, INDEX_FILL = 2, 2
    with ExitStack() as ctx:
        sb = lambda n, sh, dt=F32: ctx.enter_context(nc.sbuf_tensor(n, sh, dt))
        flat = lat[:, :, :].rearrange("p t c -> p (t c)")
        tile4 = lambda at: flat[:, at:at + W4].rearrange("p (h n) -> p h n", h=B)
        score = [flat[:, 0:SEQ], sb("mx_score", [P, SEQ])[:, :]]
        logit = [flat[:, SEQ:2 * SEQ], flat[:, 2 * SEQ:3 * SEQ], sb("mx_logit", [P, SEQ])[:, :]]
        dstr, intra, mT = (tile4(3 * SEQ + i * W4) for i in range(3))
        q_high = {kind: sb(f"mx_{kind}_high", [P, H, P], F32R) for kind in ("index", "head")}
        q_low = {kind: sb(f"mx_{kind}_low", [A_DIM, H, P], F32R) for kind in ("index", "head")}
        probT = sb("mx_probT", [P, 2, NT, P])
        top8 = sb("mx_top8", [P, 8])
        nmax, rsum, rinv = sb("mx_nmax", [P, 2, H]), sb("mx_rsum", [P, 2, H]), sb("mx_rinv", [P, H])
        nat, zs = sb("mx_nat", [P, 2, 3 * B, P]), sb("mx_zs", [P, 2, B, P])
        square = sb("mx_square", [P, B, P])
        gon = sb("mx_gon", [P, P])
        oss, orinv, power = sb("mx_oss", [P, B]), sb("mx_orinv", [P, B]), sb("mx_power", [P, B])
        state = sb("mx_state", [P, 2, B, P])
        inv = sb("mx_inv", [P, 2, 2, 2, P])
        cT, y, diag, vnew, qd, vb, kbg, ktail, qT_, kT_, qdT, decay, intraT = (
            sb(f"mx_{n}", [P, B, P]) for n in ("cT", "y", "diag", "vnew", "qd", "vb", "kbg", "ktail", "qT", "kT", "qdT", "decay", "intraT"))
        u, m, wT, o = cT, qd, kT_, y
        ps = ctx.enter_context(nc.psum_tensor("mx_ps", [P, 8, 512], F32))
        psS = ps[:, 0:4, :].rearrange("p (a b) n -> p a (b n)", a=2)
        psT = ps[:, 4:6, :].rearrange("p a n -> p (a n)")
        psO = ps[:, 7, :]
        psY, psX = (ps[:, 2, 0:256], ps[:, 1, 0:256]), (ps[:, 4, :], ps[:, 3, :])
        pq, pk, pd, pg, pc, px, po = (ps[:, i, :].rearrange("p (h n) -> p h n", h=B) for i in range(7))
        s = ctx.enter_context(phase(nc, "mix",
            "gon_loaded index_loaded head_loaded nat0 nat1 zs0 zs1 vorder porder power_ready dots_mm relu_done relu_used logit_done max_ready exp_done prob_mm prob_ready out_mm out_done "
            "nat_free side_ready diag_ready qd_ready transposed qT_ready qdT_ready row_mm kk_mm dexp_ready decay_ready m_ready mT_mm intraT_ready "
            "c_ready y_mm y_ready x_mm uw_mm wT_ready u_ready vp_mm vnew_ready kv_mm o_mm inv_ready state_ready oss_ready orinv_ready zg_ready"))
        block = ctx.enter_context(nc.Block())
        one = lambda z, t: z[:, t, :]
        wide = lambda z, t: bcast(z[:, t, :], 2, P)
        uses, nidx, nhead = [], 0, 0
        for b in range(NT):
            if FIRST <= b + 1 < NT:
                for h in range(H):
                    uses.append((b + 1, "index", h, nidx))
                    nidx += 1
            for h in range(H):
                uses.append((b, "head", h, nhead))
                nhead += 1
        taken = {(b, kind, h): (i, n) for i, (b, kind, h, n) in enumerate(uses)}

        @block.sync
        def _(sp):
            def load_queries(kind, b):
                if (b - 1, kind, H - 1) in taken:
                    sp.wait_ge(s["dots_mm"], taken[b - 1, kind, H - 1][0] + 1)
                src = a["qi_parts" if kind == "index" else "q_parts"]
                for parity in range(2):
                    rows, own = slice(parity * A_DIM, (parity + 1) * A_DIM), slice(parity * 4, (parity + 1) * 4)
                    for copy in range(2):
                        sp.dma_start(q_high[kind][copy * A_DIM:(copy + 1) * A_DIM, own, :].bitcast(F32), src[0, rows, b]).then_inc(s[f"{kind}_loaded"], 16)
                    sp.dma_start(q_low[kind][:, own, :].bitcast(F32), src[1, rows, b]).then_inc(s[f"{kind}_loaded"], 16)

            def load_delta(t):
                wait(sp, s["nat_free"], t - 1)
                sp.dma_start(nat[:, t % 2].rearrange("p h n -> p (h n)"), a["nat"][t]).then_inc(s[f"nat{t % 2}"], 16)
                sp.dma_start(zs[:, t % 2].rearrange("p h n -> p (h n)"), a["silu_z"][t]).then_inc(s[f"zs{t % 2}"], 16)

            load_queries("head", 0)
            load_queries("index", FIRST)
            sp.dma_start(gon[:, :], a["g_onorm"].partition_broadcast(P)).then_inc(s["gon_loaded"], 16)
            load_delta(0)
            load_delta(1)
            for b in range(NT):
                if b + 1 < NT:
                    if b >= FIRST:
                        load_queries("index", b + 1)
                        for t in DELTAS[b]:
                            if t + 2 < NT:
                                load_delta(t + 2)
                    load_queries("head", b + 1)

        @block.tensor
        def _(pe):
            def dots(b, kind, h):
                W = (b + 1) * P
                i, n = taken[b, kind, h]
                if i >= 2:
                    _, before, _, k = uses[i - 2]
                    pe.wait_ge(s["relu_done" if before == "index" else "logit_done"], k + 1)
                at = h % 2 * 4 + h // 2
                if h == 0:
                    pe.wait_ge(s[f"{kind}_loaded"], 96 * (b + 1 - (FIRST if kind == "index" else 0)))
                key = idx_keys if kind == "index" else keys_hl[:, at]
                for c in range(0, W, 512):
                    e = c + max(256, min(W - c, 512))
                    pe.matmul(psS[:, i % 2, c:e], lhsT=q_high[kind][:, at, :], rhs=key[:, c:e], start=True, stop=False)
                    last = pe.matmul(psS[:, i % 2, c:e], lhsT=q_low[kind][:, at, :], rhs=key[0:A_DIM, c:e], start=False, stop=True)
                last.then_inc(s["dots_mm"], 1)

            def transpose_probs(n):
                b, h = divmod(n, H)
                pe.wait_ge(s["exp_done"], n + 1)
                wait(pe, s["prob_ready"], n)
                for j in range(b + 1):
                    last = pe.transpose(psT[:, j * P:(j + 1) * P], logit[n % 3][:, j * P:(j + 1) * P], ident)
                last.then_inc(s["prob_mm"], 1)

            def weigh_values(n):
                b, h = divmod(n, H)
                pe.wait_ge(s["prob_ready"], n + 1)
                if h == 0:
                    wait(pe, s["out_done"], b)
                for j in range(b + 1):
                    last = pe.matmul(psO[:, h * A_DIM:(h + 1) * A_DIM], lhsT=probT[:, n % 2, j, :], rhs=v[:, j, h * A_DIM:(h + 1) * A_DIM], start=(j == 0), stop=(j == b))
                last.then_inc(s["out_mm"], 1)

            def delta(t):
                pe.wait_ge(s["qd_ready"], t + 1)
                pe.wait_ge(s["state_ready"], 2 * t + 1)
                for h in range(B):
                    pe.transpose(pq[:, h], nat[:, t % 2, h, :], ident)
                for h in range(B):
                    pe.transpose(pk[:, h], nat[:, t % 2, B + h, :], ident)
                for h in range(B):
                    last = pe.transpose(pd[:, h], qd[:, h, :], ident)
                last.then_inc(s["transposed"], 1)
                pe.wait_ge(s["diag_ready"], t + 1)
                pe.matmul(ps[:, 3, :], lhsT=consts["ones"], rhs=diag[:, :, :].rearrange("p h n -> p (h n)"), start=True, stop=True).then_inc(s["row_mm"], 1)
                pe.wait_ge(s["qT_ready"], t + 1)
                for h in range(B):
                    pe.matmul(pc[:, h], lhsT=kT_[:, h, :], rhs=kT_[:, h, :], start=True, stop=True)
                for h in range(B):
                    last = pe.matmul(px[:, h], lhsT=qT_[:, h, :], rhs=kT_[:, h, :], start=True, stop=True)
                last.then_inc(s["kk_mm"], 1)
                pe.wait_ge(s["m_ready"], t + 1)
                for h in range(B):
                    pe.transpose(pq[:, h], m[:, h, :], ident)
                for h in range(B):
                    last = pe.transpose(pk[:, h], intra[:, h, :], ident)
                last.then_inc(s["mT_mm"], 1)
                pe.wait_ge(s["qdT_ready"], t + 1)
                pe.wait_ge(s["intraT_ready"], t + 1)
                for l in range(5):
                    pe.wait_ge(s["c_ready"], t * 5 + l + 1)
                    for pair in range(2):
                        pe.wait_ge(s["inv_ready"], t * 11 + (2 * l + pair if l else 1))
                        for h in range(2):
                            last = pe.matmul(psY[pair][:, h * P:(h + 1) * P], lhsT=cT[:, 2 * pair + h, :], rhs=inv[:, pair, 1, h, :], start=True, stop=True)
                        last.then_inc(s["y_mm"], 1)
                    for pair in range(2):
                        pe.wait_ge(s["y_ready"], t * 10 + 2 * l + pair + 1)
                        for h in range(2):
                            last = pe.matmul(psX[pair][:, h * P:(h + 1) * P], lhsT=y[:, 2 * pair + h, :], rhs=inv[:, pair, 0, h, :], start=True, stop=True)
                        if l < 4:
                            for h in range(2):
                                last = pe.matmul(psX[pair][:, (2 + h) * P:(3 + h) * P], lhsT=inv[:, pair, 0, h, :], rhs=y[:, 2 * pair + h, :], start=True, stop=True)
                        last.then_inc(s["x_mm"], 1)
                pe.wait_ge(s["inv_ready"], t * 11 + 11)
                pe.wait_ge(s["side_ready"], t + 1)
                for h in range(B):
                    pe.matmul(px[:, h], lhsT=kbg[:, h, :], rhs=inv[:, h // 2, 0, h % 2, :], start=True, stop=True)
                for h in range(B):
                    last = pe.matmul(pc[:, h], lhsT=inv[:, h // 2, 0, h % 2, :], rhs=vb[:, h, :], start=True, stop=True)
                last.then_inc(s["uw_mm"], 1)
                pe.wait_ge(s["wT_ready"], t + 1)
                for c in range(2):
                    r = slice(c * CHUNK, (c + 1) * CHUNK)
                    pe.wait_ge(s["state_ready"], 2 * t + c + 1)
                    for h in range(B):
                        last = pe.matmul(pd[r, h], lhsT=wT[:, h, r], rhs=state[:, c, h, :], start=True, stop=True)
                    last.then_inc(s["vp_mm"], 1)
                    pe.wait_ge(s["vnew_ready"], 2 * t + c + 1)
                    for h in range(B):
                        last = pe.matmul(pq[:, h], lhsT=ktail[r, h, :], rhs=vnew[r, h, :], start=True, stop=True)
                    last.then_inc(s["kv_mm"], 1)
                    for h in range(B):
                        pe.matmul(po[r, h], lhsT=qdT[:, h, r], rhs=state[:, c, h, :], start=True, stop=False)
                        last = pe.matmul(po[r, h], lhsT=intraT[r, h, r], rhs=vnew[r, h, :], start=False, stop=True)
                    last.then_inc(s["o_mm"], 1)

            for b in range(NT):
                if b >= FIRST:
                    pe.wait_ge(s["relu_done"], (b - FIRST + 1) * H)
                    pe.wait_ge(s["logit_done"], b * H)
                    pe.wait_ge(s["prob_ready"], b * H)
                    for t in DELTAS[b]:
                        delta(t)
                    pe.wait_ge(s["state_ready"], 2 * DELTAS[b][-1] + 3)
                if FIRST <= b + 1 < NT:
                    for h in range(H):
                        dots(b + 1, "index", h)
                for h in range(H):
                    n = b * H + h
                    dots(b, "head", h)
                    if h >= 1:
                        transpose_probs(n - 1)
                    if h >= 2:
                        weigh_values(n - 2)
                transpose_probs(n)
                weigh_values(n - 1)
                weigh_values(n)

        @block.scalar
        def _(act):
            def probs_out(n):
                b = n // H
                act.wait_ge(s["prob_mm"], n + 1)
                wait(act, s["out_mm"], n - 1)
                act.activation(probT[:, n % 2, 0:b + 1, :].rearrange("p j q -> p (j q)"), psT[:, 0:(b + 1) * P], ACT.Copy).then_inc(s["prob_ready"], 1)

            def delta(t):
                act.wait_ge(s["transposed"], t + 1)
                act.activation(kT_[:, :, :], pk, ACT.Copy)
                act.activation(qT_[:, :, :], pq, ACT.Copy).then_inc(s["qT_ready"], 1)
                act.wait_ge(s["dexp_ready"], t + 1)
                act.activation(decay[:, :, :], decay[:, :, :], ACT.Exp).then_inc(s["decay_ready"], 1)
                act.activation(qdT[:, :, :], pd, ACT.Copy).then_inc(s["qdT_ready"], 1)
                act.wait_ge(s["mT_mm"], t + 1)
                act.activation(intraT[:, :, :], pk, ACT.Copy).then_inc(s["intraT_ready"], 1)
                for i in range(10):
                    pair = i % 2
                    act.wait_ge(s["y_mm"], t * 10 + i + 1)
                    act.activation(y[:, 2 * pair:2 * pair + 2, :].rearrange("p h n -> p (h n)"), psY[pair], ACT.Copy).then_inc(s["y_ready"], 1)
                act.wait_ge(s["uw_mm"], t + 1)
                act.activation(wT[:, :, :], px, ACT.Copy).then_inc(s["wT_ready"], 1)
                act.activation(u[:, :, :], pc, ACT.Copy).then_inc(s["u_ready"], 1)
                act.wait_ge(s["o_mm"], 2 * t + 2)
                wait(act, s["orinv_ready"], t)
                for h in range(B):
                    last = act.activation(square[:, h, :], po[:, h], ACT.Square, accum_out=oss[:, h:h + 1])
                last.then_inc(s["oss_ready"], 1)

            for b in range(NT):
                W = (b + 1) * P
                for t in DELTAS.get(b, ()):
                    delta(t)
                if FIRST <= b + 1 < NT:
                    for h in range(H):
                        i, n = taken[b + 1, "index", h]
                        act.wait_ge(s["dots_mm"], i + 1)
                        if h < 3:
                            act.wait_ge(s["prob_mm"], b * H)
                        else:
                            act.wait_ge(s["relu_used"], n - 2)
                        act.activation(logit[n % 3][:, 0:W + P], psS[:, i % 2, 0:W + P], ACT.Relu).then_inc(s["relu_done"], 1)
                for h in range(H):
                    n = b * H + h
                    act.wait_ge(s["max_ready"], n + 1)
                    act.activation(logit[n % 3][:, 0:W], logit[n % 3][:, 0:W], ACT.Exp, bias=nmax[:, b % 2, h:h + 1], accum_out=rsum[:, b % 2, h:h + 1]).then_inc(s["exp_done"], 1)
                    if h >= 1:
                        probs_out(n - 1)
                probs_out(n)

        @block.gpsimd
        def _(pool):
            order = Order(pool, s["porder"])
            order.then(pool.memset(power[:, :], -0.5))
            pool.wait_ge(s["gon_loaded"], 16)
            def decayed(t):
                pool.wait_ge(s[f"nat{t % 2}"], 16 * (t // 2) + 16)
                if t >= 1:
                    pool.wait_ge(s["mT_mm"], t)
                    pool.wait_ge(s["c_ready"], (t - 1) * 5 + 1)
                pool.tensor_tensor(qd[:, :, :], nat[:, t % 2, 0:B], wide(eg, t), ALU.mult).then_inc(s["qd_ready"], 1)
                pool.tensor_tensor(diag[:, :, :], bcast(ident, 1, B), wide(g, t), ALU.mult).then_inc(s["diag_ready"], 1)

            decayed(0)
            for t in range(NT):
                pool.wait_ge(s[f"nat{t % 2}"], 16 * (t // 2) + 16)
                wait(pool, s["uw_mm"], t)
                pool.tensor_tensor(vb[:, :, :], nat[:, t % 2, 2 * B:], wide(beta, t), ALU.mult)
                pool.tensor_tensor(kbg[:, :, :], nat[:, t % 2, B:2 * B], wide(beg, t), ALU.mult)
                wait(pool, s["o_mm"], 2 * t)
                pool.tensor_tensor(ktail[:, :, :], nat[:, t % 2, B:2 * B], wide(etail, t), ALU.mult).then_inc(s["side_ready"], 1)
                pool.wait_ge(s[f"zs{t % 2}"], 16 * (t // 2) + 16)
                pool.tensor_tensor(zs[:, t % 2], zs[:, t % 2], bcast(gon[:, :], 1, B), ALU.mult).then_inc(s["zg_ready"], 1)
                if t + 1 < NT:
                    decayed(t + 1)
                pool.wait_ge(s["oss_ready"], t + 1)
                order.then(pool.tensor_scalar(orinv[:, :], oss[:, :], 1.0 / B_DIM, EPS, ALU.mult, ALU.add))
                pool.tensor_tensor(orinv[:, :], orinv[:, :], power[:, :], ALU.pow).then_inc(s["orinv_ready"], 1)

        @block.vector
        def _(dve):
            order = Order(dve, s["vorder"])
            idents = bcast(ident, 1, B)

            def top_rounds(b):
                keys = score[b % 2][:, 0:(b + 1) * P]
                order.then(dve.memset(score[b % 2][0:CHUNK, (b + 1) * P - CHUNK:(b + 1) * P], INADMISSIBLE))
                for _ in range(TOPK // 8):
                    order.then(dve.max(top8[:, :], keys))
                    yield
                    order.then(dve.match_replace(keys, top8[:, :], keys, TAKEN))
                    yield
                order.then(dve.tensor_scalar(keys, keys, -1e38, MASKED, ALU.is_gt, ALU.mult))

            def outputs(b):
                dve.wait_ge(s["out_mm"], H * (b + 1))
                order.then(dve.reciprocal(rinv[:, :], rsum[:, b % 2, :]))
                dve.tensor_tensor(mix[:, b, 0:H * A_DIM].rearrange("p (h d) -> p h d", h=H), psO.rearrange("p (h d) -> p h d", h=H), bcast(rinv[:, :], 2, A_DIM), ALU.mult).then_inc(s["out_done"], 1)

            def delta(t, fill):
                fill()
                dve.wait_ge(s["row_mm"], t + 1)
                order.then(dve.scalar_tensor_tensor(decay[:, :, :], pg, -1.0, bcast(dmask, 1, B), ALU.mult, ALU.add))
                dve.tensor_tensor(decay[:, :, :], decay[:, :, :], wide(g, t), ALU.add).then_inc(s["dexp_ready"], 1)
                fill()
                dve.wait_ge(s["decay_ready"], t + 1)
                order.then(dve.tensor_tensor(dstr, decay[:, :, :], wide(beta, t), ALU.mult))
                dve.wait_ge(s["kk_mm"], t + 1)
                dve.tensor_tensor(intra, px, decay[:, :, :], ALU.mult)
                dve.tensor_tensor(m[:, :, :], pc, dstr, ALU.mult).then_inc(s["m_ready"], 1)
                dve.wait_ge(s["m_ready"], t + 1)
                pairs = lambda z: z.rearrange("p (a b) n -> p a b n", a=2)
                order.then(dve.tensor_tensor(inv[:, :, 1], pairs(m[:, :, :]), pairs(bcast(lev, 1, B)), ALU.mult))
                order.then(dve.tensor_tensor(inv[:, :, 1], pairs(idents), inv[:, :, 1], ALU.subtract))
                fill()
                dve.wait_ge(s["mT_mm"], t + 1)
                order.then(dve.tensor_copy(mT, pq))
                dve.tensor_tensor(cT[:, :, :], mT, bcast(levT[:, 1, :], 1, B), ALU.mult).then_inc(s["c_ready"], 1)
                order.then(dve.tensor_tensor(inv[:, :, 0], pairs(mT), pairs(bcast(levT[:, 0, :], 1, B)), ALU.mult))
                dve.tensor_tensor(inv[:, :, 0], pairs(idents), inv[:, :, 0], ALU.subtract).then_inc(s["inv_ready"], 1)
                dve.wait_ge(s["inv_ready"], t * 11 + 1)
                for l in range(5):
                    if l < 4:
                        dve.wait_ge(s["y_mm"], t * 10 + 2 * l + 2)
                        dve.tensor_tensor(cT[:, :, :], mT, bcast(levT[:, l + 2, :], 1, B), ALU.mult).then_inc(s["c_ready"], 1)
                    fill()
                    for pair in range(2):
                        dve.wait_ge(s["x_mm"], t * 10 + 2 * l + pair + 1)
                        out = inv[:, pair].rearrange("p a h n -> p (a h n)")[:, 0:512 if l < 4 else 256]
                        dve.tensor_tensor(out, out, psX[pair][:, 0:512 if l < 4 else 256], ALU.subtract).then_inc(s["inv_ready"], 1)
                    dve.wait_ge(s["inv_ready"], t * 11 + 2 * l + 3)
                fill()
                dve.wait_ge(s["u_ready"], t + 1)
                for c in range(2):
                    r = slice(c * CHUNK, (c + 1) * CHUNK)
                    wait(dve, s["o_mm"], 2 * t + c)
                    order.then(dve.tensor_tensor(state[:, 1 - c], state[:, c], bcast(dch[:, c, t, :], 2, P), ALU.mult))
                    dve.wait_ge(s["vp_mm"], 2 * t + c + 1)
                    dve.tensor_tensor(vnew[r, :, :], u[r, :, :], pd[r], ALU.subtract).then_inc(s["vnew_ready"], 1)
                    if c == 0:
                        fill()
                    dve.wait_ge(s["kv_mm"], 2 * t + c + 1)
                    dve.tensor_tensor(state[:, 1 - c], state[:, 1 - c], pq, ALU.add).then_inc(s["state_ready"], 1)
                    dve.wait_ge(s["state_ready"], 2 * t + c + 2)
                fill()
                dve.wait_ge(s["zg_ready"], t + 1)
                dve.wait_ge(s["oss_ready"], t + 1)
                order.then(dve.tensor_tensor(o[:, :, :], po, zs[:, t % 2], ALU.mult))
                fill()
                dve.wait_ge(s["orinv_ready"], t + 1)
                dve.tensor_tensor(mix[:, t, W4:].rearrange("p (h n) -> p h n", n=P), o[:, :, :], bcast(orinv[:, :], 2, P), ALU.mult).then_inc(s["nat_free"], 1)

            order.then(dve.memset(state[:, :, :, :], 0.0))
            dve.sem_inc(s["state_ready"], 1)
            def index_head(b, h):
                i, n = taken[b, "index", h]
                keys = score[b % 2][:, 0:(b + 1) * P]
                dve.wait_ge(s["relu_done"], n + 1)
                if h == 0:
                    ins = dve.tensor_scalar(keys, logit[n % 3][:, 0:(b + 1) * P], widx[:, b, h:h + 1], None, ALU.mult)
                else:
                    ins = dve.scalar_tensor_tensor(keys, logit[n % 3][:, 0:(b + 1) * P], widx[:, b, h:h + 1], keys, ALU.mult, ALU.add)
                ins.then_inc(s["relu_used"], 1)
                dve.wait_ge(s["relu_used"], n + 1)

            def head(b, h):
                W = (b + 1) * P
                i, n = taken[b, "head", h]
                dve.wait_ge(s["dots_mm"], i + 1)
                wait(dve, s["prob_mm"], n - 2)
                dve.tensor_tensor(logit[n % 3][:, 0:W], psS[:, i % 2, 0:W], score[b % 2][:, 0:W], ALU.add).then_inc(s["logit_done"], 1)
                dve.wait_ge(s["logit_done"], n + 1)
                lo = max(0, W - NEAR)
                tail = logit[n % 3][:, lo:W]
                order.then(dve.tensor_tensor(tail, tail, near[:, h, NEAR - (W - lo):NEAR], ALU.add))
                dve.tensor_reduce(nmax[:, b % 2, h:h + 1], logit[n % 3][:, 0:W], AX.X, ALU.max, negate=True).then_inc(s["max_ready"], 1)

            def steps(rounds, n):
                for _ in range(n):
                    next(rounds, None)

            rounds = iter(())
            for b in range(NT):
                W = (b + 1) * P
                for t in DELTAS.get(b, ()):
                    delta(t, lambda: steps(rounds, FILL[b]))
                if FIRST <= b + 1 < NT:
                    for h in range(H):
                        index_head(b + 1, h)
                        steps(rounds, INDEX_FILL)
                for _ in rounds:
                    pass
                if b < FIRST:
                    order.then(dve.memset(score[b % 2][:, 0:W], 0.0))
                    order.then(dve.memset(score[b % 2][0:CHUNK, W - CHUNK:W], MASKED))
                rounds = top_rounds(b + 1) if FIRST <= b + 1 < NT else iter(())
                for h in range(H):
                    head(b, h)
                    steps(rounds, HEAD_FILL)
                outputs(b)


def mix_out(nc, a, mix, x, ident):
    with ExitStack() as ctx:
        sb = lambda n, sh, dt=F32: ctx.enter_context(nc.sbuf_tensor(n, sh, dt))
        w = sb("mo_w", [P, 2, D_MODEL])
        wh, wl = sb("mo_wh", [P, DK, D_MODEL], F32R), sb("mo_wl", [P, DK, D_MODEL], F32R)
        mixh, mixl = sb("mo_mixh", [P, 2, DK, P], F32R), sb("mo_mixl", [P, 2, DK, P], F32R)
        pst = ctx.enter_context(nc.psum_tensor("mo_t", [P, 2, DK, P], F32))
        psy = ctx.enter_context(nc.psum_tensor("mo_y", [P, 4, 512], F32))
        s = ctx.enter_context(phase(nc, "mix_out", "w_loaded0 w_loaded1 x_loaded w_high w_low transposed mix_high mix_low y_mm y_added"))
        block = ctx.enter_context(nc.Block())

        @block.sync
        def _(sp):
            for k in range(DK):
                wait(sp, s["w_low"], k - 1)
                sp.dma_start(w[:, k % 2, :], a["w_out"][k * P:(k + 1) * P, :]).then_inc(s[f"w_loaded{k % 2}"], 16)
            sp.dma_start(x[:, :, :], a["x"].rearrange("(t p) c -> p t c", p=P)).then_inc(s["x_loaded"], 16)

        @block.tensor
        def _(pe):
            def transposes(t):
                wait(pe, s["mix_low"], t - 1)
                for k in range(DK):
                    last = pe.transpose(pst[:, t % 2, k, :], mix[:, t, k * P:(k + 1) * P], ident)
                last.then_inc(s["transposed"], 1)

            transposes(0)
            for t in range(NT):
                if t + 1 < NT:
                    transposes(t + 1)
                pe.wait_ge(s["mix_low"], t + 1)
                for half in range(2):
                    n = 2 * t + half
                    cols = slice(half * 512, (half + 1) * 512)
                    wait(pe, s["y_added"], n - 3)
                    for k in range(DK):
                        if n == 0:
                            pe.wait_ge(s["w_low"], k + 1)
                        pe.matmul(psy[:, n % 4, :], lhsT=mixh[:, t % 2, k, :], rhs=wh[:, k, cols], start=(k == 0), stop=False)
                        pe.matmul(psy[:, n % 4, :], lhsT=mixh[:, t % 2, k, :], rhs=wl[:, k, cols], start=False, stop=False)
                        last = pe.matmul(psy[:, n % 4, :], lhsT=mixl[:, t % 2, k, :], rhs=wh[:, k, cols], start=False, stop=(k == DK - 1))
                    last.then_inc(s["y_mm"], 1)

        @block.scalar
        def _(act):
            def mix_high(t):
                act.wait_ge(s["transposed"], t + 1)
                wait(act, s["y_mm"], 2 * (t - 1))
                act.activation(mixh[:, t % 2], pst[:, t % 2], ACT.Copy).then_inc(s["mix_high"], 1)

            mix_high(0)
            for k in range(DK):
                act.wait_ge(s[f"w_loaded{k % 2}"], 16 * (k // 2 + 1))
                act.activation(wh[:, k, :], w[:, k % 2, :], ACT.Copy).then_inc(s["w_high"], 1)
            for t in range(1, NT):
                mix_high(t)

        @block.vector
        def _(dve):
            def mix_low(t):
                dve.wait_ge(s["mix_high"], t + 1)
                dve.tensor_tensor(mixl[:, t % 2], pst[:, t % 2], mixh[:, t % 2].bitcast(F32), ALU.subtract).then_inc(s["mix_low"], 1)

            mix_low(0)
            for k in range(DK):
                dve.wait_ge(s["w_high"], k + 1)
                dve.tensor_tensor(wl[:, k, :], w[:, k % 2, :], wh[:, k, :].bitcast(F32), ALU.subtract).then_inc(s["w_low"], 1)
            dve.wait_ge(s["x_loaded"], 16)
            for t in range(NT):
                if t + 1 < NT:
                    mix_low(t + 1)
                for half in range(2):
                    xr = x[:, t, half * 512:(half + 1) * 512]
                    dve.wait_ge(s["y_mm"], 2 * t + half + 1)
                    dve.tensor_tensor(xr, xr, psy[:, (2 * t + half) % 4, :], ALU.add).then_inc(s["y_added"], 1)


def cross_project(nc, a, hT, memT, qT, kT, v):
    with ExitStack() as ctx:
        w = {n: ctx.enter_context(nc.sbuf_tensor(f"cp_{n}", [P, DK, 512], F32)) for n in ("wk_x", "wv_x", "wq_x")}
        ps = ctx.enter_context(nc.psum_tensor("cp_ps", [P, 4, 512], F32))
        s = ctx.enter_context(phase(nc, "cross_proj", "wk_x wv_x wq_x proj_mm evac"))
        block = ctx.enter_context(nc.Block())
        jobs = [("wk_x", lambda k, h=h: w["wk_x"][:, k, h * P:(h + 1) * P], lambda k: memT[:, k, :], kT[:, h, :], MEM) for h in range(X_HEADS)]
        jobs += [("wv_x", lambda k, m=m: memT[:, k, m * P:(m + 1) * P], lambda k: w["wv_x"][:, k, :], v[:, m, :], 512) for m in range(MEM // P)]
        jobs += [("wq_x", lambda k, h=h: w["wq_x"][:, k, h * P:(h + 1) * P], lambda k, g=g: hT[:, k, g * 512:(g + 1) * 512], qT[:, h, g * 512:(g + 1) * 512], 512)
                 for h in range(X_HEADS) for g in range(2)]

        @block.sync
        def _(sp):
            for n in w:
                sp.dma_start(w[n][:, :, :], a[n].rearrange("(k p) c -> p k c", p=P)).then_inc(s[n], 16)

        @block.tensor
        def _(pe):
            for i, (name, lhsT, rhs, out, width) in enumerate(jobs):
                pe.wait_ge(s[name], 16)
                if i >= 4:
                    pe.wait_ge(s["evac"], i - 3)
                for k in range(DK):
                    last = pe.matmul(ps[:, i % 4, 0:width], lhsT=lhsT(k), rhs=rhs(k), start=(k == 0), stop=(k == DK - 1))
                last.then_inc(s["proj_mm"], 1)

        @block.vector
        def _(dve):
            for i, (name, lhsT, rhs, out, width) in enumerate(jobs):
                dve.wait_ge(s["proj_mm"], i + 1)
                dve.tensor_copy(out, ps[:, i % 4, 0:width]).then_inc(s["evac"], 1)


def cross_attend(nc, a, qT, kT, v, x, ident):
    H, SCALE = X_HEADS, X_DIM ** -0.5
    with ExitStack() as ctx:
        sb = lambda n, sh: ctx.enter_context(nc.sbuf_tensor(n, sh, F32))
        wo = sb("ca_wo", [P, H, D_MODEL])
        prob = sb("ca_prob", [P, 2, H, MEM])
        probT = sb("ca_probT", [P, H, 2, P])
        oT = sb("ca_oT", [P, H, P])
        nmax, rsum, rinv = sb("ca_nmax", [P, H]), sb("ca_rsum", [P, H]), sb("ca_rinv", [P, H])
        psL = ctx.enter_context(nc.psum_tensor("ca_l", [P, H, MEM], F32))
        psT = ctx.enter_context(nc.psum_tensor("ca_t", [P, H, 2, P], F32))
        psO = ctx.enter_context(nc.psum_tensor("ca_o", [P, H, P], F32))
        psY = ctx.enter_context(nc.psum_tensor("ca_y", [P, 2, 512], F32))
        s = ctx.enter_context(phase(nc, "cross", "wo_loaded logit_mm vorder max_ready exp_done prob_ready probT_mm probT_ready o_mm oT_ready y_mm y_added"))
        block = ctx.enter_context(nc.Block())

        @block.sync
        def _(sp):
            sp.dma_start(wo[:, :, :], a["wo_x"].rearrange("(h p) c -> p h c", p=P)).then_inc(s["wo_loaded"], 16)

        @block.tensor
        def _(pe):
            def logits(t):
                wait(pe, s["exp_done"], t)
                for h in range(H):
                    last = pe.matmul(psL[:, h, :], lhsT=qT[:, h, t * P:(t + 1) * P], rhs=kT[:, h, :], start=True, stop=True)
                last.then_inc(s["logit_mm"], 1)

            def output(t):
                pe.wait_ge(s["oT_ready"], t + 1)
                wait(pe, s["y_added"], t)
                for half in range(2):
                    for h in range(H):
                        last = pe.matmul(psY[:, half, :], lhsT=oT[:, h, :], rhs=wo[:, h, half * 512:(half + 1) * 512], start=(h == 0), stop=(h == H - 1))
                last.then_inc(s["y_mm"], 1)

            logits(0)
            pe.wait_ge(s["wo_loaded"], 16)
            for t in range(NT):
                pe.wait_ge(s["prob_ready"], t + 1)
                for h in range(H):
                    for m in range(2):
                        last = pe.transpose(psT[:, h, m, :], prob[:, t % 2, h, m * P:(m + 1) * P], ident)
                last.then_inc(s["probT_mm"], 1)
                if t + 1 < NT:
                    logits(t + 1)
                if t >= 1:
                    output(t - 1)
                pe.wait_ge(s["probT_ready"], t + 1)
                for h in range(H):
                    for m in range(2):
                        last = pe.matmul(psO[:, h, :], lhsT=v[:, m, h * P:(h + 1) * P], rhs=probT[:, h, m, :], start=(m == 0), stop=(m == 1))
                last.then_inc(s["o_mm"], 1)
            output(NT - 1)

        @block.scalar
        def _(act):
            def exps(t):
                act.wait_ge(s["max_ready"], t + 1)
                wait(act, s["probT_mm"], t - 1)
                for h in range(H):
                    last = act.activation(prob[:, t % 2, h, :], psL[:, h, :], ACT.Exp, bias=nmax[:, h:h + 1], scale=SCALE, accum_out=rsum[:, h:h + 1])
                last.then_inc(s["exp_done"], 1)

            exps(0)
            for t in range(NT):
                act.wait_ge(s["probT_mm"], t + 1)
                wait(act, s["o_mm"], t)
                act.activation(probT[:, :, :, :], psT[:, :, :, :], ACT.Copy).then_inc(s["probT_ready"], 1)
                if t + 1 < NT:
                    exps(t + 1)
                act.wait_ge(s["o_mm"], t + 1)
                act.activation(oT[:, :, :], psO[:, :, :], ACT.Copy).then_inc(s["oT_ready"], 1)

        @block.vector
        def _(dve):
            order = Order(dve, s["vorder"])

            def softmax(t):
                dve.wait_ge(s["logit_mm"], t + 1)
                order.then(dve.tensor_reduce(nmax[:, :], psL[:, :, :], AX.X, ALU.max))
                dve.tensor_scalar(nmax[:, :], nmax[:, :], -SCALE, None, ALU.mult).then_inc(s["max_ready"], 1)
                dve.wait_ge(s["exp_done"], t + 1)
                order.then(dve.reciprocal(rinv[:, :], rsum[:, :]))
                dve.tensor_tensor(prob[:, t % 2], prob[:, t % 2], bcast(rinv[:, :], 2, MEM), ALU.mult).then_inc(s["prob_ready"], 1)

            def add_output(t):
                dve.wait_ge(s["y_mm"], t + 1)
                dve.tensor_tensor(x[:, t, :], x[:, t, :], psY[:, :, :].rearrange("p a n -> p (a n)"), ALU.add).then_inc(s["y_added"], 1)

            softmax(0)
            for t in range(NT):
                if t + 1 < NT:
                    softmax(t + 1)
                if t >= 1:
                    add_output(t - 1)
            add_output(NT - 1)


def route_scores(nc, a, hT, hL, top, topi):
    NS = 2 * P_HEADS
    with ExitStack() as ctx:
        sb = lambda n, sh: ctx.enter_context(nc.sbuf_tensor(n, sh, F32))
        w, keys = sb("rs_w", [P, 2, DK, P]), sb("rs_keys", [P, NS, N_KEYS])
        wh, wl = (ctx.enter_context(nc.sbuf_tensor(f"rs_{n}", [P, 2, DK, P], F32R)) for n in ("wh", "wl"))
        qT, sc = sb("rs_qT", [P, 2, SEQ]), sb("rs_sc", [P, 2, NT, N_KEYS])
        psq = ctx.enter_context(nc.psum_tensor("rs_q", [P, 2, 1024], F32))
        pss = ctx.enter_context(nc.psum_tensor("rs_s", [P, 2, 1024], F32))
        s = ctx.enter_context(phase(nc, "route", "keys_loaded w0 w1 w_high w_low kept q_mm q_ready s_mm s_ready vorder picked"))
        block = ctx.enter_context(nc.Block())
        w_pq = a["w_pq"].rearrange("(k p) c -> p k c", p=P)

        @block.sync
        def _(sp):
            for i in range(NS):
                if i >= 2:
                    sp.wait_ge(s["w_low"], i - 1)
                sp.dma_start(w[:, i % 2], w_pq[:, :, i * P:(i + 1) * P]).then_inc(s[f"w{i % 2}"], 16)
                if i == 1:
                    sp.dma_start(keys[:, :, :], a["sub_keys"]).then_inc(s["keys_loaded"], 16)
                    sp.dma_start(a["h_high"], hT[:, :, :].bitcast(F32)).then_inc(s["kept"], 16)
                    sp.dma_start(a["h_low"], hL[:, :, :].bitcast(F32)).then_inc(s["kept"], 16)
            sp.wait_ge(s["kept"], 32)

        @block.tensor
        def _(pe):
            def scores(i):
                pe.wait_ge(s["q_ready"], i + 1)
                if i >= 2:
                    pe.wait_ge(s["s_ready"], i - 1)
                for t in range(NT):
                    last = pe.matmul(pss[:, i % 2, t * P:(t + 1) * P], lhsT=qT[:, i % 2, t * P:(t + 1) * P], rhs=keys[:, i, :], start=True, stop=True)
                last.then_inc(s["s_mm"], 1)

            for i in range(NS):
                pe.wait_ge(s["w_low"], i + 1)
                if i >= 2:
                    pe.wait_ge(s["q_ready"], i - 1)
                for half in range(2):
                    cols = slice(half * 512, (half + 1) * 512)
                    last = product(pe, psq[:, i % 2, cols], lambda k: (wh[:, i % 2, k, :], wl[:, i % 2, k, :]), lambda k: (hT[:, k, cols], hL[:, k, cols]), DK)
                last.then_inc(s["q_mm"], 1)
                if i == 0:
                    pe.wait_ge(s["keys_loaded"], 16)
                else:
                    scores(i - 1)
            scores(NS - 1)

        @block.scalar
        def _(act):
            def scores_out(i):
                act.wait_ge(s["s_mm"], i + 1)
                if i >= 2:
                    act.wait_ge(s["picked"], i - 1)
                act.activation(sc[:, i % 2].rearrange("p t k -> p (t k)"), pss[:, i % 2, :], ACT.Copy).then_inc(s["s_ready"], 1)

            def weights_high(i):
                act.wait_ge(s[f"w{i % 2}"], 16 * (i // 2 + 1))
                if i >= 2:
                    act.wait_ge(s["q_mm"], i - 1)
                act.activation(wh[:, i % 2], w[:, i % 2], ACT.Copy).then_inc(s["w_high"], 1)

            weights_high(0)
            for i in range(NS):
                if i + 1 < NS:
                    weights_high(i + 1)
                act.wait_ge(s["q_mm"], i + 1)
                if i >= 2:
                    act.wait_ge(s["s_mm"], i - 1)
                act.activation(qT[:, i % 2, :], psq[:, i % 2, :], ACT.Copy).then_inc(s["q_ready"], 1)
                if i >= 1:
                    scores_out(i - 1)
            scores_out(NS - 1)

        @block.vector
        def _(dve):
            order = Order(dve, s["vorder"])

            def weights_low(i):
                dve.wait_ge(s["w_high"], i + 1)
                dve.tensor_tensor(wl[:, i % 2], w[:, i % 2], wh[:, i % 2].bitcast(F32), ALU.subtract).then_inc(s["w_low"], 1)

            weights_low(0)
            weights_low(1)
            for i in range(NS):
                if i + 2 < NS:
                    weights_low(i + 2)
                dve.wait_ge(s["s_ready"], i + 1)
                for r in range(2):
                    part = slice(8 * r, 8 * r + 8)
                    for t in range(NT):
                        last = dve.max(top[:, t, i, part], sc[:, i % 2, t, :])
                    order.then(last)
                    for t in range(NT):
                        last = dve.max_index(topi[:, t, i, part], top[:, t, i, part], sc[:, i % 2, t, :])
                    if r == 0:
                        for t in range(NT):
                            last = dve.match_replace(sc[:, i % 2, t, :], top[:, t, i, part], sc[:, i % 2, t, :], TAKEN)
                        order.then(last)
                last.then_inc(s["picked"], 1)


def route_gates(nc, a, top, topi, consts):
    H, K, W = P_HEADS, P_TOPK, 8
    NC = K + (W - 1) * W + (K - W)
    LAST = NC - (K - W)
    T, SLOTS = 8, 4
    UNITS = P // T
    UH = UNITS // 2
    HALF = P // 2
    POOL_UNITS = 6
    ident, iota, starts = consts["ident"], consts["iota"], consts["row_starts"]
    with ExitStack() as ctx:
        sb = lambda n, sh, dt=F32: ctx.enter_context(nc.sbuf_tensor(n, sh, dt))
        routeT = sb("rg_routeT", [P, 2, 3, P])
        keyf = sb("rg_keyf", [P, NT, 2 * H, K])
        steps = sb("rg_steps", [P, NT, H, K])
        cand, hot = sb("rg_cand", [P, H, NC]), sb("rg_hot", [P, 2, H * K, K])
        best, pos = sb("rg_best", [P, H, K]), sb("rg_pos", [P, H * K], U32)
        low3, posf, low3f, col = sb("rg_low3", [P, H * K], U32), sb("rg_posf", [P, H * K]), sb("rg_low3f", [P, H * K]), sb("rg_col", [P, H * K])
        colr = sb("rg_colr", [P, H * K])
        sel = sb("rg_sel", [P, 2, 3, H * K])
        gsum, ginv = sb("rg_gsum", [P, H]), sb("rg_ginv", [P, H])
        hot1, hot2 = sb("rg_hot1", [P, SLOTS, T, P]), sb("rg_hot2", [P, SLOTS, T, P])
        gates = sb("rg_gates", [P, 2, N_KEYS, HALF])
        psR = ctx.enter_context(nc.psum_tensor("rg_r", [P, 2, 512], F32))
        ps = ctx.enter_context(nc.psum_tensor("rg_ps", [P, 2, T, P], F32))
        s = ctx.enter_context(phase(nc, "gates", "vorder porder keyf_ready col_ready hot_weighed rows_made rows_weighed shifted exp_done sel_ready transposed route_ready hot1_made hot1_ready hot1_ready_pool hot2_ready gate_mm evac stored0 stored1"))
        block = ctx.enter_context(nc.Block())
        pair = lambda z, t, half: z[:, t, half::2, :]
        hot4 = lambda half: hot[:, half].rearrange("p (h k) j -> p h k j", h=H)

        @block.vector
        def _(dve):
            order = Order(dve, s["vorder"])
            order.then(dve.tensor_copy(keyf[:, :, :, :], topi))
            rows = keyf[:, :, 0::2, :]
            dve.tensor_copy(steps[:, :, :, 0], rows[:, :, :, 0])
            order.then(dve.tensor_tensor(steps[:, :, :, 1:], rows[:, :, :, 1:], rows[:, :, :, 0:K - 1], ALU.subtract))
            dve.sem_inc(s["keyf_ready"], 1)
            dve.sem_inc(s["gate_mm"], SLOTS)

            def choose(t):
                s1, s2 = pair(top, t, 0), pair(top, t, 1)
                dve.tensor_tensor(cand[:, :, 0:K], bcast(s1[:, :, 0], 2, K), s2, ALU.add)
                dve.tensor_tensor(cand[:, :, K:LAST].rearrange("p h (i j) -> p h i j", j=W), bcast(s1[:, :, 1:W], 3, W), bcast(s2[:, :, 0:W], 2, W - 1), ALU.add)
                order.then(dve.tensor_tensor(cand[:, :, LAST:], s1[:, :, W:], bcast(s2[:, :, 0], 2, K - W), ALU.add))
                for r in range(2):
                    part = slice(8 * r, 8 * r + 8)
                    for h in range(H):
                        last = dve.max(best[:, h, part], cand[:, h, :])
                    order.then(last)
                    yield
                    for h in range(H):
                        last = dve.max_index(pos[:, h * K + 8 * r:h * K + 8 * r + 8], best[:, h, part], cand[:, h, :])
                    if r == 0:
                        for h in range(H):
                            last = dve.match_replace(cand[:, h, :], best[:, h, part], cand[:, h, :], TAKEN)
                    order.then(last)
                    yield
                if t >= 2:
                    dve.wait_ge(s["transposed"], t - 1)
                gate = sel[:, t % 2, 2, :].rearrange("p (h k) -> p h k", h=H)
                dve.tensor_tensor(gate, best[:, :, :], bcast(best[:, :, 0], 2, K), ALU.subtract).then_inc(s["shifted"], 1)
                dve.tensor_copy(posf[:, :], pos[:, :])
                order.then(dve.tensor_scalar(low3[:, :], pos[:, :], W - 1, None, ALU.bitwise_and))
                order.then(dve.tensor_copy(low3f[:, :], low3[:, :]))
                dve.scalar_tensor_tensor(colr[:, :], posf[:, :], float(K), posf[:, :], ALU.is_lt, ALU.mult)
                order.then(dve.scalar_tensor_tensor(low3f[:, :], posf[:, :], float(K), low3f[:, :], ALU.is_ge, ALU.mult))
                order.then(dve.scalar_tensor_tensor(low3f[:, :], posf[:, :], float(LAST), low3f[:, :], ALU.is_lt, ALU.mult))
                if t >= 1:
                    dve.wait_ge(s["hot_weighed"], t)
                dve.tensor_tensor(col[:, :], colr[:, :], low3f[:, :], ALU.add).then_inc(s["col_ready"], 1)
                yield
                dve.tensor_tensor(hot[:, 0], bcast(posf[:, :], 2, K), bcast(starts, 1, H * K), ALU.is_ge).then_inc(s["rows_made"], 1)
                for _ in range(POOL_UNITS):
                    yield
                dve.wait_ge(s["exp_done"], t + 1)
                order.then(dve.tensor_reduce(gsum[:, :], gate, AX.X, ALU.add))
                order.then(dve.reciprocal(ginv[:, :], gsum[:, :]))
                order.then(dve.tensor_tensor(gate, gate, bcast(ginv[:, :], 2, K), ALU.mult))
                yield
                dve.wait_ge(s["hot_weighed"], t + 1)
                dve.tensor_reduce(sel[:, t % 2, 1, :], hot[:, 1, :, 0:K // 2], AX.X, ALU.add)
                yield
                dve.wait_ge(s["rows_weighed"], t + 1)
                dve.tensor_reduce(sel[:, t % 2, 0, :], hot[:, 0, :, 0:K // 2], AX.X, ALU.add).then_inc(s["sel_ready"], 1)
                dve.wait_ge(s["sel_ready"], t + 1)

            def one_hots(t):
                for m in range(UNITS):
                    dve.wait_ge(s["gate_mm"], t * UNITS + m + 1)
                    for c, hot_, ready in ((0, hot1, "hot1_made"), (1, hot2, "hot2_ready")):
                        key = routeT[:, t % 2, c, m * T:(m + 1) * T]
                        dve.tensor_tensor(hot_[:, m % SLOTS], bcast(iota, 1, T), bcast(key, 2, P), ALU.is_equal).then_inc(s[ready], 1)
                    yield

            for _ in choose(0):
                pass
            for t in range(NT):
                dve.wait_ge(s["route_ready"], t + 1)
                later = choose(t + 1) if t + 1 < NT else iter(())
                for _ in one_hots(t):
                    next(later, None)
                assert next(later, None) is None and next(later, "done") == "done"

        @block.gpsimd
        def _(pool):
            order = Order(pool, s["porder"])

            def columns(t):
                pool.wait_ge(s["col_ready"], t + 1)
                if t >= 1:
                    pool.wait_ge(s["sel_ready"], t)
                order.then(pool.tensor_tensor(hot[:, 1], bcast(col[:, :], 2, K), bcast(iota[:, 0:K], 1, H * K), ALU.subtract))
                order.then(pool.tensor_scalar(hot[:, 1], hot[:, 1], 0.0, None, ALU.is_equal))

            def second_keys(t):
                order.then(pool.tensor_tensor(hot4(1), hot4(1), bcast(pair(keyf, t, 1), 2, K), ALU.mult))
                pool.tensor_tensor(hot[:, 1, :, 0:K // 2], hot[:, 1, :, 0:K // 2], hot[:, 1, :, K // 2:], ALU.add).then_inc(s["hot_weighed"], 1)

            def first_keys(t):
                pool.wait_ge(s["rows_made"], t + 1)
                order.then(pool.tensor_tensor(hot4(0), hot4(0), bcast(steps[:, t], 2, K), ALU.mult))

            def first_sums(t):
                pool.tensor_tensor(hot[:, 0, :, 0:K // 2], hot[:, 0, :, 0:K // 2], hot[:, 0, :, K // 2:], ALU.add).then_inc(s["rows_weighed"], 1)

            def scale(t, m):
                pool.wait_ge(s["hot1_made"], t * UNITS + m + 1)
                rows = hot1[:, m % SLOTS]
                pool.tensor_tensor(rows, rows, bcast(routeT[:, t % 2, 2, m * T:(m + 1) * T], 2, P), ALU.mult).then_inc(s["hot1_ready_pool"], 1)

            pool.wait_ge(s["keyf_ready"], 1)
            columns(0)
            second_keys(0)
            first_keys(0)
            first_sums(0)
            for t in range(NT):
                scale(t, SLOTS - 1)
                if t + 1 < NT:
                    columns(t + 1)
                scale(t, 2 * SLOTS - 1)
                if t + 1 < NT:
                    second_keys(t + 1)
                    first_keys(t + 1)
                scale(t, 3 * SLOTS - 1)
                if t + 1 < NT:
                    first_sums(t + 1)
                scale(t, 4 * SLOTS - 1)

        @block.tensor
        def _(pe):
            def transposes(t):
                pe.wait_ge(s["sel_ready"], t + 1)
                if t >= 2:
                    pe.wait_ge(s["route_ready"], t - 1)
                for i in range(3):
                    last = pe.transpose(psR[:, t % 2, i * P:(i + 1) * P], sel[:, t % 2, i, :], ident)
                last.then_inc(s["transposed"], 1)

            pe.sem_inc(s["evac"], 2)
            def units(t, g, slots):
                for u in slots:
                    n = g * SLOTS + (t * UNITS + u + 1)
                    if u < SLOTS - 1:
                        pe.wait_ge(s["hot1_ready"], g * (SLOTS - 1) + (t * UNITS // SLOTS * (SLOTS - 1) + u + 1))
                    else:
                        pe.wait_ge(s["hot1_ready_pool"], g + (t * UNITS // SLOTS + 1))
                    pe.wait_ge(s["hot2_ready"], n)
                    pe.wait_ge(s["evac"], n)
                    for j in range(T):
                        last = pe.matmul(ps[:, u % 2, j, :], lhsT=hot2[:, u, j, :], rhs=hot1[:, u, j, :], start=True, stop=True)
                    last.then_inc(s["gate_mm"], 1)

            transposes(0)
            for t in range(NT):
                with pe.Fori(0, UNITS // SLOTS - 1) as g:
                    units(t, g, range(SLOTS))
                units(t, UNITS // SLOTS - 1, range(2))
                if t + 1 < NT:
                    transposes(t + 1)
                units(t, UNITS // SLOTS - 1, range(2, SLOTS))

        @block.scalar
        def _(act):
            def exps(t):
                act.wait_ge(s["shifted"], t + 1)
                act.activation(sel[:, t % 2, 2, :], sel[:, t % 2, 2, :], ACT.Exp).then_inc(s["exp_done"], 1)

            def routes(t):
                act.wait_ge(s["transposed"], t + 1)
                if t >= 2:
                    act.wait_ge(s["gate_mm"], SLOTS + (t - 1) * UNITS)
                act.activation(routeT[:, t % 2], psR[:, t % 2, 0:3 * P].rearrange("p (a n) -> p a n", a=3), ACT.Copy).then_inc(s["route_ready"], 1)

            def scale(t, m):
                if m % SLOTS == SLOTS - 1:
                    return
                act.wait_ge(s["hot1_made"], m + (t * UNITS + 1))
                for j in range(T):
                    rows = hot1[:, bass.ds(m % SLOTS, 1), j, :].rearrange("p a k -> p (a k)") if not isinstance(m, int) else hot1[:, m % SLOTS, j, :]
                    last = act.activation(rows, rows, ACT.Copy, scale=routeT[:, t % 2, 2, bass.ds(m * T + j, 1)])
                last.then_inc(s["hot1_ready"], 1)

            def leave(t, p, m, slot):
                act.wait_ge(s["gate_mm"], m + (SLOTS + (2 * t + p) * UH + 1))
                act.activation(gates[:, p, :, bass.ds(m * T, T)], ps[:, slot].rearrange("j n i -> j i n"), ACT.Copy).then_inc(s["evac"], 1)

            for p in range(2):
                act.sem_inc(s[f"stored{p}"], 16)
            exps(0)
            routes(0)
            for t in range(NT):
                for p in range(2):
                    if p == 0 and t >= 1:
                        leave(t - 1, 1, UH - 1, 1)
                    scale(t, p * UH)
                    if p == 1 and t + 1 < NT:
                        exps(t + 1)
                    if p == 1:
                        leave(t, 0, UH - 1, 1)
                    act.wait_ge(s[f"stored{p}"], t * 16 + 16)
                    for m in range(1, UH):
                        scale(t, p * UH + m)
                        leave(t, p, m - 1, (m - 1) % 2)
                        if p == 1 and m == UH - 2 and t + 1 < NT:
                            routes(t + 1)
            leave(NT - 1, 1, UH - 1, 1)

        @block.sync
        def _(sp):
            for t in range(NT):
                for p in range(2):
                    sp.wait_ge(s["evac"], (2 * t + p + 1) * UH + 2)
                    sp.dma_start(a["gates"][2 * t + p], gates[:, p]).then_inc(s[f"stored{p}"], 16)
            for p in range(2):
                sp.wait_ge(s[f"stored{p}"], 16 * (NT + 1))


def experts(nc, a, x):
    G = 2
    NG = N_KEYS // G
    NY = 2 * NT // G
    with ExitStack() as ctx:
        sb = lambda n, sh, dt=F32: ctx.enter_context(nc.sbuf_tensor(n, sh, dt))
        hh, hl = sb("ex_hh", [P, DK, SEQ], F32R), sb("ex_hl", [P, DK, SEQ], F32R)
        u_sb, v_sb, g_sb = sb("ex_u", [P, DK, P]), sb("ex_v", [P, D_MODEL]), sb("ex_g", [P, SEQ])
        act_sb = sb("ex_act", [P, SEQ])
        uh, ul = sb("ex_uh", [P, 2, DK, P], F32R), sb("ex_ul", [P, 2, DK, P], F32R)
        vh, vl = sb("ex_vh", [P, 2, G, D_MODEL], F32R), sb("ex_vl", [P, 2, G, D_MODEL], F32R)
        wh, wl = sb("ex_wh", [P, 2, G, SEQ], F32R), sb("ex_wl", [P, 2, G, SEQ], F32R)
        psA = ctx.enter_context(nc.psum_tensor("ex_a", [P, 2, 1024], F32))
        psY = ctx.enter_context(nc.psum_tensor("ex_y", [P, 4, 512], F32))
        s = ctx.enter_context(phase(nc, "experts", "h0 h1 h2 h3 u_loaded v_loaded g_loaded u_high u_low v_high v_low act_mm gelu_done weighed w_high w_low y_mm y_added"))
        block = ctx.enter_context(nc.Block())

        def chunks(eng, slot):
            for n in range(4):
                slot(n, n)
            with eng.Fori(1, N_KEYS // 4 - 1) as i:
                for j in range(4):
                    slot(i * 4 + j, j)
            for n in range(N_KEYS - 4, N_KEYS):
                slot(n, n % 4)

        def groups_second_done(eng, n, j, back):
            wait(eng, s["y_mm"], (n - j % 2) * NY - (back - 1) * G * NY)

        @block.sync
        def _(sp):
            sp.dma_start(u_sb[:, :, :], a["u_emb"][0]).then_inc(s["u_loaded"], 16)
            for piece in range(4):
                cols, ks = slice(piece // 2 * 512, (piece // 2 + 1) * 512), slice(piece % 2 * 4, (piece % 2 + 1) * 4)
                for dst, src in ((hh, "h_high"), (hl, "h_low")):
                    sp.dma_start(dst[:, ks, cols].bitcast(F32), a[src][:, ks, cols]).then_inc(s[f"h{piece}"], 16)

            def loads(n, j):
                wait(sp, s["u_low"], n)
                if not isinstance(n, int) or n > 0:
                    sp.dma_start(u_sb[:, :, :], a["u_emb"][bass.ds(n, 1)].rearrange("a p k e -> p (a k) e")).then_inc(s["u_loaded"], 16)
                wait(sp, s["v_low"], n)
                sp.dma_start(v_sb[:, :], a["v_emb"][bass.ds(n, 1)].rearrange("a e d -> e (a d)")).then_inc(s["v_loaded"], 16)
                wait(sp, s["weighed"], n)
                sp.dma_start(g_sb[:, :].rearrange("j (b n) -> j b n", n=P // 2), a["gates"][:, :, bass.ds(n, 1), :].rearrange("b j a n -> j (b a) n")).then_inc(s["g_loaded"], 16)

            chunks(sp, loads)

        @block.tensor
        def _(pe):
            def first(n, j):
                pe.wait_ge(s["u_low"], n + 1)
                wait(pe, s["gelu_done"], n - 1)
                for half in range(2):
                    cols = slice(half * 512, (half + 1) * 512)

                    def tokens(k):
                        if isinstance(n, int) and n == 0 and k % 4 == 0:
                            pe.wait_ge(s[f"h{2 * half + k // 4}"], 32)
                        return hh[:, k, cols], hl[:, k, cols]

                    last = product(pe, psA[:, j % 2, cols], lambda k: (uh[:, j % 2, k, :], ul[:, j % 2, k, :]), tokens, DK)
                last.then_inc(s["act_mm"], 1)

            def second(n, j):
                q, p = j % 2, 1 - j // 2
                if q == 0:
                    pe.wait_ge(s["v_low"], n)
                    pe.wait_ge(s["w_low"], n)
                for y in range(NY):
                    t, half = (q * NY + y) // 2, y % 2
                    toks, cols = slice(t * P, (t + 1) * P), slice(half * 512, (half + 1) * 512)
                    wait(pe, s["y_added"], (n - G) * NY + y - 3)
                    product(pe, psY[:, y % 4, :], lambda c: (wh[:, p, c, toks], wl[:, p, c, toks]), lambda c: (vh[:, p, c, cols], vl[:, p, c, cols]), G).then_inc(s["y_mm"], 1)

            def slot(n, j):
                first(n, j)
                if not isinstance(n, int) or n >= G:
                    second(n, j)

            chunks(pe, slot)
            for n in range(N_KEYS, N_KEYS + G):
                second(n, n % 4)

        @block.scalar
        def _(act):
            def u_high(n, j):
                act.wait_ge(s["u_loaded"], n * 16 + 16)
                wait(act, s["act_mm"], n - 1)
                act.activation(uh[:, j % 2], u_sb[:, :, :], ACT.Copy).then_inc(s["u_high"], 1)

            def slot(n, j):
                if not (isinstance(n, int) and n == N_KEYS - 1):
                    u_high(n + 1, (j + 1) % 4)
                act.wait_ge(s["v_loaded"], n * 16 + 16)
                groups_second_done(act, n, j, 2)
                act.activation(vh[:, j // 2, j % 2, :], v_sb[:, :], ACT.Copy).then_inc(s["v_high"], 1)
                act.wait_ge(s["act_mm"], n + 1)
                wait(act, s["w_low"], n)
                act.activation(act_sb[:, :], psA[:, j % 2, :], ACT.Gelu).then_inc(s["gelu_done"], 1)
                act.wait_ge(s["weighed"], n + 1)
                act.activation(wh[:, j // 2, j % 2, :], act_sb[:, :], ACT.Copy).then_inc(s["w_high"], 1)

            u_high(0, 0)
            chunks(act, slot)

        @block.vector
        def _(dve):
            def low(out, whole, high):
                return dve.tensor_tensor(out, whole, high.bitcast(F32), ALU.subtract)

            def u_low(n, j):
                dve.wait_ge(s["u_high"], n + 1)
                low(ul[:, j % 2], u_sb[:, :, :], uh[:, j % 2]).then_inc(s["u_low"], 1)

            def add(n, j, sums):
                for y in sums if not isinstance(n, int) or n >= G else ():
                    t, half = ((j % 2) * NY + y) // 2, y % 2
                    xr = x[:, t, half * 512:(half + 1) * 512]
                    dve.wait_ge(s["y_mm"], (n - G) * NY + y + 1)
                    dve.tensor_tensor(xr, xr, psY[:, y % 4, :], ALU.add).then_inc(s["y_added"], 1)

            def slot(n, j):
                if not (isinstance(n, int) and n == N_KEYS - 1):
                    u_low(n + 1, (j + 1) % 4)
                dve.wait_ge(s["v_high"], n + 1)
                low(vl[:, j // 2, j % 2, :], v_sb[:, :], vh[:, j // 2, j % 2, :]).then_inc(s["v_low"], 1)
                dve.wait_ge(s["gelu_done"], n + 1)
                dve.wait_ge(s["g_loaded"], n * 16 + 16)
                dve.tensor_tensor(act_sb[:, :], act_sb[:, :], g_sb[:, :], ALU.mult).then_inc(s["weighed"], 1)
                add(n, j, range(2))
                dve.wait_ge(s["w_high"], n + 1)
                low(wl[:, j // 2, j % 2, :], act_sb[:, :], wh[:, j // 2, j % 2, :]).then_inc(s["w_low"], 1)
                add(n, j, range(2, NY))

            u_low(0, 0)
            chunks(dve, slot)
            for n in range(N_KEYS, N_KEYS + G):
                add(n, n % 4, range(NY))


def final_norm(nc, a, x, out):
    with ExitStack() as ctx:
        sb = lambda n, sh: ctx.enter_context(nc.sbuf_tensor(n, sh, F32))
        gain, junk, y = sb("fn_gain", [P, D_MODEL]), sb("fn_junk", [P, 2, D_MODEL]), sb("fn_y", [P, NT, D_MODEL])
        ssq, root, rinv, epst = sb("fn_ssq", [P, NT]), sb("fn_root", [P, NT]), sb("fn_rinv", [P, NT]), sb("fn_eps", [P, 1])
        s = ctx.enter_context(phase(nc, "final", "gain_loaded eps_ready squared rooted inverted y_ready stored"))
        block = ctx.enter_context(nc.Block())

        @block.sync
        def _(sp):
            sp.dma_start(gain[:, :], a["g_final"].partition_broadcast(P)).then_inc(s["gain_loaded"], 16)
            for t in range(NT):
                sp.wait_ge(s["y_ready"], t + 1)
                sp.dma_start(out[t * P:(t + 1) * P, :], y[:, t, :]).then_inc(s["stored"], 16)
            sp.wait_ge(s["stored"], 16 * NT)

        @block.scalar
        def _(act):
            for t in range(NT):
                if t >= 2:
                    act.wait_ge(s["squared"], t - 1)
                act.activation(junk[:, t % 2, :], x[:, t, :], ACT.Square, accum_out=ssq[:, t:t + 1]).then_inc(s["squared"], 1)
            act.wait_ge(s["squared"], NT)
            act.wait_ge(s["eps_ready"], 1)
            act.activation(root[:, :], ssq[:, :], ACT.Sqrt, bias=epst[:, :], scale=1.0 / D_MODEL).then_inc(s["rooted"], 1)

        @block.vector
        def _(dve):
            dve.memset(epst[:, :], EPS).then_inc(s["eps_ready"], 1)
            dve.wait_ge(s["gain_loaded"], 16)
            dve.wait_ge(s["rooted"], 1)
            dve.reciprocal(rinv[:, :], root[:, :]).then_inc(s["inverted"], 1)
            dve.wait_ge(s["inverted"], 1)
            for t in range(NT):
                dve.scalar_tensor_tensor(y[:, t, :], x[:, t, :], rinv[:, t:t + 1], gain[:, :], ALU.mult, ALU.mult).then_inc(s["y_ready"], 1)


CONSTANTS = ("ident", "flip", "ones", "relhot", "iota", "row_starts")
DELTA_CONSTANTS = ("dmask", "lev", "levT")
GAINS = {"g_mix": DK, "g_cross": DK, "g_mem": DK, "g_ffn": DK, "g_lat": 5}


def hybrid_block(nc, a, out, probe=None):
    probe = probe or (lambda *args: None)
    whole = lambda t: t[tuple(slice(None) for _ in t.shape)]
    with ExitStack() as ctx:
        def sb(stack, name, shape, dt=F32, side="left"):
            return stack.enter_context(nc.sbuf_tensor(name, shape, dt, side=side))

        small = {n: sb(ctx, f"c_{n}", list(a[f"c_{n}"].shape)) for n in CONSTANTS}
        small |= {n: sb(ctx, f"s_{n}", [P, w]) for n, w in GAINS.items()}
        load_all(nc, "constants", [(whole(t), a[f"c_{n}" if n in CONSTANTS else n]) for n, t in small.items()])
        consts = {n: whole(t) for n, t in small.items()}
        ident = consts["ident"]
        gain = lambda n: small[n]
        front = ctx.enter_context(ExitStack())
        lat = sb(front, "lat", [P, NT, N_COLS])
        with ExitStack() as sub:
            hT, hL = sb(sub, "mixT", [P, DK, SEQ], F32R), sb(sub, "mixL", [P, DK, SEQ], F32R)
            with nc.sbuf_tensor("x_in", [P, NT, D_MODEL], F32, side="right") as x_in:
                norm_transposed(nc, "norm_mix", x_in, a["x"], gain("g_mix"), ident, hT, NT, hL)
            project(nc, a, hT, hL, lat, ident)
        wide = sb(front, "wide", [P, DK, SEQ])
        with ExitStack() as mixer:
            gatings = [sb(mixer, n, [P, NT, B_HEADS]) for n in ("beta", "g", "eg", "etail")] + [sb(mixer, "dch", [P, 2, NT, B_HEADS]), sb(mixer, "beg", [P, NT, B_HEADS])]
            idx_keys, keys_hl = sb(mixer, "idx_keys", [P, SEQ], F32R), sb(mixer, "keys_hl", [P, A_HEADS, SEQ], F32R, side="right")
            v, widx, near = sb(mixer, "v", [P, NT, 512]), sb(mixer, "widx", [P, NT, IDX_HEADS]), sb(mixer, "near", [P, A_HEADS, NEAR])
            with ExitStack() as sub:
                tri = sb(sub, "c_tri", [P, 4, P])
                load_all(nc, "tri", [(tri[:, :, :], a["c_tri"])])
                delta_gates(nc, a, lat, *gatings, tri)
            sparse_prepare(nc, a, lat, small["g_lat"], consts, idx_keys, keys_hl, v, widx[:, :, :], near[:, :, :])
            masks = {n: sb(mixer, f"c_{n}", list(a[f"c_{n}"].shape)) for n in DELTA_CONSTANTS}
            load_all(nc, "masks", [(whole(t), a[f"c_{n}"]) for n, t in masks.items()])
            mixers(nc, a, (idx_keys, keys_hl, v, widx, near), gatings, lat, wide, consts | {n: whole(t) for n, t in masks.items()})
        stream = sb(ctx, "stream", [P, NT, D_MODEL], side="right")
        probe("mix", wide)
        mix_out(nc, a, wide, stream, ident)
        probe("x1", stream)

        with ExitStack() as cross:
            memT = sb(cross, "memT", [P, DK, MEM])
            xqT, xkT, xv = sb(cross, "xqT", [P, X_HEADS, SEQ]), sb(cross, "xkT", [P, X_HEADS, MEM]), sb(cross, "xv", [P, MEM // P, 512])
            norm_transposed(nc, "norm_cross", stream, None, gain("g_cross"), ident, wide, NT)
            with nc.sbuf_tensor("mem_in", [P, MEM // P, D_MODEL], F32) as mem_in:
                norm_transposed(nc, "norm_mem", mem_in, a["mem"], gain("g_mem"), ident, memT, MEM // P)
            cross_project(nc, a, wide, memT, xqT, xkT, xv)
            cross_attend(nc, a, xqT, xkT, xv, stream, ident)
        probe("x2", stream)

        front.close()
        with ExitStack() as route:
            top = sb(route, "top", [P, NT, 2 * P_HEADS, P_TOPK])
            topi = sb(route, "topi", [P, NT, 2 * P_HEADS, P_TOPK], U32)
            with ExitStack() as normed:
                hT, hL = sb(normed, "hT", [P, DK, SEQ], F32R), sb(normed, "hL", [P, DK, SEQ], F32R)
                norm_transposed(nc, "norm_ffn", stream, None, gain("g_ffn"), ident, hT, NT, hL)
                route_scores(nc, a, hT, hL, top, topi)
            route_gates(nc, a, top, topi[:, :, :, :], consts)
        experts(nc, a, stream)
        final_norm(nc, a, stream, out)


def kernel(**inputs):
    import concourse.bacc as bacc
    from concourse.bass_utils import run_bass_kernel_spmd

    g = {n: np.asarray(v) for n, v in inputs.items()}
    column = lambda v: v.reshape(-1, P).T
    arrays = {
        "x": g["x"][0], "mem": g["mem"][0], "w_in": g["w_in"][0],
        "g_mix": column(g["g_mix"][0]), "g_cross": column(g["g_cross"][0]), "g_mem": column(g["g_mem"][0]), "g_ffn": column(g["g_ffn"][0]),
        "g_lat": np.stack([*g["g_cq"][0].reshape(2, P), *g["g_ckv"][0].reshape(2, P), np.tile(g["g_kidx"][0], 2)], 1),
        "w_uq": g["w_uq"][0].reshape(A_LORA, 512), "w_iq": g["w_iq"][0].reshape(A_LORA, 512),
        "w_uk": g["w_uk"][0].reshape(A_LORA, 512), "w_uv": g["w_uv"][0].reshape(A_LORA, 512),
        "rel_bias": g["rel_bias"],
        "conv_w": g["conv_w"][0].reshape(CONV, 3 * B_QK // P, P).transpose(2, 1, 0),
        "A_log": g["A_log"][0], "dt_bias": g["dt_bias"][0], "g_onorm": g["g_onorm"][0], "w_out": g["w_out"][0],
        "wq_x": g["wq_x"][0].reshape(D_MODEL, 512), "wk_x": g["wk_x"][0].reshape(D_MODEL, 512), "wv_x": g["wv_x"][0].reshape(D_MODEL, 512),
        "wo_x": g["wo_x"][0].reshape(512, D_MODEL),
        "w_pq": g["w_pq"][0].reshape(D_MODEL, 2 * P_HEADS * P),
        "sub_keys": g["sub_keys"][0].reshape(2 * P_HEADS, N_KEYS, P).transpose(2, 0, 1),
        "u_emb": g["u_emb"][0].reshape(N_KEYS, P, DK, P).transpose(0, 3, 2, 1),
        "v_emb": g["v_emb"][0].reshape(N_KEYS, P, D_MODEL),
        "g_final": g["g_final"],
    } | {f"c_{n}": v for n, v in shape_constants().items()}
    arrays = {n: np.ascontiguousarray(v) for n, v in arrays.items()}

    nc = bacc.Bacc("TRN2", target_bir_lowering=False, num_devices=1)
    a = {n: nc.dram_tensor(f"in_{n}", v.shape, F32, kind="ExternalInput").ap() for n, v in arrays.items()}
    a["bias_rows"] = nc.dram_tensor("bias_rows", (A_HEADS, NREL), F32).ap()
    a["nat"] = nc.dram_tensor("nat", (NT, P, 3 * B_QK), F32).ap()
    a["silu_z"] = nc.dram_tensor("silu_z", (NT, P, B_QK), F32).ap()
    a["k_parts"] = nc.dram_tensor("k_parts", (2, P, 4, SEQ), F32).ap()
    a["qi_parts"] = nc.dram_tensor("qi_parts", (2, P, NT, 4, P), F32).ap()
    a["q_parts"] = nc.dram_tensor("q_parts", (2, P, NT, 4, P), F32).ap()
    a["h_high"] = nc.dram_tensor("h_high", (P, DK, SEQ), F32).ap()
    a["h_low"] = nc.dram_tensor("h_low", (P, DK, SEQ), F32).ap()
    a["gates"] = nc.dram_tensor("gates", (2 * NT, P, N_KEYS, P // 2), F32).ap()
    out = nc.dram_tensor("out_x", (SEQ, D_MODEL), F32, kind="ExternalOutput").ap()
    hybrid_block(nc, a, out)
    r = run_bass_kernel_spmd(nc, [{f"in_{n}": v for n, v in arrays.items()}], core_ids=[0])
    return r.results[0]["out_x"].reshape(1, SEQ, D_MODEL)
```
